# Optimizing a Trainium2 kernel written in Bass

```python
import math
import jax, jax.numpy as jnp
from jax import lax
import numpy as np

D_MODEL = 1024
BATCH = 1
SEQ = 1024
DEPTH = 1
DEC_BATCH = 8
DEC_SEQ = 1
PAST_LEN = 1024
PAGE_SIZE = 128

PLE_DIM = 256
BRANCH_WIDTH = D_MODEL // 2
N_BRANCH = 3
M_HEADS = 4
M_HEAD_DIM = BRANCH_WIDTH // M_HEADS
M_WIDTH = BRANCH_WIDTH
M_CHUNK = 64
FORGET_BIAS = 3.0
CONV_WIDTH = BRANCH_WIDTH
CONV_K = 3
SB_HEADS = 4
SB_HEAD_DIM = BRANCH_WIDTH // SB_HEADS
SB_WIDTH = BRANCH_WIDTH
SB_BLOCK = 128
SB_BIAS_INIT = -6.0
FFN_DIM = 4 * D_MODEL
RMS_EPS = 1e-6
SPLIT_SIZES = (M_WIDTH, M_WIDTH, M_WIDTH, M_WIDTH, M_HEADS, M_HEADS,
               CONV_WIDTH, CONV_WIDTH, CONV_WIDTH,
               SB_WIDTH, SB_WIDTH, SB_WIDTH,
               N_BRANCH * D_MODEL)
N_IN = sum(SPLIT_SIZES)

kernel_name = 'hybrid_mlstm_shortconv_stickbreaking_step'

def rmsnorm(x, g):
    xf = x.astype(jnp.float32)
    y = xf * lax.rsqrt(jnp.mean(jnp.square(xf), axis=-1, keepdims=True) + RMS_EPS)
    return (y * g.astype(jnp.float32)).astype(x.dtype)

def mlstm_chunkwise(q, k, v, i_pre, log_f, C0, n0, m0):
    B, T, H, Dh = q.shape
    L = T if T <= M_CHUNK else math.gcd(T, M_CHUNK)
    nc = T // L

    def to_chunks(a):
        a = a.reshape((B, nc, L) + a.shape[2:])
        return jnp.moveaxis(jnp.moveaxis(a, 1, 0), 2, 3)

    causal = jnp.tril(jnp.ones((L, L), dtype=bool))

    def step(carry, xs):
        C, n, m = carry
        qc, kc, vc, ic, fc = xs
        b = jnp.cumsum(fc, axis=-1)
        d = jnp.where(causal, b[..., :, None] - b[..., None, :] + ic[..., None, :], -jnp.inf)
        inter = b + m[..., None]
        m_t = jnp.maximum(inter, jnp.max(d, axis=-1))
        w = jnp.exp(d - m_t[..., None]) * jnp.einsum('bhtd,bhsd->bhts', qc, kc)
        s = jnp.exp(inter - m_t)
        num = s[..., None] * jnp.einsum('bhtd,bhde->bhte', qc, C) + jnp.einsum('bhts,bhse->bhte', w, vc)
        den = s * jnp.einsum('bhtd,bhd->bht', qc, n) + jnp.sum(w, axis=-1)
        hc = num / jnp.maximum(jnp.abs(den), jnp.exp(-m_t))[..., None]
        m_new = m_t[..., -1]
        wk = jnp.exp(b[..., -1:] - b + ic - m_new[..., None])
        decay = jnp.exp(b[..., -1] + m - m_new)
        C = decay[..., None, None] * C + jnp.einsum('bhs,bhsd,bhse->bhde', wk, kc, vc)
        n = decay[..., None] * n + jnp.einsum('bhs,bhsd->bhd', wk, kc)
        return (C, n, m_new), hc

    ks = k * (Dh ** -0.5)
    xs = (to_chunks(q), to_chunks(ks), to_chunks(v), to_chunks(i_pre), to_chunks(log_f))
    (C, n, m), hs = lax.scan(step, (C0, n0, m0), xs)
    h = jnp.swapaxes(jnp.moveaxis(hs, 0, 1), 2, 3).reshape(B, T, H, Dh)
    return h, C, n, m

def stick_breaking(q, k, v, bias, q_pos, k_pos):
    z = (jnp.einsum('bqhd,bkhd->bhqk', q, k).astype(jnp.float32) * (SB_HEAD_DIM ** -0.5)
         + bias.astype(jnp.float32)[None, :, None, None])
    mask = k_pos[None, :] < q_pos[:, None]
    log_keep = jnp.where(mask, jax.nn.log_sigmoid(-z), 0.0)
    later = lax.cumsum(log_keep, axis=3, reverse=True) - log_keep
    a = jnp.where(mask, jnp.exp(jax.nn.log_sigmoid(z) + later), 0.0)
    return jnp.einsum('bhqk,bkhd->bqhd', a.astype(v.dtype), v)

def sb_prompt(q, k, v, bias):
    B, T, H, Dh = q.shape
    blk = SB_BLOCK if T % SB_BLOCK == 0 else T
    nb = T // blk
    pos = jnp.arange(T)
    qb = jnp.swapaxes(q.reshape(B, nb, blk, H, Dh), 0, 1)
    out = lax.map(lambda a: stick_breaking(a[0], k, v, bias, a[1], pos), (qb, pos.reshape(nb, blk)))
    return jnp.swapaxes(out, 0, 1).reshape(B, T, H, Dh)

def decoder_layer(h, p_l, w, mlstm0, conv0, past_kv):
    (g_mix, w_in, b_if, b_sb, conv_w, w_branch, w_out, g_mlp, w_up, w_down, g_ple, w_ple_gate, w_ple) = w
    B, T, _ = h.shape
    f32 = jnp.float32
    xn = rmsnorm(h, g_mix)
    proj = xn @ w_in
    split_points = np.cumsum(SPLIT_SIZES)[:-1].tolist()
    (mq, mk, mv, mo, mi, mf, cb, cc, cx, sq, sk, sv, gates) = jnp.split(proj, split_points, axis=-1)

    i_pre = (mi + b_if[:M_HEADS]).astype(f32)
    log_f = jax.nn.log_sigmoid((mf + b_if[M_HEADS:]).astype(f32))
    C0, n0, m0 = mlstm0
    hm, C, n, m = mlstm_chunkwise(
        mq.reshape(B, T, M_HEADS, M_HEAD_DIM).astype(f32),
        mk.reshape(B, T, M_HEADS, M_HEAD_DIM).astype(f32),
        mv.reshape(B, T, M_HEADS, M_HEAD_DIM).astype(f32),
        i_pre, log_f, C0.astype(f32), n0.astype(f32), m0.astype(f32))
    ym = jax.nn.sigmoid(mo) * hm.reshape(B, T, M_WIDTH).astype(h.dtype)

    xc = cc * cx
    full = jnp.concatenate([conv0.astype(xc.dtype), xc], axis=1)
    conv = sum(conv_w[j] * full[:, j:j + T] for j in range(CONV_K))
    yc = cb * conv
    new_buf = full[:, T:]

    q = sq.reshape(B, T, SB_HEADS, SB_HEAD_DIM)
    k = sk.reshape(B, T, SB_HEADS, SB_HEAD_DIM)
    v = sv.reshape(B, T, SB_HEADS, SB_HEAD_DIM)
    if past_kv is None:
        ys = sb_prompt(q, k, v, b_sb)
    else:
        pk, pv = past_kv
        P = pk.shape[1]
        keys = jnp.concatenate([pk.astype(k.dtype), k], axis=1)
        vals = jnp.concatenate([pv.astype(v.dtype), v], axis=1)
        ys = stick_breaking(q, keys, vals, b_sb, P + jnp.arange(T), jnp.arange(P + T))
    ys = ys.reshape(B, T, SB_WIDTH)

    branches = jnp.stack([ym, yc, ys], axis=2)
    pb = jnp.einsum('btnw,nwd->btnd', branches, w_branch)
    g = jax.nn.sigmoid(gates.reshape(B, T, N_BRANCH, D_MODEL))
    h = h + jnp.einsum('btnd,de->bte', g * pb, w_out)

    u = rmsnorm(h, g_mlp) @ w_up
    h = h + jnp.square(jax.nn.relu(u)) @ w_down

    h = h + (p_l @ w_ple) * jax.nn.sigmoid(rmsnorm(h, g_ple) @ w_ple_gate)
    return h, (k, v, C, n, m, new_buf)

def setup_inputs(seed: int = 0) -> dict:
    key = jax.random.key(seed)
    ks = jax.random.split(key, 32)
    nrm = jax.random.normal
    f32 = jnp.float32
    n_pages = PAST_LEN // PAGE_SIZE
    n_used = DEC_BATCH * n_pages
    n_phys = n_used + max(1, n_used // 4)
    page_table = jax.random.permutation(ks[0], n_phys)[:n_used].reshape(DEC_BATCH, n_pages).astype(jnp.int32)
    b_if = jnp.concatenate([0.1 * nrm(ks[1], (DEPTH, M_HEADS), f32),
                            FORGET_BIAS + 0.1 * nrm(ks[2], (DEPTH, M_HEADS), f32)], axis=-1)
    return {
        'x_prompt': nrm(ks[3], (BATCH, SEQ, D_MODEL), f32),
        'x_sample': nrm(ks[4], (DEC_BATCH, DEC_SEQ, D_MODEL), f32),
        'cache_k': nrm(ks[5], (DEPTH, n_phys, PAGE_SIZE, SB_HEADS, SB_HEAD_DIM), f32),
        'cache_v': nrm(ks[6], (DEPTH, n_phys, PAGE_SIZE, SB_HEADS, SB_HEAD_DIM), f32),
        'state_mlstm_C': 0.1 * nrm(ks[7], (DEPTH, DEC_BATCH, M_HEADS, M_HEAD_DIM, M_HEAD_DIM), f32),
        'state_mlstm_n': 0.5 * nrm(ks[8], (DEPTH, DEC_BATCH, M_HEADS, M_HEAD_DIM), f32),
        'state_mlstm_m': nrm(ks[9], (DEPTH, DEC_BATCH, M_HEADS), f32),
        'state_conv': nrm(ks[10], (DEPTH, DEC_BATCH, CONV_K - 1, CONV_WIDTH), f32),
        'page_table': page_table,
        'p_prompt': nrm(ks[11], (DEPTH, BATCH, SEQ, PLE_DIM), f32),
        'p_sample': nrm(ks[12], (DEPTH, DEC_BATCH, DEC_SEQ, PLE_DIM), f32),
        'g_mix': 1.0 + 0.05 * nrm(ks[13], (DEPTH, D_MODEL), f32),
        'w_in': nrm(ks[14], (DEPTH, D_MODEL, N_IN), f32) * D_MODEL ** -0.5,
        'b_if': b_if,
        'b_sb': SB_BIAS_INIT + 0.1 * nrm(ks[25], (DEPTH, SB_HEADS), f32),
        'conv_w': nrm(ks[15], (DEPTH, CONV_K, CONV_WIDTH), f32) * CONV_K ** -0.5,
        'w_branch': nrm(ks[16], (DEPTH, N_BRANCH, BRANCH_WIDTH, D_MODEL), f32) * BRANCH_WIDTH ** -0.5,
        'w_out': nrm(ks[17], (DEPTH, D_MODEL, D_MODEL), f32) * D_MODEL ** -0.5,
        'g_mlp': 1.0 + 0.05 * nrm(ks[18], (DEPTH, D_MODEL), f32),
        'w_up': nrm(ks[19], (DEPTH, D_MODEL, FFN_DIM), f32) * D_MODEL ** -0.5,
        'w_down': nrm(ks[20], (DEPTH, FFN_DIM, D_MODEL), f32) * FFN_DIM ** -0.5,
        'g_ple': 1.0 + 0.05 * nrm(ks[21], (DEPTH, D_MODEL), f32),
        'w_ple_gate': nrm(ks[22], (DEPTH, D_MODEL, D_MODEL), f32) * D_MODEL ** -0.5,
        'w_ple': nrm(ks[23], (DEPTH, PLE_DIM, D_MODEL), f32) * PLE_DIM ** -0.5,
        'g_final': 1.0 + 0.05 * nrm(ks[24], (D_MODEL,), f32),
    }

def reference(x_prompt, x_sample, cache_k, cache_v, state_mlstm_C, state_mlstm_n, state_mlstm_m,
              state_conv, page_table, p_prompt, p_sample, g_mix, w_in, b_if, b_sb, conv_w, w_branch,
              w_out, g_mlp, w_up, w_down, g_ple, w_ple_gate, w_ple, g_final):
    f32 = jnp.float32
    Bp = x_prompt.shape[0]
    Bs = x_sample.shape[0]
    past_len = page_table.shape[1] * cache_k.shape[2]
    mlstm_zero = (jnp.zeros((Bp, M_HEADS, M_HEAD_DIM, M_HEAD_DIM), f32),
                  jnp.zeros((Bp, M_HEADS, M_HEAD_DIM), f32),
                  jnp.zeros((Bp, M_HEADS), f32))
    conv_zero = jnp.zeros((Bp, CONV_K - 1, CONV_WIDTH), x_prompt.dtype)
    hp, hs = x_prompt, x_sample
    sp_all, ss_all = [], []
    for li in range(DEPTH):
        w = (g_mix[li], w_in[li], b_if[li], b_sb[li], conv_w[li], w_branch[li], w_out[li], g_mlp[li],
             w_up[li], w_down[li], g_ple[li], w_ple_gate[li], w_ple[li])
        hp, sp = decoder_layer(hp, p_prompt[li], w, mlstm_zero, conv_zero, None)
        pk = cache_k[li][page_table].reshape(Bs, past_len, SB_HEADS, SB_HEAD_DIM)
        pv = cache_v[li][page_table].reshape(Bs, past_len, SB_HEADS, SB_HEAD_DIM)
        hs, ss = decoder_layer(hs, p_sample[li], w,
                               (state_mlstm_C[li], state_mlstm_n[li], state_mlstm_m[li]),
                               state_conv[li], (pk, pv))
        sp_all.append(sp)
        ss_all.append(ss)
    y_prompt = rmsnorm(hp, g_final)
    y_sample = rmsnorm(hs, g_final)
    k_p, v_p, C_p, n_p, m_p, conv_p = [jnp.stack([s[j] for s in sp_all]) for j in range(6)]
    k_s, v_s, C_s, n_s, m_s, conv_s = [jnp.stack([s[j] for s in ss_all]) for j in range(6)]
    return (y_prompt, y_sample, k_p, v_p, C_p, n_p, m_p, conv_p, k_s, v_s, C_s, n_s, m_s, conv_s)


_drawn_inputs = setup_inputs


def setup_inputs(seed=0):
    import zlib

    import numpy as np

    out = dict(_drawn_inputs(seed))
    spreads = {}
    factors = {'b_sb': 8.0, 'g_ple': 21.969}
    for name, (base, spread) in spreads.items():
        noise = np.random.default_rng([zlib.crc32(name.encode()), seed]).standard_normal(out[name].shape)
        drawn = base * np.exp(spread * noise) if base else spread * noise
        out[name] = __import__('jax').numpy.asarray(drawn.astype(out[name].dtype))
    for name, factor in factors.items():
        out[name] = (out[name] * factor).astype(out[name].dtype)
    return out
```

```python
from contextlib import ExitStack

import concourse.bass as bass
from concourse import mybir
from concourse.alu_op_type import AluOpType as ALU

ACT = mybir.ActivationFunctionType
F32 = mybir.dt.float32
F32R = mybir.dt.float32r
I32 = mybir.dt.int32
AX = mybir.AxisListType

P = 128
D = 1024
KD = D // P
T = 1024
TB = T // P
B = 8
TT = T + B
NCH = 3
CW = TT // NCH
H = 4
W = H * P
PAGES = 8
N_PHYS = 80
FFN = 4 * D
PLE = 256
EPS = 1e-6
HD_SCALE = float(P) ** -0.5
BIG = 1e30
EXP_LN = "natural_log_exp_and_others"

C_MQ, C_MK, C_MV, C_MO, C_IF = 0, W, 2 * W, 3 * W, 4 * W
C_CB = 4 * W + 2 * H
C_CC, C_CX = C_CB + W, C_CB + 2 * W
C_SQ = C_CB + 3 * W
C_SK, C_SV = C_SQ + W, C_SQ + 2 * W
C_G = C_SQ + 3 * W
N_IN = C_G + 3 * D


class Chip:

    def __init__(self, nc, io):
        self.nc = nc
        self.io = io
        self.blocks = 0
        self.loads = 0
        self.phase_sems = []

    def sb(self, ctx, name, shape, dt=F32):
        return ctx.enter_context(self.nc.sbuf_tensor(name, shape, dt))

    def ps(self, ctx, name, shape, dt=F32):
        return ctx.enter_context(self.nc.psum_tensor(name, shape, dt))

    def sem(self, ctx, name):
        handle = self.nc.alloc_semaphore(name=name)
        self.phase_sems.append(handle)
        return handle

    def retire_semaphores(self):
        with self.nc.Block() as block:
            @block.gpsimd
            def _(pool):
                for sem in self.phase_sems:
                    pool.sem_clear(sem)
        for sem in self.phase_sems:
            self.nc.release_semaphore(sem)
        self.phase_sems = []



def load_weights(k, sp, n, par, src, kb=KD):
    sp.wait_ge(k.w_split, n + 1)
    sp.dma_start(k.w_raw[:, par, 0:kb, :], src).then_inc(k.w_landed[par], 16)


def split_weights(k, pool, n, par, pair, kb=KD):
    nc = k.nc
    pool.wait_ge(k.acc_ready, n * NCH + NCH)
    pool.sem_inc(k.pool_tick, 1)
    pool.wait_ge(k.w_landed[par], pair * 16 + 16)
    pool.sem_inc(k.pool_tick, 1)
    nc.gpsimd.tensor_scalar(k.w_hi[:, par, 0:kb, :], k.w_raw[:, par, 0:kb, :], 1.0, 1.0,
                            ALU.mult, ALU.mult).then_inc(k.w_rounded, 1)
    pool.wait_ge(k.w_rounded, n + 1)
    nc.gpsimd.tensor_tensor(k.w_lo[:, par, 0:kb, :], k.w_raw[:, par, 0:kb, :],
                            k.w_hi[:, par, 0:kb, :].bitcast(F32), ALU.subtract).then_inc(k.w_split, 1)


def project_chunk(k, pe, n, par, c, x_hi, x_lo, kb=KD, k0=0):
    if c == 0:
        pe.wait_ge(k.w_split, n + 3)
    pe.wait_ge(k.acc_free, n * NCH + c + 1)
    cols = slice(c * CW, (c + 1) * CW)
    for i in range(kb):
        for j, (w, x) in enumerate(((k.w_hi, x_hi), (k.w_hi, x_lo), (k.w_lo, x_hi))):
            mm = k.nc.tensor.matmul(k.acc[:, c, 0:CW], w[:, par, i, :], x[:, k0 + i, cols],
                                    start=(i == 0 and j == 0), stop=(i == kb - 1 and j == 2))
    mm.then_inc(k.acc_ready, 1)


def acc_wait(k, eng, n, c):
    eng.wait_ge(k.acc_ready, n * NCH + c + 1 + 2 * NCH)


def constants(k):
    nc, io = k.nc, k.io
    with nc.Block() as block:
        @block.gpsimd
        def _(pool):
            nc.gpsimd.memset(k.ident[:, :], 0.0)
            nc.gpsimd.memset(k.zeros[:, :], 0.0)
            nc.gpsimd.memset(k.ones[:, :], 1.0)
            nc.gpsimd.memset(k.neg_ones[:, :], -1.0)
            nc.gpsimd.memset(k.sum_to[:, :], 1.0)
            nc.gpsimd.memset(k.neg_from[:, :], -1.0)
            nc.gpsimd.memset(k.late_big[:, :], 0.0)
            nc.gpsimd.memset(k.late_neg[:, :], 0.0)
            nc.gpsimd.memset(k.eps[:, :], EPS)
            nc.gpsimd.memset(k.before[:, :], 1.0)
            pool.drain()
            nc.gpsimd.affine_select(out=k.before[:, :], in_=k.before[:, :], compare_op=ALU.is_gt, fill=0.0,
                                    base=0, pattern=[[1, P]], channel_multiplier=-1)
            nc.gpsimd.affine_select(out=k.ident[:, :], in_=k.ident[:, :], compare_op=ALU.not_equal, fill=1.0,
                                    base=0, pattern=[[-1, P]], channel_multiplier=1)
            nc.gpsimd.affine_select(out=k.sum_to[:, :], in_=k.sum_to[:, :], compare_op=ALU.is_ge, fill=0.0,
                                    base=0, pattern=[[1, P]], channel_multiplier=-1)
            nc.gpsimd.affine_select(out=k.neg_from[:, :], in_=k.neg_from[:, :], compare_op=ALU.is_ge, fill=0.0,
                                    base=0, pattern=[[-1, P]], channel_multiplier=1)
            nc.gpsimd.affine_select(out=k.late_big[:, :], in_=k.late_big[:, :], compare_op=ALU.is_ge, fill=BIG,
                                    base=0, pattern=[[1, P]], channel_multiplier=-1)
            nc.gpsimd.affine_select(out=k.late_neg[:, :], in_=k.late_neg[:, :], compare_op=ALU.is_ge, fill=-BIG,
                                    base=0, pattern=[[-1, P]], channel_multiplier=1)
            pool.sem_inc(k.w_split, 2)
            pool.sem_inc(k.acc_ready, 2 * NCH)
            pool.sem_inc(k.acc_free, NCH)

        @block.sync
        def _(sp):
            def column(dst, src):
                sp.dma_start(dst, src, allow_slow_non_contiguous=True).then_inc(k.params_in, 16)
            column(k.g_mix[:, :], io["g_mix"].rearrange("l (k p) -> p (l k)", p=P))
            column(k.g_mlp[:, :], io["g_mlp"].rearrange("l (k p) -> p (l k)", p=P))
            column(k.g_ple[:, :], io["g_ple"].rearrange("l (k p) -> p (l k)", p=P))
            column(k.b_if[:, :], io["b_if"].to_broadcast([P, 2 * H]))
            column(k.b_sb[:, :], io["b_sb"].to_broadcast([P, H]))
            for j in range(3):
                column(k.conv_w[:, j, :], io["conv_w"][0, j, :].rearrange("(k p) -> p k", p=P))
            sp.wait_ge(k.params_in, 8 * 16)


def normalise_input(k):
    nc, io = k.nc, k.io
    tiles = [(t * P, P) for t in range(TB)] + [(T, B)]
    with ExitStack() as ctx:
        rows = k.sb(ctx, "x_rows", [P, 2, D])
        scaled = k.sb(ctx, "x_scaled", [P, 2, D])
        sums = k.sb(ctx, "x_sums", [P, len(tiles)])
        rstd = k.sb(ctx, "x_rstd", [P, 2 * len(tiles)])
        turned = k.sb(ctx, "x_turned", [P, 2, KD, P])
        gained = k.sb(ctx, "x_gained", [P, 2, KD, P])
        pt_x = k.ps(ctx, "pt_x", [P, KD, P])
        pt_s = k.ps(ctx, "pt_s", [P, KD, P])
        rows_in = [k.sem(ctx, f"rows_in{i}") for i in range(2)]
        x_out = [k.sem(ctx, f"x_out{i}") for i in range(2)]
        squared, scaled_ok, turned_x, turned_s, x_read, s_read, rounded, split, rms = (
            k.sem(ctx, n) for n in ("squared", "scaled_ok", "turned_x", "turned_s", "x_read", "s_read",
                                    "rounded", "split", "rms"))
        x_p = io["x_prompt"].rearrange("b t d -> (b t) d")
        x_s = io["x_sample"].rearrange("b t d -> (b t) d")
        with nc.Block() as block:
            @block.sync
            def _(sp):
                def store(i):
                    t0, m = tiles[i]
                    sp.wait_ge(x_read, i + 1)
                    sp.dma_start(k.x_T[:, :, t0:t0 + m], turned[:, i % 2, :, 0:m]).then_inc(x_out[i % 2], 16)

                for i, (t0, m) in enumerate(tiles):
                    if i >= 2:
                        sp.wait_ge(scaled_ok, i - 1)
                        sp.wait_ge(turned_x, i - 1)
                    src = x_p[t0:t0 + m, :] if t0 < T else x_s
                    sp.dma_start(rows[0:m, i % 2, :], src).then_inc(rows_in[i % 2], 16)
                    if i >= 2:
                        store(i - 2)
                store(len(tiles) - 2)
                store(len(tiles) - 1)
                for i in range(2):
                    sp.wait_ge(x_out[i], 16 * len(tiles[i::2]))

            @block.scalar
            def _(act):
                act.preload_act_table_set("sqrt_and_others")
                for i, (t0, m) in enumerate(tiles):
                    act.wait_ge(rows_in[i % 2], 16 * (i // 2 + 1))
                    if i >= 2:
                        act.wait_ge(turned_s, i - 1)
                    nc.scalar.activation(scaled[0:m, i % 2, :], rows[0:m, i % 2, :], ACT.Square,
                                         accum_out=sums[0:m, i:i + 1]).then_inc(squared, 1)
                    act.wait_ge(squared, i + 1)
                    act.wait_ge(k.params_in, 8 * 16)
                    nc.scalar.activation(rstd[0:m, 2 * i:2 * i + 1], sums[0:m, i:i + 1], ACT.Sqrt,
                                         scale=1.0 / D, bias=k.eps[0:m, :]).then_inc(rms, 1)
                    act.wait_ge(turned_x, i + 1)
                    if i >= 2:
                        act.wait_ge(x_out[i % 2], 16 * (i // 2))
                    nc.scalar.activation(turned[:, i % 2, :, 0:m], pt_x[:, :, 0:m], ACT.Copy).then_inc(x_read, 1)
                    act.wait_ge(s_read, i + 1)
                    nc.scalar.activation(k.x_hi[:, :, t0:t0 + m], gained[:, i % 2, :, 0:m], ACT.Copy)\
                       .then_inc(rounded, 1)

            @block.vector
            def _(dve):
                for i, (t0, m) in enumerate(tiles):
                    dve.wait_ge(rms, i + 1)
                    nc.vector.reciprocal(rstd[0:m, 2 * i + 1:2 * i + 2], rstd[0:m, 2 * i:2 * i + 1])
                    dve.drain()
                    nc.vector.tensor_scalar(scaled[0:m, i % 2, :], rows[0:m, i % 2, :],
                                            rstd[0:m, 2 * i + 1:2 * i + 2], None, ALU.mult).then_inc(scaled_ok, 1)
                    dve.wait_ge(turned_s, i + 1)
                    if i >= 2:
                        dve.wait_ge(split, i - 1)
                    nc.vector.tensor_tensor(gained[:, i % 2, :, 0:m], pt_s[:, :, 0:m],
                                            k.g_mix[:, :].unsqueeze(2).to_broadcast([P, KD, m]),
                                            ALU.mult).then_inc(s_read, 1)

            @block.gpsimd
            def _(pool):
                for i, (t0, m) in enumerate(tiles):
                    pool.wait_ge(rounded, i + 1)
                    nc.gpsimd.tensor_tensor(k.x_lo[:, :, t0:t0 + m], gained[:, i % 2, :, 0:m],
                                            k.x_hi[:, :, t0:t0 + m].bitcast(F32), ALU.subtract).then_inc(split, 1)

            @block.tensor
            def _(pe):
                for i, (t0, m) in enumerate(tiles):
                    pe.wait_ge(rows_in[i % 2], 16 * (i // 2 + 1))
                    if i:
                        pe.wait_ge(x_read, i)
                    for b in range(KD):
                        tr = nc.tensor.transpose(pt_x[:, b, 0:m], rows[0:m, i % 2, b * P:(b + 1) * P],
                                                 k.ident[0:m, 0:m])
                    tr.then_inc(turned_x, 1)
                    pe.wait_ge(scaled_ok, i + 1)
                    if i:
                        pe.wait_ge(s_read, i)
                    for b in range(KD):
                        tr = nc.tensor.transpose(pt_s[:, b, 0:m], scaled[0:m, i % 2, b * P:(b + 1) * P],
                                                 k.ident[0:m, 0:m])
                    tr.then_inc(turned_s, 1)


def project_groups(k, name, groups, gates=()):
    with ExitStack() as ctx:
        _project_groups(k, ctx, name, groups, gates)


def _project_groups(k, ctx, name, groups, gates):
    nc = k.nc
    base = k.blocks
    gate_out = k.sb(ctx, name + "_gate_out", [P, 2, TT]) if gates else None
    gate_sent = [k.sem(ctx, f"{name}_gate_sent{b}") for b in range(2)]
    if gates:
        groups = groups + [dict(groups[0], col=C_G + gates[0] * P, blocks=len(gates), out=None, scale=1.0, func=ACT.Copy)]
    with nc.Block() as block:
        def walk(eng, step):
            n = base
            for g in groups:
                with eng.Fori(0, g["blocks"] // 2) as i:
                    for par in range(2):
                        step(g, n + i * 2 + par, par, n // 2 + i, i * 2 + par)
                n += g["blocks"]

        @block.sync
        def _(sp):
            def step(g, n, par, pair, b):
                load_weights(k, sp, n, par, g["w"][:, :, bass.ds(b * P + g["col"], P)], g["kb"])
            walk(sp, step)

        @block.gpsimd
        def _(pool):
            walk(pool, lambda g, n, par, pair, b: split_weights(k, pool, n, par, pair, g["kb"]))

        @block.tensor
        def _(pe):
            def step(g, n, par, pair, b):
                for c in range(NCH):
                    project_chunk(k, pe, n, par, c, g["hi"], g["lo"], g["kb"])
            walk(pe, step)

        @block.scalar
        def _(act):
            def step(g, n, par, pair, b):
                to_dram = g["out"] is None
                if to_dram:
                    act.wait_ge(gate_sent[par], (b - par) * 8)
                out = gate_out[:, par:par + 1, :] if to_dram else g["out"](b)
                for c in range(NCH):
                    acc_wait(k, act, n, c)
                    nc.scalar.activation(out[:, :, c * CW:(c + 1) * CW], k.acc[:, c:c + 1, 0:CW],
                                         g["func"], scale=g["scale"]).then_inc(k.acc_free, 1)
                if to_dram:
                    act.wait_ge(k.acc_free, (n + 1) * NCH + NCH)
                    act.dma_start(k.gates[:, bass.ds(b + gates[0], 1), :], out).then_inc(gate_sent[par], 16)
            walk(act, step)
            if gates:
                for par in range(2):
                    act.wait_ge(gate_sent[par], len(gates) // 2 * 16)
    k.blocks = base + sum(g["blocks"] for g in groups)


def turn_states(k):
    nc, io = k.nc, k.io
    with ExitStack() as ctx:
        conv_rows = k.sb(ctx, "conv_rows", [2 * B, W])
        n_rows = k.sb(ctx, "n_rows", [B * H, P])
        pt = k.ps(ctx, "pt_states", [P, 512])
        rows_in, turned = k.sem(ctx, "states_in"), k.sem(ctx, "states_turned")
        with nc.Block() as block:
            @block.sync
            def _(sp):
                sp.dma_start(conv_rows[:, :], io["state_conv"].rearrange("l b s c -> (l b s) c")).then_inc(rows_in, 16)
                sp.dma_start(n_rows[:, :], io["state_mlstm_n"].rearrange("l b h d -> (l b h) d")).then_inc(rows_in, 16)
                sp.dma_start(io["conv_sample"][0, :, 0, :], io["state_conv"][0, :, 1, :]).then_inc(rows_in, 16)
                sp.wait_ge(rows_in, 48)

            @block.tensor
            def _(pe):
                pe.wait_ge(rows_in, 48)
                for h in range(H):
                    nc.tensor.transpose(pt[:, h * 2 * B:(h + 1) * 2 * B], conv_rows[:, h * P:(h + 1) * P],
                                        k.ident[0:2 * B, 0:2 * B])
                nc.tensor.transpose(pt[:, 128:128 + B * H], n_rows[:, :], k.ident[0:B * H, 0:B * H]).then_inc(turned, 1)

            @block.vector
            def _(dve):
                dve.wait_ge(turned, 1)
                nc.vector.tensor_copy(k.conv_state[:, :, :], pt[:, 0:H * 2 * B].rearrange("p (h c) -> p h c", h=H))
                nc.vector.tensor_copy(k.n_old[:, :], pt[:, 128:128 + B * H])


UNITS = [(half, kb, max(0, kb * P - half * 512)) for half in range(2) for kb in range(4 * half + 3, -1, -1)]
NU = len(UNITS)


def unit_is_first(u):
    return u == 0 or UNITS[u][0] != UNITS[u - 1][0]


def unit_is_diagonal(u):
    return UNITS[u][1] >= 4 * UNITS[u][0]


NDIAG = sum(unit_is_diagonal(u) for u in range(NU))
DIAG_BEFORE = [sum(unit_is_diagonal(v) for v in range(u)) for u in range(NU + 1)]


def stick_breaking_prompt(k, s_T):
    nc, io = k.nc, k.io
    base = k.blocks
    NB = 4
    SLOTS = NB * NCH
    cols = (C_CC, C_CX, C_CB, C_G)
    w_in = io["w_in"].rearrange("l (k p) n -> p (l k) n", p=P)
    with ExitStack() as ctx:
        k_head = k.sb(ctx, "k_head", [P, TT])
        v_head = k.sb(ctx, "v_head", [P, TT])
        k_tok = k.sb(ctx, "k_tok", [P, TB, P])
        v_tok = k.sb(ctx, "v_tok", [P, TB, P])
        kv_dec = k.sb(ctx, "kv_dec", [B, 2, P])
        bias = k.sb(ctx, "sb_bias", [P, 1])
        z_abs = k.sb(ctx, "z_abs", [P, 2, 512])
        z_in = k.sb(ctx, "z_in", [P, 2, 512])
        sp_ = k.sb(ctx, "softplus", [P, 2, 512])
        later = k.sb(ctx, "sp_later", [P, 2, 512])
        prob = k.sb(ctx, "prob", [P, 2, 512])
        y_out = k.sb(ctx, "y_stick", [P, T])
        proj = k.sb(ctx, "proj_out", [P, NB, TT])
        cx = k.sb(ctx, "cx", [P, 2 + TT])
        conv = proj[:, 1, :]
        tails = k.sb(ctx, "cx_tails", [P, H, 2 + B])
        tail_rows = y_out[0:2 + B, 0:W]
        z = k.ps(ctx, "z", [P, 3, 512])
        y = k.ps(ctx, "y", [P, 2, 512])
        names = ("staged", "bias_ready", "kv_turned", "v_ready", "kv_ready", "z_ready", "abs_ready", "z_read", "exp_ready", "log_ready",
                 "sp_ready", "later_ready", "sums_added", "exp_done", "prob_ready", "av_done", "y_ready", "y_read",
                 "k_out", "v_out", "kd_out", "vd_out", "y_sent", "conv_sent", "gate_sent", "cx_ready", "conv_ready",
                 "tails_turned", "tails_ready", "tails_out", "gate_ready")
        s = {n: k.sem(ctx, "sb_" + n) for n in names}
        with nc.Block() as block:
            @block.sync
            def _(sp):
                with sp.Fori(0, H) as j:
                    for b in range(NB):
                        load_weights(k, sp, base + j * NB + b, b % 2, w_in[:, :, bass.ds(j * P + cols[b], P)])
                sp.wait_ge(s["tails_ready"], 1)
                sp.dma_start(io["conv_prompt"][0, 0, :, :], tail_rows[0:2, :]).then_inc(s["tails_out"], 16)
                sp.dma_start(io["conv_sample"][0, :, 1, :], tail_rows[2:2 + B, :]).then_inc(s["tails_out"], 16)
                sp.wait_ge(s["tails_out"], 32)

            @block.tensor
            def _(pe):
                def turn_kv(j):
                    pe.wait_ge(s["staged"], j + 1)
                    pe.wait_ge(s["exp_done"], j * NU)
                    pe.wait_ge(s["y_read"], j * 2)
                    for tb in range(TB):
                        nc.tensor.transpose(z[:, tb // 4, (tb % 4) * P:(tb % 4 + 1) * P],
                                            v_head[:, tb * P:(tb + 1) * P], k.ident[:, :])
                    nc.tensor.transpose(z[0:B, 2, 0:P], v_head[:, T:TT], k.ident[:, :])
                    for tb in range(TB):
                        nc.tensor.transpose(y[:, tb // 4, (tb % 4) * P:(tb % 4 + 1) * P],
                                            k_head[:, tb * P:(tb + 1) * P], k.ident[:, :])
                    nc.tensor.transpose(z[0:B, 2, P:2 * P], k_head[:, T:TT], k.ident[:, :]).then_inc(s["kv_turned"], 1)

                def scores(j, u):
                    half, kb, first = UNITS[u]
                    if u == 0:
                        pe.wait_ge(s["v_ready"], j + 1)
                        pe.wait_ge(s["kv_ready"], j + 1)
                    if u >= 3:
                        pe.wait_ge(s["exp_done"], j * NU + u - 2)
                    nc.tensor.matmul(z[:, u % 3, first:512], k_head[:, kb * P:(kb + 1) * P],
                                     s_T[:, bass.ds(j, 1), half * 512 + first:(half + 1) * 512],
                                     start=True, stop=True).then_inc(s["z_ready"], 1)

                def sums(j, u):
                    half, kb, first = UNITS[u]
                    pe.wait_ge(s["sp_ready"], j * NU + u + 1)
                    mm = nc.tensor.matmul(z[:, u % 3, first:512], k.neg_from[:, :], sp_[:, u % 2, first:512],
                                          start=False, stop=True, skip_group_check=True)
                    if not unit_is_first(u):
                        pe.wait_ge(s["later_ready"], j * NU + u)
                        before = UNITS[u - 1][2]
                        mm = nc.tensor.matmul(z[:, u % 3, before:512], k.neg_ones[:, :], later[:, (u - 1) % 2, before:512],
                                              start=False, stop=True, skip_group_check=True)
                    mm.then_inc(s["sums_added"], 1)

                def values(j, u):
                    half, kb, first = UNITS[u]
                    pe.wait_ge(s["exp_done"], j * NU + u + 1)
                    if unit_is_diagonal(u):
                        pe.wait_ge(s["prob_ready"], j * NDIAG + DIAG_BEFORE[u] + 1)
                    nc.tensor.matmul(y[:, half, first:512], v_tok[:, kb, :], prob[:, u % 2, first:512],
                                     start=unit_is_first(u), stop=(kb == 0), skip_group_check=True)\
                        .then_inc(s["av_done"], 1)

                with pe.Fori(0, H) as j:
                    for slot in range(SLOTS + 3):
                        if slot < SLOTS:
                            b, c = divmod(slot, NCH)
                            project_chunk(k, pe, base + j * NB + b, b % 2, c, k.x_hi, k.x_lo)
                        if slot == 0:
                            turn_kv(j)
                        if 0 <= slot - 1 < NU:
                            scores(j, slot - 1)
                        if 0 <= slot - 2 < NU:
                            sums(j, slot - 2)
                        if 0 <= slot - 3 < NU:
                            values(j, slot - 3)
                pe.wait_ge(s["conv_ready"], H)
                for h in range(H):
                    tr = nc.tensor.transpose(z[0:2 + B, 0, h * P:(h + 1) * P], tails[:, h, :], k.ident[:, :])
                tr.then_inc(s["tails_turned"], 1)

            @block.scalar
            def _(act):
                act.preload_act_table_set(EXP_LN)

                def softplus_log(j, u):
                    _, _, first = UNITS[u]
                    act.wait_ge(s["z_read"], j * NU + u + 1)
                    act.wait_ge(s["sp_ready"], j * NU + max(u - 1, 0))
                    nc.scalar.activation(z_abs[:, u % 2, first:512], z_in[:, u % 2, first:512], ACT.Abs).then_inc(s["abs_ready"], 1)
                    act.wait_ge(s["abs_ready"], j * NU + u + 1)
                    nc.scalar.activation(z_abs[:, u % 2, first:512], z_abs[:, u % 2, first:512], ACT.Exp,
                                         scale=-1.0).then_inc(s["exp_ready"], 1)
                    act.wait_ge(s["exp_ready"], j * NU + u + 1)
                    nc.scalar.activation(z_abs[:, u % 2, first:512], z_abs[:, u % 2, first:512], ACT.Ln,
                                         bias=1.0).then_inc(s["log_ready"], 1)

                def probs(j, u):
                    _, _, first = UNITS[u]
                    act.wait_ge(s["sums_added"], j * NU + u + 1)
                    if u >= 2:
                        act.wait_ge(s["av_done"], j * NU + u - 1)
                    nc.scalar.activation(prob[:, u % 2, first:512], z[:, u % 3, first:512], ACT.Exp,
                                         bias=bias[:, :]).then_inc(s["exp_done"], 1)

                with act.Fori(0, H) as j:
                    act.wait_ge(s["z_ready"], j * NU)
                    nc.scalar.activation(k_head[:, :].unsqueeze(1), s_T[:, bass.ds(j + H, 1), :], ACT.Copy)
                    nc.scalar.activation(v_head[:, :].unsqueeze(1), s_T[:, bass.ds(j + 2 * H, 1), :], ACT.Copy)\
                      .then_inc(s["staged"], 1)
                    for slot in range(SLOTS + 2):
                        if slot < SLOTS:
                            b, c = divmod(slot, NCH)
                            if slot == 0:
                                act.wait_ge(s["cx_ready"], j)
                            if slot == NCH:
                                act.wait_ge(s["conv_sent"], j * 16)
                            if slot == 2 * NCH:
                                act.wait_ge(s["conv_ready"], j)
                            if slot == 3 * NCH:
                                act.wait_ge(s["gate_sent"], j * 16)
                            acc_wait(k, act, base + j * NB + b, c)
                            nc.scalar.activation(proj[:, b, c * CW:(c + 1) * CW], k.acc[:, c, 0:CW], ACT.Copy)\
                              .then_inc(k.acc_free, 1)
                        if slot == 0:
                            act.wait_ge(s["kv_turned"], j + 1)
                            act.wait_ge(s["v_out"], j * 16)
                            act.wait_ge(s["av_done"], j * NU)
                            nc.scalar.activation(v_tok[:, :, :], z[:, 0:2, :].rearrange("p a (b d) -> p (a b) d", d=P),
                                                 ACT.Copy).then_inc(s["v_ready"], 1)
                            act.wait_ge(s["v_ready"], j + 1)
                            act.dma_start(io["v_prompt"][0, 0, :, bass.ds(j, 1), :].rearrange("(b p) o d -> p (b o) d", p=P),
                                          v_tok[:, :, :]).then_inc(s["v_out"], 16)
                            act.wait_ge(s["kv_ready"], j + 1)
                            act.dma_start(io["k_prompt"][0, 0, :, bass.ds(j, 1), :].rearrange("(b p) o d -> p (b o) d", p=P),
                                          k_tok[:, :, :]).then_inc(s["k_out"], 16)
                            act.dma_start(io["v_sample"][0, :, 0, bass.ds(j, 1), :].rearrange("b o d -> b (o d)"),
                                          kv_dec[:, 0, :]).then_inc(s["vd_out"], 16)
                            act.dma_start(io["k_sample"][0, :, 0, bass.ds(j, 1), :].rearrange("b o d -> b (o d)"),
                                          kv_dec[:, 1, :]).then_inc(s["kd_out"], 16)
                        if 0 <= slot - 1 < NU:
                            softplus_log(j, slot - 1)
                        if 0 <= slot - 2 < NU:
                            probs(j, slot - 2)
                    act.wait_ge(k.acc_free, (base + j * NB + NB) * NCH + NCH)
                    act.dma_start(k.gates[:, bass.ds(j, 1), :], proj[:, 3:4, :]).then_inc(s["gate_sent"], 16)
                    act.wait_ge(s["conv_ready"], j + 1)
                    act.dma_start(k.branch[1, :, bass.ds(j, 1), :], proj[:, 1:2, :]).then_inc(s["conv_sent"], 16)
                    act.wait_ge(s["y_read"], j * 2 + 2)
                    act.dma_start(k.branch[2, :, bass.ds(j, 1), 0:T], y_out[:, :].unsqueeze(1)).then_inc(s["y_sent"], 16)
                for n in ("v_out", "k_out", "vd_out", "kd_out", "gate_sent", "conv_sent", "y_sent"):
                    act.wait_ge(s[n], 16 * H)

            @block.vector
            def _(dve):
                nc.vector.memset(cx[:, 0:2], 0.0)

                def softplus_parts(j, u):
                    _, _, first = UNITS[u]
                    dve.wait_ge(s["z_ready"], j * NU + u + 1)
                    nc.vector.tensor_scalar(z_in[:, u % 2, first:512], z[:, u % 3, first:512], bias[:, :], None,
                                            ALU.add).then_inc(s["z_read"], 1)

                def softplus_sum(j, u):
                    _, _, first = UNITS[u]
                    dve.wait_ge(s["log_ready"], j * NU + u + 1)
                    dve.wait_ge(s["z_read"], j * NU + u + 1)
                    if u >= 2:
                        dve.wait_ge(s["sums_added"], j * NU + u - 1)
                        dve.wait_ge(s["later_ready"], j * NU + u - 1)
                    nc.vector.scalar_tensor_tensor(out=sp_[:, u % 2, first:512], in0=z_in[:, u % 2, first:512], scalar=0.0,
                                                   in1=z_abs[:, u % 2, first:512], op0=ALU.max, op1=ALU.add)
                    if unit_is_diagonal(u):
                        dve.drain()
                        nc.vector.tensor_tensor(sp_[:, u % 2, first:first + P], sp_[:, u % 2, first:first + P],
                                                k.before[:, :], ALU.mult).then_inc(s["sp_ready"], 1)
                    else:
                        dve.drain().then_inc(s["sp_ready"], 1)

                def read_y(j, half):
                    u = 4 if half == 0 else NU
                    dve.wait_ge(s["av_done"], j * NU + u)
                    nc.vector.tensor_copy(y_out[:, half * 512:(half + 1) * 512], y[:, half, :]).then_inc(s["y_read"], 1)

                with dve.Fori(0, H) as j:
                    dve.wait_ge(s["exp_done"], j * NU)
                    nc.vector.tensor_copy(bias[:, :], k.b_sb[:, bass.ds(j, 1)]).then_inc(s["bias_ready"], 1)
                    dve.wait_ge(s["bias_ready"], j + 1)
                    dve.wait_ge(s["kv_turned"], j + 1)
                    dve.wait_ge(s["k_out"], j * 16)
                    dve.wait_ge(s["vd_out"], j * 16)
                    dve.wait_ge(s["kd_out"], j * 16)
                    nc.vector.tensor_copy(k_tok[:, :, :], y[:, :, :].rearrange("p a (b d) -> p (a b) d", d=P))
                    nc.vector.tensor_copy(kv_dec[:, :, :], z[0:B, 2, 0:2 * P].rearrange("p (a d) -> p a d", d=P))\
                      .then_inc(s["kv_ready"], 1)
                    for u in range(NU):
                        softplus_parts(j, u)
                        softplus_sum(j, u)
                        if u == 6:
                            dve.wait_ge(s["y_sent"], j * 16)
                            read_y(j, 0)
                        if u == 8:
                            dve.wait_ge(k.acc_free, (base + j * NB + 2) * NCH + NCH)
                            nc.vector.tensor_tensor(cx[:, 2:2 + TT], proj[:, 0, :], proj[:, 1, :],
                                                    ALU.mult).then_inc(s["cx_ready"], 1)
                    dve.wait_ge(k.acc_free, (base + j * NB + 3) * NCH + NCH)
                    dve.wait_ge(s["cx_ready"], j + 1)
                    nc.vector.tensor_scalar(conv[:, :], cx[:, 2:2 + TT], k.conv_w[:, 2, bass.ds(j, 1)], None, ALU.mult)
                    nc.vector.tensor_copy(tails[:, bass.ds(j, 1), :], cx[:, T:T + 2 + B].unsqueeze(1))
                    for tap in (1, 0):
                        dve.drain()
                        nc.vector.scalar_tensor_tensor(out=conv[:, 0:T], in0=cx[:, tap:tap + T],
                                                       scalar=k.conv_w[:, tap, bass.ds(j, 1)], in1=conv[:, 0:T],
                                                       op0=ALU.mult, op1=ALU.add)
                        nc.vector.scalar_tensor_tensor(out=conv[:, T:TT], in0=k.conv_state[:, bass.ds(j, 1), tap::2].squeeze(1),
                                                       scalar=k.conv_w[:, tap, bass.ds(j, 1)], in1=conv[:, T:TT],
                                                       op0=ALU.mult, op1=ALU.add)
                    dve.drain()
                    nc.vector.tensor_tensor(conv[:, :], conv[:, :], proj[:, 2, :], ALU.mult).then_inc(s["conv_ready"], 1)
                    read_y(j, 1)
                dve.wait_ge(s["tails_turned"], 1)
                dve.wait_ge(s["y_sent"], H * 16)
                nc.vector.tensor_copy(tail_rows[:, :], z[0:2 + B, 0, :]).then_inc(s["tails_ready"], 1)

            @block.gpsimd
            def _(pool):
                def add_later(j, u):
                    _, _, first = UNITS[u]
                    pool.wait_ge(s["sp_ready"], j * NU + u + 1)
                    if u >= 2:
                        pool.wait_ge(s["sums_added"], j * NU + u)
                    pool.wait_ge(s["later_ready"], j * NU + u)
                    before = 512 if unit_is_first(u) else UNITS[u - 1][2]
                    if first < before:
                        pool.sem_inc(k.pool_tick, 1)
                        op = nc.gpsimd.tensor_scalar(later[:, u % 2, first:before], sp_[:, u % 2, first:before], 1.0, 1.0,
                                                     ALU.mult, ALU.mult)
                    if before < 512:
                        op = nc.gpsimd.tensor_tensor(later[:, u % 2, before:512], later[:, (u - 1) % 2, before:512],
                                                     sp_[:, u % 2, before:512], ALU.add)
                    op.then_inc(s["later_ready"], 1)

                def mask_prob(j, u):
                    _, _, first = UNITS[u]
                    pool.wait_ge(s["exp_done"], j * NU + u + 1)
                    pool.sem_inc(k.pool_tick, 1)
                    nc.gpsimd.affine_select(out=prob[:, u % 2, first:first + P], in_=prob[:, u % 2, first:first + P],
                                            compare_op=ALU.is_gt, fill=0.0, base=0, pattern=[[1, P]],
                                            channel_multiplier=-1).then_inc(s["prob_ready"], 1)

                with pool.Fori(0, H) as j:
                    for slot in range(SLOTS + 2):
                        if slot % NCH == 0 and slot < SLOTS:
                            b = slot // NCH
                            n = base + j * NB + b
                            split_weights(k, pool, n, b % 2, base // 2 + j * (NB // 2) + b // 2)
                        if 0 <= slot - 1 < NU:
                            add_later(j, slot - 1)
                        if 0 <= slot - 2 < NU and unit_is_diagonal(slot - 2):
                            mask_prob(j, slot - 2)
    k.blocks = base + H * NB


N_E = 4
E_STATE, E_NEGM, E_KEY, E_DECAY = range(N_E)
GATE_COLS = TB * H


def gate_terms(k):
    nc, io = k.nc, k.io
    with ExitStack() as ctx:
        w_if = k.sb(ctx, "w_if", [P, KD, 2 * H])
        w_if2 = k.sb(ctx, "w_if2", [P, KD, 2, 2 * H], F32R)
        raw = k.sb(ctx, "if_raw", [P, TB + 1, 2 * H])
        f_abs = k.sb(ctx, "f_abs", [P, TB, H])
        log_f = k.sb(ctx, "log_f", [P, TB, H])
        total = k.sb(ctx, "log_f_total", [P, TB, H])
        b_sum = k.sb(ctx, "b_sum", [P, TB, H])
        spread = k.sb(ctx, "g_spread", [P, 2, H, P])
        junk = k.sb(ctx, "max_junk", [P, P])
        g_max = k.sb(ctx, "g_max", [P, TB, H])
        mu_last = k.sb(ctx, "mu_last", [P, TB, H])
        m_prev = k.sb(ctx, "m_prev", [P, TB + 1, H])
        gp = k.ps(ctx, "if_ps", [P, TB + 1, 2, 2 * H])
        sums = k.ps(ctx, "if_sums", [P, 2, GATE_COLS])
        g_rows = k.ps(ctx, "g_rows", [P, 2, 512])
        s = {n: k.sem(ctx, "gt_" + n) for n in (
            "w_in", "w_hi", "w_ready", "projected", "raw_ready", "log_ready", "log_f_ready", "summed", "spread_ready",
            "rows_ready", "rows_read", "exps_in", "m_out")}
        with nc.Block() as block:
            @block.sync
            def _(sp):
                sp.dma_start(w_if[:, :, :], io["w_in"].rearrange("l (k p) n -> p (l k) n", p=P)[:, :, C_IF:C_IF + 2 * H],
                             allow_slow_non_contiguous=True).then_inc(s["w_in"], 16)
                sp.wait_ge(s["exps_in"], 1)
                sp.dma_start(io["m_prompt"].rearrange("l b h -> (l b) h"), m_prev[0:1, TB, :]).then_inc(s["m_out"], 16)
                sp.wait_ge(s["m_out"], 16)

            @block.tensor
            def _(pe):
                pe.wait_ge(s["w_ready"], 1)
                for tb in range(TB + 1):
                    m = P if tb < TB else B
                    for i in range(KD):
                        nc.tensor.matmul(gp[0:m, tb, :, :], k.x_hi[:, i, tb * P:tb * P + m], w_if2[:, i, :, :],
                                         start=(i == 0), stop=False, skip_group_check=True)
                        mm = nc.tensor.matmul(gp[0:m, tb, 0, :], k.x_lo[:, i, tb * P:tb * P + m], w_if2[:, i, 0, :],
                                              start=False, stop=(i == KD - 1), skip_group_check=True)
                mm.then_inc(s["projected"], 1)
                pe.wait_ge(s["log_f_ready"], 1)
                flat = log_f[:, :, :].rearrange("p c h -> p (c h)")
                nc.tensor.matmul(sums[:, 0, :], k.sum_to[:, :], flat, start=True, stop=True)
                nc.tensor.matmul(sums[:, 1, :], k.ones[:, :], flat, start=True, stop=True).then_inc(s["summed"], 1)
                for c in range(TB):
                    pe.wait_ge(s["spread_ready"], c + 1)
                    if c >= 2:
                        pe.wait_ge(s["rows_read"], c - 1)
                    nc.tensor.matmul(g_rows[:, c % 2, :], k.ones[:, :], spread[:, c % 2, :, :], start=True, stop=True)\
                        .then_inc(s["rows_ready"], 1)

            @block.vector
            def _(dve):
                dve.wait_ge(s["w_in"], 16)
                nc.vector.tensor_copy(w_if2[:, :, 0, :], w_if[:, :, :])
                dve.drain()
                nc.vector.tensor_tensor(w_if2[:, :, 1, :], w_if[:, :, :], w_if2[:, :, 0, :].bitcast(F32),
                                        ALU.subtract).then_inc(s["w_ready"], 1)
                dve.wait_ge(s["projected"], 1)
                for tbs, m in ((slice(0, TB), P), (slice(TB, TB + 1), B)):
                    nc.vector.tensor_copy(raw[0:m, tbs, :], gp[0:m, tbs, 0, :])
                    dve.drain()
                    nc.vector.tensor_tensor(raw[0:m, tbs, :], raw[0:m, tbs, :], gp[0:m, tbs, 1, :], ALU.add)
                    dve.drain()
                nc.vector.tensor_tensor(raw[:, 0:TB, :], raw[:, 0:TB, :],
                                        k.b_if[:, :].unsqueeze(1).to_broadcast([P, TB, 2 * H]), ALU.add)
                nc.vector.tensor_tensor(k.gates_dec[:, :], raw[0:B, TB, :], k.b_if[0:B, :], ALU.add)
                dve.drain().then_inc(s["raw_ready"], 1)
                nc.vector.tensor_scalar(total[:, :, :], raw[:, 0:TB, H:2 * H], -1.0, 0.0, ALU.mult, ALU.max)
                dve.drain()
                dve.wait_ge(s["log_ready"], 1)
                nc.vector.scalar_tensor_tensor(out=log_f[:, :, :], in0=total[:, :, :], scalar=-1.0, in1=f_abs[:, :, :],
                                               op0=ALU.mult, op1=ALU.subtract).then_inc(s["log_f_ready"], 1)
                dve.wait_ge(s["summed"], 1)
                dve.wait_ge(s["log_f_ready"], 1)
                view = [P, TB, H]
                nc.vector.tensor_copy(b_sum[:, :, :], sums[:, 0, :].rearrange("p (c h) -> p c h", h=H))
                nc.vector.tensor_copy(total[:, :, :], sums[:, 1, :].rearrange("p (c h) -> p c h", h=H))
                nc.vector.memset(m_prev[:, 0, :], 0.0)
                dve.drain()
                nc.vector.tensor_tensor(k.g_col[:, :, :], raw[:, 0:TB, 0:H], b_sum[:, :, :], ALU.subtract)
                dve.drain()
                for c in range(TB):
                    if c >= 2:
                        dve.wait_ge(s["rows_ready"], c - 1)
                    nc.vector.tensor_tensor(spread[:, c % 2, :, :], k.ident[:, :].unsqueeze(1).to_broadcast([P, H, P]),
                                            k.g_col[:, c, :].unsqueeze(2).to_broadcast([P, H, P]),
                                            ALU.mult).then_inc(s["spread_ready"], 1)
                    dve.wait_ge(s["rows_ready"], c + 1)
                    rows = g_rows[:, c % 2, :].rearrange("p (h t) -> p h t", h=H)
                    nc.vector.tensor_reduce(g_max[:, c, :], rows, AX.X, ALU.max)
                    for h in range(H):
                        dve.drain()
                        op = nc.vector.tensor_tensor_reduce(junk[:, :], rows[:, h, :], k.late_neg[:, :], 1.0, -3.0e38,
                                                            ALU.add, ALU.max, k.mu[:, c, h:h + 1])
                    dve.drain().then_inc(s["rows_read"], 1)
                for c in range(TB):
                    nc.vector.tensor_tensor(mu_last[:, c, :], m_prev[:, c, :], g_max[:, c, :], ALU.max)
                    dve.drain()
                    nc.vector.tensor_tensor(m_prev[:, c + 1, :], total[:, c, :], mu_last[:, c, :], ALU.add)
                    dve.drain()
                nc.vector.tensor_tensor(k.mu[:, :, :], k.mu[:, :, :], m_prev[:, 0:TB, :], ALU.max)
                dve.drain()
                nc.vector.tensor_tensor(k.exps[:, E_STATE, :, :], m_prev[:, 0:TB, :], k.mu[:, :, :], ALU.subtract)
                nc.vector.scalar_tensor_tensor(out=k.exps[:, E_NEGM, :, :], in0=b_sum[:, :, :], scalar=-1.0,
                                               in1=k.mu[:, :, :], op0=ALU.mult, op1=ALU.subtract)
                nc.vector.tensor_tensor(k.exps[:, E_KEY, :, :], k.g_col[:, :, :], mu_last[:, :, :], ALU.subtract)
                nc.vector.tensor_tensor(k.exps[:, E_DECAY, :, :], m_prev[:, 0:TB, :], mu_last[:, :, :], ALU.subtract)
                dve.drain().then_inc(s["exps_in"], 1)

            @block.scalar
            def _(act):
                act.preload_act_table_set(EXP_LN)
                act.wait_ge(s["raw_ready"], 1)
                nc.scalar.activation(f_abs[:, :, :], raw[:, 0:TB, H:2 * H], ACT.Abs)
                act.drain()
                nc.scalar.activation(f_abs[:, :, :], f_abs[:, :, :], ACT.Exp, scale=-1.0)
                act.drain()
                nc.scalar.activation(f_abs[:, :, :], f_abs[:, :, :], ACT.Ln, bias=1.0).then_inc(s["log_ready"], 1)
                act.wait_ge(s["exps_in"], 1)
                nc.scalar.activation(k.exps[:, :, :, :], k.exps[:, :, :, :], ACT.Exp)


def mlstm_prompt(k, m_T):
    nc, io = k.nc, k.io
    base = k.blocks
    NB, FIRST_GATE = 2, H
    SLOTS = NB * NCH
    S_, M_, K_, V_, X_ = range(5)
    INTER, INTRA, STATE = (X_, K_), (M_, V_), (S_, X_)
    TURNED = K_
    w_in = io["w_in"].rearrange("l (k p) n -> p (l k) n", p=P)
    V1 = P + 1
    with ExitStack() as ctx:
        qkv = k.sb(ctx, "qkv", [P, 3, H, P])
        spread = k.sb(ctx, "mu_spread", [P, H, P])
        expo = k.sb(ctx, "expo", [P, H, P])
        w_T = k.sb(ctx, "w_T", [P, H, P])
        v_one = k.sb(ctx, "v_one", [P, H, V1])
        k_w = k.sb(ctx, "k_weighed", [P, H, P])
        inter = k.sb(ctx, "inter", [P, H, V1])
        num = k.sb(ctx, "num", [P, H, V1])
        den = k.sb(ctx, "den", [P, 3, H])
        h_tok = k.sb(ctx, "h_tok", [P, H, P])
        y_m = k.sb(ctx, "y_m", [P, H, P])
        state = k.sb(ctx, "state", [P, H, V1])
        gate_out = k.sb(ctx, "gate_out", [P, NB, TT])
        q = k.ps(ctx, "ml_ps", [P, 5, 512])
        s = {n: k.sem(ctx, "ml_" + n) for n in (
            "staged", "spread_ready", "pe1", "args_ready", "expo_ready", "weights_ready", "v_ready", "kw_ready", "pe2",
            "inter_ready", "num_ready", "h_ready", "pe3", "state_ready", "y_ready", "y_sent", "state_out")}
        gate_sent = [k.sem(ctx, f"gate_sent{b}") for b in range(NB)]

        def bank(i):
            return q[:, i, :].rearrange("p (h t) -> p h t", h=H)

        def pair(i):
            return q[:, i, 0:2 * V1].rearrange("p (h t) -> p h t", h=2)

        with nc.Block() as block:
            @block.sync
            def _(sp):
                with sp.Fori(0, TB) as c:
                    for b in range(NB):
                        load_weights(k, sp, base + c * NB + b, b, w_in[:, :, bass.ds((c * NB + b + FIRST_GATE) * P + C_G, P)])
                sp.wait_ge(s["state_ready"], TB + 1)
                sp.dma_start(io["C_prompt"][0, 0].rearrange("h d e -> d h e"), state[:, :, 0:P]).then_inc(s["state_out"], 16)
                sp.dma_start(io["n_prompt"][0, 0].rearrange("h d -> d h").unsqueeze(2), state[:, :, P:V1],
                             allow_slow_non_contiguous=True).then_inc(s["state_out"], 16)
                sp.wait_ge(s["state_out"], 32)

            @block.gpsimd
            def _(pool):
                with pool.Fori(0, TB) as c:
                    for b in range(NB):
                        split_weights(k, pool, base + c * NB + b, b, base // 2 + c)

            @block.tensor
            def _(pe):
                def turn_and_score(c):
                    pe.wait_ge(s["staged"], c + 1)
                    pe.wait_ge(s["state_ready"], c + 1)
                    pe.wait_ge(s["y_ready"], c)
                    pe.wait_ge(s["num_ready"], c)
                    for h in range(H):
                        nc.tensor.matmul(bank(S_)[:, h, :], qkv[:, 1, h, :], qkv[:, 0, h, :], start=True, stop=True)
                    pe.wait_ge(s["spread_ready"], c + 1)
                    nc.tensor.matmul(q[:, M_, :], k.ones[:, :], spread[:, :, :], start=True, stop=True)
                    for h in range(H):
                        nc.tensor.transpose(bank(K_)[:, h, :], qkv[:, 1, h, :], k.ident[:, :])
                    for h in range(H):
                        tr = nc.tensor.transpose(bank(V_)[:, h, :], qkv[:, 2, h, :], k.ident[:, :])
                    tr.then_inc(s["pe1"], 1)

                def outputs(c):
                    pe.wait_ge(s["kw_ready"], c + 1)
                    for h in range(H):
                        nc.tensor.matmul(pair(INTER[h // 2])[:, h % 2, :], qkv[:, 0, h, :], state[:, h, :],
                                         start=True, stop=True)
                    pe.wait_ge(s["v_ready"], c + 1)
                    pe.wait_ge(s["weights_ready"], c + 1)
                    for h in range(H):
                        mm = nc.tensor.matmul(pair(INTRA[h // 2])[:, h % 2, :], w_T[:, h, :], v_one[:, h, :],
                                              start=True, stop=True)
                    mm.then_inc(s["pe2"], 1)

                def new_state(c):
                    pe.wait_ge(s["inter_ready"], c + 1)
                    for h in range(H):
                        nc.tensor.matmul(pair(STATE[h // 2])[:, h % 2, :], k_w[:, h, :], v_one[:, h, :],
                                         start=True, stop=True)
                    pe.wait_ge(s["h_ready"], c + 1)
                    for h in range(H):
                        tr = nc.tensor.transpose(bank(TURNED)[:, h, :], h_tok[:, h, :], k.ident[:, :])
                    tr.then_inc(s["pe3"], 1)

                with pe.Fori(0, TB) as c:
                    for slot in range(SLOTS):
                        b, ch = divmod(slot, NCH)
                        project_chunk(k, pe, base + c * NB + b, b, ch, k.x_hi, k.x_lo)
                        if slot == 0:
                            turn_and_score(c)
                        if slot == 2:
                            outputs(c)
                        if slot == 4:
                            new_state(c)

            @block.scalar
            def _(act):
                act.preload_act_table_set(EXP_LN)
                with act.Fori(0, TB) as c:
                    act.wait_ge(s["pe2"], c)
                    nc.scalar.activation(qkv[:, :, :, :].rearrange("p a h t -> p (a h) t"),
                                         m_T[:, 0:3 * H, bass.ds(c * P, P)], ACT.Copy).then_inc(s["staged"], 1)
                    for slot in range(SLOTS):
                        b, ch = divmod(slot, NCH)
                        if ch == 0:
                            act.wait_ge(gate_sent[b], c * 16)
                        acc_wait(k, act, base + c * NB + b, ch)
                        nc.scalar.activation(gate_out[:, b, ch * CW:(ch + 1) * CW], k.acc[:, ch, 0:CW], ACT.Copy)\
                          .then_inc(k.acc_free, 1)
                        if ch == NCH - 1:
                            act.wait_ge(k.acc_free, (base + c * NB + b + 1) * NCH + NCH)
                            act.dma_start(k.gates[:, bass.ds(c * NB + b + FIRST_GATE, 1), :],
                                          gate_out[:, b:b + 1, :]).then_inc(gate_sent[b], 16)
                        if slot == 0:
                            act.wait_ge(s["pe1"], c + 1)
                            act.wait_ge(s["pe3"], c)
                            nc.scalar.activation(v_one[:, :, 0:P], bank(V_), ACT.Copy).then_inc(s["v_ready"], 1)
                            for h in range(H):
                                op = nc.scalar.activation(k_w[:, h:h + 1, :], bank(K_)[:, h:h + 1, :], ACT.Copy,
                                                          scale=k.exps[:, E_KEY, bass.ds(c, 1), h])
                            op.then_inc(s["kw_ready"], 1)
                            act.wait_ge(s["args_ready"], c + 1)
                            nc.scalar.activation(expo[:, :, :], expo[:, :, :], ACT.Exp, scale=-1.0)\
                              .then_inc(s["expo_ready"], 1)
                        if slot == 2:
                            act.wait_ge(s["pe2"], c + 1)
                            act.wait_ge(s["num_ready"], c)
                            for h in range(H):
                                op = nc.scalar.activation(inter[:, h, :], pair(INTER[h // 2])[:, h % 2, :], ACT.Copy,
                                                          scale=k.exps[:, E_STATE, bass.ds(c, 1), h])
                            op.then_inc(s["inter_ready"], 1)
                    act.wait_ge(s["y_ready"], c + 1)
                    act.dma_start(k.branch[0, :, :, bass.ds(c * P, P)], y_m[:, :, :]).then_inc(s["y_sent"], 16)
                act.wait_ge(s["y_sent"], TB * 16)
                for b in range(NB):
                    act.wait_ge(gate_sent[b], TB * 16)

            @block.vector
            def _(dve):
                nc.vector.memset(state[:, :, :], 0.0)
                nc.vector.memset(v_one[:, :, P:V1], 1.0)
                dve.drain().then_inc(s["state_ready"], 1)
                with dve.Fori(0, TB) as c:
                    dve.wait_ge(s["pe1"], c)
                    nc.vector.tensor_tensor(spread[:, :, :], k.ident[:, :].unsqueeze(1).to_broadcast([P, H, P]),
                                            k.mu[:, bass.ds(c, 1), :].squeeze(1).unsqueeze(2).to_broadcast([P, H, P]),
                                            ALU.mult).then_inc(s["spread_ready"], 1)
                    dve.wait_ge(s["pe1"], c + 1)
                    dve.wait_ge(s["expo_ready"], c)
                    for h in range(H):
                        op = nc.vector.scalar_tensor_tensor(out=expo[:, h, :], in0=bank(M_)[:, h, :],
                                                            scalar=k.g_col[:, bass.ds(c, 1), h], in1=k.late_big[:, :],
                                                            op0=ALU.subtract, op1=ALU.max)
                    op.then_inc(s["args_ready"], 1)
                    dve.wait_ge(s["expo_ready"], c + 1)
                    dve.wait_ge(s["pe2"], c)
                    nc.vector.tensor_tensor(w_T[:, :, :], expo[:, :, :], bank(S_), ALU.mult).then_inc(s["weights_ready"], 1)
                    dve.wait_ge(s["inter_ready"], c + 1)
                    for i in range(2):
                        op = nc.vector.tensor_tensor(num[:, 2 * i:2 * i + 2, :], inter[:, 2 * i:2 * i + 2, :],
                                                     pair(INTRA[i]), ALU.add)
                    dve.drain().then_inc(s["num_ready"], 1)
                    nc.vector.scalar_tensor_tensor(out=den[:, 0, :], in0=num[:, :, P], scalar=-1.0, in1=num[:, :, P],
                                                   op0=ALU.mult, op1=ALU.max)
                    dve.drain()
                    nc.vector.tensor_tensor(den[:, 1, :], den[:, 0, :], k.exps[:, E_NEGM, bass.ds(c, 1), :].squeeze(1), ALU.max)
                    dve.drain()
                    nc.vector.reciprocal(den[:, 2, :], den[:, 1, :])
                    dve.drain()
                    dve.wait_ge(s["pe3"], c)
                    nc.vector.tensor_tensor(h_tok[:, :, :], num[:, :, 0:P],
                                            den[:, 2, :].unsqueeze(2).to_broadcast([P, H, P]), ALU.mult)\
                      .then_inc(s["h_ready"], 1)
                    dve.wait_ge(s["pe3"], c + 1)
                    for h in range(H):
                        op = nc.vector.scalar_tensor_tensor(out=state[:, h, :], in0=state[:, h, :],
                                                            scalar=k.exps[:, E_DECAY, bass.ds(c, 1), h],
                                                            in1=pair(STATE[h // 2])[:, h % 2, :], op0=ALU.mult, op1=ALU.add)
                    op.then_inc(s["state_ready"], 1)
                    dve.wait_ge(s["y_sent"], c * 16)
                    nc.vector.tensor_tensor(y_m[:, :, :], bank(TURNED), m_T[:, 3 * H:4 * H, bass.ds(c * P, P)],
                                            ALU.mult).then_inc(s["y_ready"], 1)
    k.blocks = base + TB * NB


def mlstm_decode(k, m_T):
    nc, io = k.nc, k.io
    N = B * H
    dec = slice(T, TT)
    with ExitStack() as ctx:
        spread = k.sb(ctx, "dec_spread", [B, B, 2 * H])
        m_old = k.sb(ctx, "m_old", [P, N])
        gate = k.sb(ctx, "dec_gate", [P, B, 2 * H])
        f_abs = k.sb(ctx, "dec_f_abs", [P, B, H])
        f_pos = k.sb(ctx, "dec_f_pos", [P, B, H])
        m_new = k.sb(ctx, "m_new", [P, B, H])
        terms = k.sb(ctx, "dec_terms", [P, 3, B, H])
        kv = k.sb(ctx, "dec_kv", [B, 2, H, P])
        own = k.sb(ctx, "dec_own", [B, B, H])
        v_own = k.sb(ctx, "dec_v_own", [B, 2, B, P])
        old = k.sb(ctx, "C_old", [P, 2, B, P])
        new = k.sb(ctx, "C_new", [P, 2, B, P])
        n_new = k.sb(ctx, "n_new", [P, B, H])
        n_add = k.sb(ctx, "n_add", [P, B, H])
        n_rows = k.sb(ctx, "n_new_rows", [N, P])
        dot = k.sb(ctx, "dec_dot", [P, B, H])
        den = k.sb(ctx, "dec_den", [P, B, H])
        y_d = k.sb(ctx, "y_dec", [P, H, B])
        reps = k.ps(ctx, "dec_reps", [P, 512])
        turned = k.ps(ctx, "dec_turned", [B, 2, 512])
        outer = k.ps(ctx, "dec_outer", [P, B, P])
        s = {n: k.sem(ctx, "md_" + n) for n in (
            "m_in", "spread_ready", "gates_ready", "gate_ready", "log_ready", "terms_in", "terms_ready", "kv_turned",
            "kv_ready", "own_ready", "outer_ready", "new_ready", "dot_ready", "dots", "nums", "n_ready", "n_turned",
            "n_rows_ready", "y_ready", "sent")}
        old_in = [k.sem(ctx, f"C_old_in{i}") for i in range(2)]
        new_out = [k.sem(ctx, f"C_new_out{i}") for i in range(2)]
        qd = m_T[:, 0:H, dec]
        flat = "p b h -> p (b h)"
        with nc.Block() as block:
            @block.sync
            def _(sp):
                sp.dma_start(m_old[:, :], io["state_mlstm_m"].rearrange("l b h -> l (b h)").to_broadcast([P, N]),
                             allow_slow_non_contiguous=True).then_inc(s["m_in"], 16)
                for h in range(H):
                    if h >= 2:
                        sp.wait_ge(s["new_ready"], h - 1)
                    sp.dma_start(old[:, h % 2, :, :], io["state_mlstm_C"][0, :, h].rearrange("b d e -> d b e"))\
                      .then_inc(old_in[h % 2], 16)
                for h in range(H):
                    sp.wait_ge(s["new_ready"], h + 1)
                    sp.dma_start(io["C_sample"][0, :, h].rearrange("b d e -> d b e"), new[:, h % 2, :, :])\
                      .then_inc(new_out[h % 2], 16)
                sp.wait_ge(s["terms_in"], 1)
                sp.dma_start(io["m_sample"].rearrange("l b h -> l (b h)"), m_new[0:1, :, :].rearrange(flat)).then_inc(s["sent"], 16)
                sp.wait_ge(s["n_rows_ready"], 1)
                sp.dma_start(io["n_sample"].rearrange("l b h d -> (l b h) d"), n_rows[:, :]).then_inc(s["sent"], 16)
                sp.wait_ge(s["y_ready"], 1)
                sp.dma_start(k.branch[0, :, :, dec], y_d[:, :, :]).then_inc(s["sent"], 16)
                sp.wait_ge(s["sent"], 48)
                for i in range(2):
                    sp.wait_ge(new_out[i], 32)

            @block.tensor
            def _(pe):
                for a in range(2):
                    for h in range(H):
                        tr = nc.tensor.transpose(turned[:, a, h * P:(h + 1) * P], m_T[:, (a + 1) * H + h, dec], k.ident[:, :])
                tr.then_inc(s["kv_turned"], 1)
                pe.wait_ge(s["spread_ready"], 1)
                nc.tensor.matmul(reps[:, 0:B * 2 * H], k.ones[0:B, :], spread[:, :, :].rearrange("p b g -> p (b g)"),
                                 start=True, stop=True).then_inc(s["gates_ready"], 1)
                for h in range(H):
                    pe.wait_ge(s["own_ready"], h + 1)
                    if h:
                        pe.wait_ge(s["new_ready"], h)
                    for half in range(2):
                        mm = nc.tensor.matmul(outer[:, 4 * half:4 * half + 4, :], kv[:, 0, h, :],
                                              v_own[:, h % 2, 4 * half:4 * half + 4, :], start=True, stop=True)
                    mm.then_inc(s["outer_ready"], 1)
                    pe.wait_ge(s["new_ready"], h + 1)
                    for b in range(B):
                        mm = nc.tensor.matmul(reps[:, 128 + h * B + b:129 + h * B + b], new[:, h % 2, b, :],
                                              m_T[:, h, T + b:T + b + 1], start=True, stop=True)
                    mm.then_inc(s["nums"], 1)
                pe.wait_ge(s["dot_ready"], 1)
                nc.tensor.matmul(reps[:, 256:256 + N], k.ones[:, :], dot[:, :, :].rearrange(flat), start=True, stop=True)\
                    .then_inc(s["dots"], 1)
                pe.wait_ge(s["kv_ready"], 1)
                nc.tensor.transpose(outer[0:N, 0, :], n_new[:, :, :].rearrange(flat),
                                    k.ident[:, :]).then_inc(s["n_turned"], 1)

            @block.scalar
            def _(act):
                act.preload_act_table_set(EXP_LN)
                act.wait_ge(s["gate_ready"], 1)
                nc.scalar.activation(f_abs[:, :, :], gate[:, :, H:2 * H], ACT.Abs)
                act.drain()
                nc.scalar.activation(f_abs[:, :, :], f_abs[:, :, :], ACT.Exp, scale=-1.0)
                act.drain()
                nc.scalar.activation(f_abs[:, :, :], f_abs[:, :, :], ACT.Ln, bias=1.0).then_inc(s["log_ready"], 1)
                act.wait_ge(s["terms_in"], 1)
                nc.scalar.activation(terms[:, :, :, :], terms[:, :, :, :], ACT.Exp).then_inc(s["terms_ready"], 1)

            @block.vector
            def _(dve):
                nc.vector.tensor_tensor(spread[:, :, :], k.ident[0:B, 0:B].unsqueeze(2).to_broadcast([B, B, 2 * H]),
                                        k.gates_dec[:, :].unsqueeze(1).to_broadcast([B, B, 2 * H]),
                                        ALU.mult).then_inc(s["spread_ready"], 1)
                dve.wait_ge(s["kv_turned"], 1)
                nc.vector.tensor_copy(kv[:, :, :, :].rearrange("p a h d -> p a (h d)"), turned[:, :, :]).then_inc(s["kv_ready"], 1)
                dve.wait_ge(s["gates_ready"], 1)
                nc.vector.tensor_copy(gate[:, :, :].rearrange("p b g -> p (b g)"), reps[:, 0:B * 2 * H])\
                  .then_inc(s["gate_ready"], 1)
                dve.wait_ge(s["gate_ready"], 1)
                nc.vector.tensor_scalar(f_pos[:, :, :], gate[:, :, H:2 * H], -1.0, 0.0, ALU.mult, ALU.max)
                dve.drain()
                dve.wait_ge(s["log_ready"], 1)
                nc.vector.scalar_tensor_tensor(out=f_pos[:, :, :], in0=f_pos[:, :, :], scalar=-1.0, in1=f_abs[:, :, :],
                                               op0=ALU.mult, op1=ALU.subtract)
                dve.drain()
                dve.wait_ge(s["m_in"], 16)
                nc.vector.tensor_tensor(f_pos[:, :, :], f_pos[:, :, :], m_old[:, :].rearrange("p (b h) -> p b h", h=H), ALU.add)
                dve.drain()
                nc.vector.tensor_tensor(m_new[:, :, :], f_pos[:, :, :], gate[:, :, 0:H], ALU.max)
                dve.drain()
                nc.vector.tensor_tensor(terms[:, 0, :, :], f_pos[:, :, :], m_new[:, :, :], ALU.subtract)
                nc.vector.tensor_tensor(terms[:, 1, :, :], gate[:, :, 0:H], m_new[:, :, :], ALU.subtract)
                nc.vector.tensor_scalar(terms[:, 2, :, :], m_new[:, :, :], -1.0, None, ALU.mult)
                dve.drain().then_inc(s["terms_in"], 1)
                dve.wait_ge(s["terms_ready"], 1)
                nc.vector.tensor_tensor(own[:, :, :], k.ident[0:B, 0:B].unsqueeze(2).to_broadcast([B, B, H]),
                                        terms[0:B, 1, :, :], ALU.mult)
                nc.vector.tensor_tensor(n_new[:, :, :], k.n_old[:, :].rearrange("p (b h) -> p b h", h=H), terms[:, 0, :, :], ALU.mult)
                nc.vector.tensor_tensor(n_add[:, :, :], m_T[:, H:2 * H, dec].rearrange("p h b -> p b h"), terms[:, 1, :, :], ALU.mult)
                dve.drain()
                nc.vector.tensor_tensor(n_new[:, :, :], n_new[:, :, :], n_add[:, :, :], ALU.add)
                dve.drain()
                nc.vector.tensor_tensor(dot[:, :, :], n_new[:, :, :], qd.rearrange("p h b -> p b h"), ALU.mult).then_inc(s["dot_ready"], 1)
                for h in range(H):
                    nc.vector.tensor_tensor(v_own[:, h % 2, :, :], kv[:, 1, h, :].unsqueeze(1).to_broadcast([B, B, P]),
                                            own[:, :, h].unsqueeze(2).to_broadcast([B, B, P]), ALU.mult).then_inc(s["own_ready"], 1)
                    dve.wait_ge(old_in[h % 2], 16 * (h // 2 + 1))
                    nc.vector.tensor_tensor(old[:, h % 2, :, :], old[:, h % 2, :, :],
                                            terms[:, 0, :, h].unsqueeze(2).to_broadcast([P, B, P]), ALU.mult)
                    dve.drain()
                    dve.wait_ge(s["outer_ready"], h + 1)
                    if h >= 2:
                        dve.wait_ge(new_out[h % 2], 16)
                        dve.wait_ge(s["nums"], h - 1)
                    nc.vector.tensor_tensor(new[:, h % 2, :, :], old[:, h % 2, :, :], outer[:, :, :], ALU.add)\
                      .then_inc(s["new_ready"], 1)
                dve.wait_ge(s["dots"], 1)
                nc.vector.tensor_copy(den[:, :, :].rearrange(flat), reps[:, 256:256 + N])
                dve.drain()
                nc.vector.scalar_tensor_tensor(out=dot[:, :, :], in0=den[:, :, :], scalar=-1.0, in1=den[:, :, :],
                                               op0=ALU.mult, op1=ALU.max)
                dve.drain()
                nc.vector.tensor_tensor(den[:, :, :], dot[:, :, :], terms[:, 2, :, :], ALU.max)
                dve.drain()
                nc.vector.reciprocal(dot[:, :, :], den[:, :, :])
                dve.wait_ge(s["nums"], H)
                nc.vector.tensor_tensor(y_d[:, :, :], reps[:, 128:128 + N].rearrange("p (h b) -> p h b", h=H),
                                        m_T[:, 3 * H:4 * H, dec], ALU.mult)
                dve.drain()
                nc.vector.tensor_tensor(y_d[:, :, :], y_d[:, :, :], dot[:, :, :].rearrange("p b h -> p h b"), ALU.mult)\
                  .then_inc(s["y_ready"], 1)
                dve.wait_ge(s["n_turned"], 1)
                nc.vector.tensor_copy(n_rows[:, :], outer[0:N, 0, :]).then_inc(s["n_rows_ready"], 1)



def attention_decode(k, s_T):
    nc, io = k.nc, k.io
    N = B * PAGES * H
    RING = 4
    dec = slice(T, TT)
    with ExitStack() as ctx:
        table = k.sb(ctx, "pages", [1, B * PAGES], I32)
        page = k.sb(ctx, "page", [P, RING, W])
        q_tok = k.sb(ctx, "q_tok", [B, W])
        q_own = k.sb(ctx, "q_own", [B, 2, W])
        q_all = k.sb(ctx, "q_all", [P, B, W])
        prod = k.sb(ctx, "qk_prod", [P, 2, W])
        z = k.sb(ctx, "dec_z", [P, B, PAGES, H])
        z_abs = k.sb(ctx, "dec_z_abs", [P, B, PAGES, H])
        sp_ = k.sb(ctx, "dec_sp", [P, B, PAGES, H])
        later = k.sb(ctx, "dec_later", [P, B, PAGES, H])
        prob = k.sb(ctx, "dec_prob", [P, B, PAGES, H])
        y_d = k.sb(ctx, "y_dec_s", [P, H, B])
        turned = k.ps(ctx, "q_turned", [B, W])
        q_rows = k.ps(ctx, "q_rows", [P, 2, W])
        sums = k.ps(ctx, "dec_sums", [P, N])
        y = k.ps(ctx, "dec_y", [P, B, H])
        s = {n: k.sem(ctx, "ad_" + n) for n in (
            "table_in", "q_turned", "q_ready", "own_ready", "rows_ready", "q_all_ready", "multiplied", "reduced", "z_ready",
            "log_ready", "sp_ready", "summed", "arg_ready", "prob_ready", "page_used", "y_ready", "y_out", "sent")}
        landed = [k.sem(ctx, f"page_landed{i}") for i in range(RING)]
        flat = "p b g h -> p (b g h)"
        with nc.Block() as block:
            @block.sync
            def _(sp):
                sp.dma_start(table[:, :], io["page_table"].rearrange("b g -> (b g)").unsqueeze(0)).then_inc(s["table_in"], 16)
                sp.wait_ge(s["table_in"], 16)
                for cache, used, first in ((io["cache_k"], s["multiplied"], 0), (io["cache_v"], s["page_used"], 1)):
                    if first:
                        sp.wait_ge(s["multiplied"], B * PAGES + RING)
                    with sp.Fori(0, B) as b:
                        for g in range(PAGES):
                            number = sp.value_load(table[0:1, bass.ds(b * PAGES + g, 1)], min_val=0, max_val=N_PHYS - 1)
                            sp.wait_ge(used, b * PAGES + g + 1)
                            sp.dma_start(page[:, g % RING, :],
                                         cache[0, bass.ds(number, 1), :, :, :].rearrange("a t h d -> (a t) (h d)"))\
                              .then_inc(landed[g % RING], 16)
                sp.wait_ge(s["y_out"], 1)
                sp.dma_start(k.branch[2, :, :, dec], y_d[:, :, :]).then_inc(s["sent"], 16)
                sp.wait_ge(s["sent"], 16)

            @block.tensor
            def _(pe):
                pe.sem_inc(s["page_used"], RING)
                for h in range(H):
                    tr = nc.tensor.transpose(turned[:, h * P:(h + 1) * P], s_T[:, h, dec], k.ident[:, :])
                tr.then_inc(s["q_turned"], 1)
                for b in range(B):
                    pe.wait_ge(s["own_ready"], b + 1)
                    if b >= 2:
                        pe.wait_ge(s["q_all_ready"], b - 1)
                    nc.tensor.matmul(q_rows[:, b % 2, :], k.ones[0:B, :], q_own[:, b % 2, :], start=True, stop=True)\
                        .then_inc(s["rows_ready"], 1)
                pe.wait_ge(s["sp_ready"], 1)
                nc.tensor.matmul(sums[:, :], k.neg_from[:, :], sp_[:, :, :, :].rearrange(flat), start=True, stop=False)
                nc.tensor.matmul(sums[:, :], k.neg_ones[:, :], later[:, :, :, :].rearrange(flat), start=False, stop=True)\
                    .then_inc(s["summed"], 1)
                nc.tensor.matmul(y[:, :, :].rearrange("p b h -> p (b h)"), k.ident[:, :], k.zeros[:, :], start=True, stop=True)
                pe.wait_ge(s["prob_ready"], 1)
                with pe.Fori(0, B) as b:
                    for g in range(PAGES):
                        pe.wait_ge(landed[g % RING], (b + B) * (PAGES // RING * 16) + (g // RING + 1) * 16)
                        for h in range(H):
                            mm = nc.tensor.matmul(y[:, bass.ds(b, 1), h], page[:, g % RING, h * P:(h + 1) * P],
                                                  prob[:, bass.ds(b, 1), g, h], start=False, stop=True, skip_group_check=True)
                        mm.then_inc(s["page_used"], 1)
                pe.drain().then_inc(s["y_ready"], 1)

            @block.vector
            def _(dve):
                dve.sem_inc(s["multiplied"], RING)
                dve.wait_ge(s["q_turned"], 1)
                nc.vector.tensor_copy(q_tok[:, :], turned[:, :])
                dve.drain()
                for b in range(B):
                    if b >= 2:
                        dve.wait_ge(s["rows_ready"], b - 1)
                    nc.vector.tensor_scalar(q_own[:, b % 2, :], q_tok[:, :], k.ident[0:B, b:b + 1], None, ALU.mult)\
                      .then_inc(s["own_ready"], 1)
                    dve.wait_ge(s["rows_ready"], b + 1)
                    nc.vector.tensor_copy(q_all[:, b, :], q_rows[:, b % 2, :]).then_inc(s["q_all_ready"], 1)
                dve.wait_ge(s["q_all_ready"], B)
                with dve.Fori(0, B) as b:
                    for g in range(PAGES):
                        dve.wait_ge(landed[g % RING], b * (PAGES // RING * 16) + (g // RING + 1) * 16)
                        dve.wait_ge(s["reduced"], b * PAGES + max(g - 1, 0))
                        nc.vector.tensor_tensor(prod[:, g % 2, :].unsqueeze(1), page[:, g % RING, :].unsqueeze(1),
                                                q_all[:, bass.ds(b, 1), :], ALU.mult).then_inc(s["multiplied"], 1)
                        dve.wait_ge(s["multiplied"], b * PAGES + g + 1 + RING)
                        nc.vector.tensor_reduce(z[:, bass.ds(b, 1), g, :].squeeze(1),
                                                prod[:, g % 2, :].rearrange("p (h d) -> p h d", h=H), AX.X, ALU.add)\
                          .then_inc(s["reduced"], 1)
                dve.wait_ge(s["reduced"], B * PAGES)
                bias = k.b_sb[:, :].unsqueeze(1).to_broadcast([P, B * PAGES, H])
                zf = z[:, :, :, :].rearrange("p b g h -> p (b g) h")
                nc.vector.tensor_tensor(zf, zf, bias, ALU.add).then_inc(s["z_ready"], 1)
                dve.wait_ge(s["log_ready"], 1)
                dve.wait_ge(s["z_ready"], 1)
                fz, fs, fa = (t[:, :, :, :].rearrange(flat) for t in (z, sp_, z_abs))
                nc.vector.scalar_tensor_tensor(out=fs, in0=fz, scalar=0.0, in1=fa, op0=ALU.max, op1=ALU.add)
                nc.vector.memset(later[:, :, PAGES - 1, :], 0.0)
                for g in range(PAGES - 2, -1, -1):
                    dve.drain()
                    nc.vector.tensor_tensor(later[:, :, g, :], later[:, :, g + 1, :], sp_[:, :, g + 1, :], ALU.add)
                dve.drain().then_inc(s["sp_ready"], 1)
                dve.wait_ge(s["summed"], 1)
                nc.vector.tensor_tensor(fa, fz, sums[:, :], ALU.add).then_inc(s["arg_ready"], 1)
                dve.wait_ge(s["y_ready"], 1)
                nc.vector.tensor_copy(y_d[:, :, :], y[:, :, :].rearrange("p b h -> p h b")).then_inc(s["y_out"], 1)

            @block.scalar
            def _(act):
                act.preload_act_table_set(EXP_LN)
                fz, fa, fp = (t[:, :, :, :].rearrange(flat) for t in (z, z_abs, prob))
                act.wait_ge(s["z_ready"], 1)
                nc.scalar.activation(fa, fz, ACT.Abs)
                act.drain()
                nc.scalar.activation(fa, fa, ACT.Exp, scale=-1.0)
                act.drain()
                nc.scalar.activation(fa, fa, ACT.Ln, bias=1.0).then_inc(s["log_ready"], 1)
                act.wait_ge(s["arg_ready"], 1)
                nc.scalar.activation(fp, fa, ACT.Exp).then_inc(s["prob_ready"], 1)


def merge_branches(k, merged):
    nc, io = k.nc, k.io
    base = k.blocks
    NBR = 3
    with ExitStack() as ctx:
        y_raw = k.sb(ctx, "y_raw", [P, H, TT])
        y_hi = k.sb(ctx, "y_hi", [P, H, TT], F32R)
        y_lo = k.sb(ctx, "y_lo", [P, H, TT], F32R)
        gate = k.sb(ctx, "merge_gate", [P, 2, TT])
        part = k.sb(ctx, "merge_part", [P, TT])
        s = {n: k.sem(ctx, "mb_" + n) for n in ("y_in", "y_rounded", "y_split", "sigmoid", "part_ready", "merged", "hi_ready")}
        gate_in = [k.sem(ctx, f"gate_in{i}") for i in range(2)]
        with nc.Block() as block:
            @block.sync
            def _(sp):
                for r in range(NBR):
                    w = io["w_branch"][0, r].rearrange("(k p) n -> p k n", p=P)
                    if r:
                        sp.wait_ge(s["y_split"], r)
                    sp.dma_start(y_raw[:, :, :], k.branch[r]).then_inc(s["y_in"], 16)
                    with sp.Fori(0, KD // 2) as i:
                        for par in range(2):
                            m = i * 2 + par
                            load_weights(k, sp, base + r * KD + m, par, w[:, :, bass.ds(m * P, P)], H)
                            sp.wait_ge(s["merged"], r * KD + m + 1)
                            sp.dma_start(gate[:, par:par + 1, :], k.gates[:, bass.ds(m + r * KD, 1), :]).then_inc(gate_in[par], 16)

            @block.gpsimd
            def _(pool):
                for r in range(NBR):
                    with pool.Fori(0, KD // 2) as i:
                        for par in range(2):
                            n = base + r * KD + i * 2 + par
                            split_weights(k, pool, n, par, (base + r * KD) // 2 + i, H)

            @block.tensor
            def _(pe):
                for r in range(NBR):
                    pe.wait_ge(s["y_split"], r + 1)
                    with pe.Fori(0, KD // 2) as i:
                        for par in range(2):
                            for c in range(NCH):
                                project_chunk(k, pe, base + r * KD + i * 2 + par, par, c, y_hi[:, :, :], y_lo[:, :, :], H)

            @block.scalar
            def _(act):
                act.preload_act_table_set("sigmoid_and_others")
                for r in range(NBR):
                    act.wait_ge(s["y_in"], 16 * (r + 1))
                    if r:
                        act.wait_ge(k.acc_ready, (base + r * KD) * NCH + 2 * NCH)
                    nc.scalar.activation(y_hi[:, :, :], y_raw[:, :, :], ACT.Copy).then_inc(s["y_rounded"], 1)
                    with act.Fori(0, KD // 2) as i:
                        for par in range(2):
                            m = i * 2 + par
                            act.wait_ge(gate_in[par], (i + r * (KD // 2) + 1) * 16)
                            nc.scalar.activation(gate[:, par, :], gate[:, par, :], ACT.Sigmoid).then_inc(s["sigmoid"], 1)
                            if r == NBR - 1:
                                act.wait_ge(s["merged"], r * KD + m + 1 + 2)
                                nc.scalar.activation(k.x_hi[:, bass.ds(m, 1), :], merged[:, bass.ds(m, 1), :], ACT.Copy)\
                                  .then_inc(s["hi_ready"], 1)

            @block.vector
            def _(dve):
                dve.sem_inc(s["merged"], 2)
                for r in range(NBR):
                    dve.wait_ge(s["y_rounded"], r + 1)
                    nc.vector.tensor_tensor(y_lo[:, :, :], y_raw[:, :, :], y_hi[:, :, :].bitcast(F32), ALU.subtract)\
                      .then_inc(s["y_split"], 1)
                    with dve.Fori(0, KD // 2) as i:
                        for par in range(2):
                            m = i * 2 + par
                            n = base + r * KD + m
                            dve.wait_ge(s["sigmoid"], r * KD + m + 1)
                            if r:
                                dve.wait_ge(s["merged"], r * KD + m + 2)
                            for c in range(NCH):
                                acc_wait(k, dve, n, c)
                                cols = slice(c * CW, (c + 1) * CW)
                                out = merged[:, bass.ds(m, 1), cols] if r == 0 else part[:, cols].unsqueeze(1)
                                nc.vector.tensor_tensor(out, k.acc[:, c:c + 1, 0:CW], gate[:, par:par + 1, cols],
                                                        ALU.mult).then_inc(k.acc_free, 1)
                            if r == 0:
                                dve.drain().then_inc(s["merged"], 1)
                            else:
                                dve.wait_ge(k.acc_free, (n + 1) * NCH + NCH)
                                nc.vector.tensor_tensor(merged[:, bass.ds(m, 1), :], merged[:, bass.ds(m, 1), :],
                                                        part[:, :].unsqueeze(1), ALU.add).then_inc(s["merged"], 1)
                            if r == NBR - 1:
                                dve.wait_ge(s["hi_ready"], m + 1)
                                nc.vector.tensor_tensor(k.x_lo[:, bass.ds(m, 1), :], merged[:, bass.ds(m, 1), :],
                                                        k.x_hi[:, bass.ds(m, 1), :].bitcast(F32), ALU.subtract)
    k.blocks = base + NBR * KD


def mix_out(k, h):
    nc, io = k.nc, k.io
    base = k.blocks
    w = io["w_out"][0].rearrange("(k p) n -> p k n", p=P)
    with ExitStack() as ctx:
        h_in = k.sem(ctx, "h_in")
        with nc.Block() as block:
            @block.sync
            def _(sp):
                sp.dma_start(h[:, :, :], k.x_T).then_inc(h_in, 16)
                with sp.Fori(0, KD // 2) as i:
                    for par in range(2):
                        load_weights(k, sp, base + i * 2 + par, par, w[:, :, bass.ds((i * 2 + par) * P, P)])

            @block.gpsimd
            def _(pool):
                with pool.Fori(0, KD // 2) as i:
                    for par in range(2):
                        split_weights(k, pool, base + i * 2 + par, par, base // 2 + i)

            @block.tensor
            def _(pe):
                with pe.Fori(0, KD // 2) as i:
                    for par in range(2):
                        for c in range(NCH):
                            project_chunk(k, pe, base + i * 2 + par, par, c, k.x_hi, k.x_lo)

            @block.vector
            def _(dve):
                dve.wait_ge(h_in, 16)
                with dve.Fori(0, KD // 2) as i:
                    for par in range(2):
                        for c in range(NCH):
                            add_chunk(k, dve, base + i * 2 + par, c, h[:, bass.ds(i * 2 + par, 1), :])
    k.blocks = base + KD


def add_chunk(k, dve, n, c, out):
    cols = slice(c * CW, (c + 1) * CW)
    acc_wait(k, dve, n, c)
    k.nc.vector.tensor_tensor(out[:, :, cols], k.acc[:, c:c + 1, 0:CW], out[:, :, cols], ALU.add).then_inc(k.acc_free, 1)


def normalise(k, h, gain, name):
    nc = k.nc
    with ExitStack() as ctx:
        square = k.sb(ctx, name + "_sq", [P, 2, TT])
        root = k.sb(ctx, name + "_root", [P, NCH, CW])
        rstd = k.sb(ctx, name + "_rstd", [P, NCH, CW])
        x = k.sb(ctx, name + "_x", [P, 2, TT])
        sums = k.ps(ctx, name + "_sums", [P, NCH, 512])
        s = {n: k.sem(ctx, f"{name}_{n}") for n in ("squared", "added", "root_ready", "rstd_ready", "x_ready", "rounded", "split")}
        with nc.Block() as block:
            @block.scalar
            def _(act):
                act.preload_act_table_set("sqrt_and_others")
                for m in range(KD):
                    if m >= 2:
                        act.wait_ge(s["added"], m - 1)
                    nc.scalar.activation(square[:, m % 2, :], h[:, m, :], ACT.Square).then_inc(s["squared"], 1)
                act.wait_ge(s["added"], KD)
                for c in range(NCH):
                    nc.scalar.activation(root[:, c, :], sums[:, c, 0:CW], ACT.Sqrt, scale=1.0 / D,
                                         bias=k.eps[:, :]).then_inc(s["root_ready"], 1)
                for m in range(KD):
                    act.wait_ge(s["x_ready"], m + 1)
                    nc.scalar.activation(k.x_hi[:, m, :], x[:, m % 2, :], ACT.Copy).then_inc(s["rounded"], 1)

            @block.tensor
            def _(pe):
                for m in range(KD):
                    pe.wait_ge(s["squared"], m + 1)
                    for c in range(NCH):
                        mm = nc.tensor.matmul(sums[:, c, 0:CW], k.ones[:, :], square[:, m % 2, c * CW:(c + 1) * CW],
                                              start=(m == 0), stop=(m == KD - 1))
                    mm.then_inc(s["added"], 1)

            @block.vector
            def _(dve):
                for c in range(NCH):
                    dve.wait_ge(s["root_ready"], c + 1)
                    nc.vector.reciprocal(rstd[:, c, :], root[:, c, :]).then_inc(s["rstd_ready"], 1)
                dve.wait_ge(s["rstd_ready"], NCH)
                for m in range(KD):
                    if m >= 2:
                        dve.wait_ge(s["split"], m - 1)
                    nc.vector.scalar_tensor_tensor(out=x[:, m % 2, :], in0=h[:, m, :], scalar=gain[:, m:m + 1],
                                                   in1=rstd[:, :, :].rearrange("p c n -> p (c n)"),
                                                   op0=ALU.mult, op1=ALU.mult).then_inc(s["x_ready"], 1)

            @block.gpsimd
            def _(pool):
                for m in range(KD):
                    pool.wait_ge(s["rounded"], m + 1)
                    nc.gpsimd.tensor_tensor(k.x_lo[:, m, :], x[:, m % 2, :], k.x_hi[:, m, :].bitcast(F32),
                                            ALU.subtract).then_inc(s["split"], 1)


def feed_forward(k, h):
    nc, io = k.nc, k.io
    base = k.blocks
    G = FFN // D
    w_up = io["w_up"][0].rearrange("(k p) n -> p k n", p=P)
    w_down = io["w_down"][0].rearrange("(g k p) n -> p g k n", p=P, k=KD)
    with ExitStack() as ctx:
        u_hi = k.sb(ctx, "u_hi", [P, KD, TT], F32R)
        u_lo = k.sb(ctx, "u_lo", [P, KD, TT], F32R)
        relu = k.sb(ctx, "relu", [P, 3, CW])
        square = k.sb(ctx, "relu_sq", [P, 3, CW])
        s = {n: k.sem(ctx, "ff_" + n) for n in ("relu_ready", "squared", "rounded", "split")}
        PG = KD * NCH
        with nc.Block() as block:
            @block.sync
            def _(sp):
                with sp.Fori(0, G) as g:
                    with sp.Fori(0, KD // 2) as i:
                        for par in range(2):
                            load_weights(k, sp, base + g * (2 * KD) + i * 2 + par, par,
                                         w_up[:, :, bass.ds(g * D + (i * 2 + par) * P, P)])
                    with sp.Fori(0, KD // 2) as i:
                        for par in range(2):
                            load_weights(k, sp, base + g * (2 * KD) + KD + i * 2 + par, par,
                                         w_down[:, bass.ds(g, 1), :, bass.ds((i * 2 + par) * P, P)].squeeze(1))

            @block.gpsimd
            def _(pool):
                with pool.Fori(0, G * KD) as i:
                    for par in range(2):
                        split_weights(k, pool, base + i * 2 + par, par, base // 2 + i)

            @block.tensor
            def _(pe):
                with pe.Fori(0, G) as g:
                    n0 = base + g * (2 * KD)
                    with pe.Fori(0, KD // 2) as i:
                        for par in range(2):
                            for c in range(NCH):
                                project_chunk(k, pe, n0 + i * 2 + par, par, c, k.x_hi, k.x_lo)
                    for par in range(2):
                        for c in range(NCH):
                            if par == 0:
                                pe.wait_ge(s["split"], g * PG + (KD - 1) * NCH + c + 1)
                            project_chunk(k, pe, n0 + KD + par, par, c, u_hi, u_lo)
                    with pe.Fori(1, KD // 2) as i:
                        for par in range(2):
                            for c in range(NCH):
                                project_chunk(k, pe, n0 + KD + i * 2 + par, par, c, u_hi, u_lo)

            @block.vector
            def _(dve):
                with dve.Fori(0, G) as g:
                    n0 = base + g * (2 * KD)
                    with dve.Fori(0, KD // 2) as i:
                        def finish(e):
                            par, c = divmod(e, NCH)
                            t = g * PG + i * (2 * NCH) + e
                            dve.wait_ge(s["rounded"], t + 1)
                            nc.vector.tensor_tensor(u_lo[:, bass.ds(i * 2 + par, 1), c * CW:(c + 1) * CW],
                                                    square[:, c:c + 1, :],
                                                    u_hi[:, bass.ds(i * 2 + par, 1), c * CW:(c + 1) * CW].bitcast(F32),
                                                    ALU.subtract).then_inc(s["split"], 1)
                        for e in range(2 * NCH):
                            par, c = divmod(e, NCH)
                            acc_wait(k, dve, n0 + i * 2 + par, c)
                            if e >= NCH:
                                dve.wait_ge(s["rounded"], g * PG + i * (2 * NCH) + e - NCH + 1)
                            nc.vector.tensor_scalar(relu[:, c, :], k.acc[:, c, 0:CW], 0.0, None, ALU.max)\
                              .then_inc(k.acc_free, 1)
                            dve.drain().then_inc(s["relu_ready"], 1)
                            if e:
                                finish(e - 1)
                        finish(2 * NCH - 1)
                    with dve.Fori(0, KD // 2) as i:
                        for par in range(2):
                            for c in range(NCH):
                                add_chunk(k, dve, n0 + KD + i * 2 + par, c, h[:, bass.ds(i * 2 + par, 1), :])

            @block.scalar
            def _(act):
                with act.Fori(0, G) as g:
                    with act.Fori(0, KD // 2) as i:
                        for e in range(2 * NCH):
                            par, c = divmod(e, NCH)
                            t = g * PG + i * (2 * NCH) + e
                            act.wait_ge(s["relu_ready"], t + 1)
                            act.wait_ge(s["split"], t - NCH + 1 if e >= NCH else g * PG + i * (2 * NCH))
                            nc.scalar.activation(square[:, c, :], relu[:, c, :], ACT.Square).then_inc(s["squared"], 1)
                            nc.scalar.activation(u_hi[:, bass.ds(i * 2 + par, 1), c * CW:(c + 1) * CW], relu[:, c:c + 1, :],
                                                 ACT.Square).then_inc(s["rounded"], 1)
    k.blocks = base + G * 2 * KD


def turn_ple(k):
    nc, io = k.nc, k.io
    KP = PLE // P
    with ExitStack() as ctx:
        rows = k.sb(ctx, "p_rows", [P, TB + 1, PLE])
        pt = k.ps(ctx, "p_turned", [P, 2, 4, P])
        raw = k.sb(ctx, "p_raw", [P, 2, KP, P])
        s = {n: k.sem(ctx, "tp_" + n) for n in ("rows_in", "turned", "read", "rounded", "split")}
        with nc.Block() as block:
            @block.sync
            def _(sp):
                sp.dma_start(rows[:, 0:TB, :], io["p_prompt"][0, 0].rearrange("(b p) c -> p b c", p=P)).then_inc(s["rows_in"], 16)
                sp.dma_start(rows[0:B, TB, :], io["p_sample"][0, :, 0, :]).then_inc(s["rows_in"], 16)
                sp.wait_ge(s["rows_in"], 32)

            @block.tensor
            def _(pe):
                pe.wait_ge(s["rows_in"], 32)
                for t in range(TB + 1):
                    m = P if t < TB else B
                    if t >= 2:
                        pe.wait_ge(s["read"], t - 1)
                    for i in range(KP):
                        tr = nc.tensor.transpose(pt[:, t % 2, i, 0:m], rows[0:m, t, i * P:(i + 1) * P], k.ident[0:m, 0:m])
                    tr.then_inc(s["turned"], 1)

            @block.vector
            def _(dve):
                for t in range(TB + 1):
                    m = P if t < TB else B
                    dve.wait_ge(s["turned"], t + 1)
                    nc.vector.tensor_copy(raw[:, t % 2, :, 0:m], pt[:, t % 2, 0:KP, 0:m]).then_inc(s["read"], 1)
                    dve.wait_ge(s["read"], t + 1)
                    nc.vector.tensor_copy(k.p_hi[:, :, t * P:t * P + m], raw[:, t % 2, :, 0:m]).then_inc(s["rounded"], 1)
                    dve.wait_ge(s["rounded"], t + 1)
                    nc.vector.tensor_tensor(k.p_lo[:, :, t * P:t * P + m], raw[:, t % 2, :, 0:m],
                                            k.p_hi[:, :, t * P:t * P + m].bitcast(F32), ALU.subtract)


def per_layer_embedding(k, h):
    nc, io = k.nc, k.io
    base = k.blocks
    KP = PLE // P
    w_gate = io["w_ple_gate"][0].rearrange("(k p) n -> p k n", p=P)
    w_ple = io["w_ple"][0].rearrange("(k p) n -> p k n", p=P)
    with ExitStack() as ctx:
        gate = k.sb(ctx, "ple_gate", [P, TT])
        emb = k.sb(ctx, "ple_emb", [P, TT])
        s = {n: k.sem(ctx, "pl_" + n) for n in ("gate_ready", "added", "product")}
        with nc.Block() as block:
            @block.sync
            def _(sp):
                with sp.Fori(0, KD) as m:
                    load_weights(k, sp, base + m * 2, 0, w_gate[:, :, bass.ds(m * P, P)])
                    load_weights(k, sp, base + m * 2 + 1, 1, w_ple[:, :, bass.ds(m * P, P)], KP)

            @block.gpsimd
            def _(pool):
                with pool.Fori(0, KD) as m:
                    split_weights(k, pool, base + m * 2, 0, base // 2 + m)
                    split_weights(k, pool, base + m * 2 + 1, 1, base // 2 + m, KP)

            @block.tensor
            def _(pe):
                with pe.Fori(0, KD) as m:
                    for c in range(NCH):
                        project_chunk(k, pe, base + m * 2, 0, c, k.x_hi, k.x_lo)
                    for c in range(NCH):
                        project_chunk(k, pe, base + m * 2 + 1, 1, c, k.p_hi, k.p_lo, KP)

            @block.scalar
            def _(act):
                act.preload_act_table_set("sigmoid_and_others")
                with act.Fori(0, KD) as m:
                    for half, (out, func) in enumerate(((gate, ACT.Sigmoid), (emb, ACT.Copy))):
                        for c in range(NCH):
                            acc_wait(k, act, base + m * 2 + half, c)
                            if half == 0 and c == 0:
                                act.wait_ge(s["product"], m)
                            nc.scalar.activation(out[:, c * CW:(c + 1) * CW], k.acc[:, c, 0:CW], func).then_inc(k.acc_free, 1)

            @block.vector
            def _(dve):
                with dve.Fori(0, KD) as m:
                    dve.wait_ge(k.acc_free, (base + m * 2 + 2) * NCH + NCH)
                    dve.wait_ge(s["added"], m)
                    nc.vector.tensor_tensor(k.ple_prod[:, :], gate[:, :], emb[:, :], ALU.mult).then_inc(s["product"], 1)
                    dve.wait_ge(s["product"], m + 1)
                    nc.vector.tensor_tensor(h[:, bass.ds(m, 1), :], h[:, bass.ds(m, 1), :], k.ple_prod[:, :].unsqueeze(1),
                                            ALU.add).then_inc(s["added"], 1)
    k.blocks = base + KD * 2


def final_norm(k, h):
    nc, io = k.nc, k.io
    tiles = [(t * P, P) for t in range(TB)] + [(T, B)]
    with ExitStack() as ctx:
        gain = k.sb(ctx, "g_final_rows", [P, D])
        junk = k.sb(ctx, "fn_junk", [P, 2, D])
        sums = k.sb(ctx, "fn_sums", [P, len(tiles)])
        rstd = k.sb(ctx, "fn_rstd", [P, 2 * len(tiles)])
        scaled = k.sb(ctx, "fn_scaled", [P, 2, D])
        y = k.sb(ctx, "fn_y", [P, 2, D])
        pt = k.ps(ctx, "fn_pt", [P, 2, D])
        s = {n: k.sem(ctx, "fn_" + n) for n in ("gain_in", "turned", "root_ready", "rstd_ready", "scaled", "y_ready", "squared")}
        sent = [k.sem(ctx, f"y_sent{i}") for i in range(2)]
        y_p = io["y_prompt"].rearrange("b t d -> (b t) d")
        y_s = io["y_sample"].rearrange("b t d -> (b t) d")
        with nc.Block() as block:
            @block.sync
            def _(sp):
                sp.dma_start(gain[:, :], io["g_final"].unsqueeze(0).to_broadcast([P, D])).then_inc(s["gain_in"], 16)
                for i, (t0, m) in enumerate(tiles):
                    sp.wait_ge(s["y_ready"], i + 1)
                    sp.dma_start(y_p[t0:t0 + m, :] if t0 < T else y_s, y[0:m, i % 2, :]).then_inc(sent[i % 2], 16)
                for i in range(2):
                    sp.wait_ge(sent[i], 16 * len(tiles[i::2]))

            @block.tensor
            def _(pe):
                for i, (t0, m) in enumerate(tiles):
                    if i >= 2:
                        pe.wait_ge(s["scaled"], i - 1)
                    for b in range(KD):
                        tr = nc.tensor.transpose(pt[0:m, i % 2, b * P:(b + 1) * P], h[:, b, t0:t0 + m], k.ident[:, :])
                    tr.then_inc(s["turned"], 1)

            @block.scalar
            def _(act):
                act.preload_act_table_set("sqrt_and_others")
                for i, (t0, m) in enumerate(tiles):
                    act.wait_ge(s["turned"], i + 1)
                    nc.scalar.activation(junk[0:m, i % 2, :], pt[0:m, i % 2, :], ACT.Square, accum_out=sums[0:m, i:i + 1])\
                      .then_inc(s["squared"], 1)
                    act.wait_ge(s["squared"], i + 1)
                    nc.scalar.activation(rstd[0:m, 2 * i:2 * i + 1], sums[0:m, i:i + 1], ACT.Sqrt, scale=1.0 / D,
                                         bias=k.eps[0:m, :]).then_inc(s["root_ready"], 1)
                    act.wait_ge(s["rstd_ready"], i + 1)
                    if i >= 2:
                        act.wait_ge(s["y_ready"], i - 1)
                    nc.scalar.activation(scaled[0:m, i % 2, :], pt[0:m, i % 2, :], ACT.Copy,
                                         scale=rstd[0:m, 2 * i + 1:2 * i + 2]).then_inc(s["scaled"], 1)

            @block.vector
            def _(dve):
                dve.wait_ge(s["gain_in"], 16)
                for i, (t0, m) in enumerate(tiles):
                    dve.wait_ge(s["root_ready"], i + 1)
                    nc.vector.reciprocal(rstd[0:m, 2 * i + 1:2 * i + 2], rstd[0:m, 2 * i:2 * i + 1]).then_inc(s["rstd_ready"], 1)
                    dve.wait_ge(s["scaled"], i + 1)
                    if i >= 2:
                        dve.wait_ge(sent[i % 2], 16 * (i // 2))
                    nc.vector.tensor_tensor(y[0:m, i % 2, :], scaled[0:m, i % 2, :], gain[0:m, :], ALU.mult)\
                      .then_inc(s["y_ready"], 1)

def allocate(k, ctx):
    k.x_hi = k.sb(ctx, "x_hi", [P, KD, TT], F32R)
    k.x_lo = k.sb(ctx, "x_lo", [P, KD, TT], F32R)
    k.w_raw = k.sb(ctx, "w_raw", [P, 2, KD, P])
    k.w_hi = k.sb(ctx, "w_hi", [P, 2, KD, P], F32R)
    k.w_lo = k.sb(ctx, "w_lo", [P, 2, KD, P], F32R)
    k.ident, k.ones, k.neg_ones, k.sum_to, k.neg_from, k.late_big, k.late_neg = (
        k.sb(ctx, name, [P, P])
        for name in ("ident", "ones", "neg_ones", "sum_to", "neg_from", "late_big", "late_neg"))
    k.eps = k.sb(ctx, "eps", [P, 1])
    k.g_mix, k.g_mlp, k.g_ple = (k.sb(ctx, name, [P, KD]) for name in ("g_mix_c", "g_mlp_c", "g_ple_c"))
    k.b_if = k.sb(ctx, "b_if_c", [P, 2 * H])
    k.b_sb = k.sb(ctx, "b_sb_c", [P, H])
    k.conv_w = k.sb(ctx, "conv_w_c", [P, 3, H])
    k.acc = k.ps(ctx, "acc", [P, NCH, 512])
    k.w_landed = [k.sem(ctx, f"w_landed{i}") for i in range(2)]
    k.w_rounded, k.w_split, k.acc_ready, k.acc_free, k.pool_tick, k.params_in = (
        k.sem(ctx, name) for name in ("w_rounded", "w_split", "acc_ready", "acc_free", "pool_tick", "params_in"))
    k.before = k.sb(ctx, "before", [P, P])
    k.conv_state = k.sb(ctx, "conv_state", [P, H, 2 * B])
    k.n_old = k.sb(ctx, "n_old", [P, B * H])
    k.g_col = k.sb(ctx, "g_col", [P, TB, H])
    k.mu = k.sb(ctx, "mu", [P, TB, H])
    k.exps = k.sb(ctx, "exps", [P, N_E, TB, H])
    k.gates_dec = k.sb(ctx, "gates_dec", [B, 2 * H])
    k.zeros = k.sb(ctx, "zeros", [P, B * H])


def hybrid_layer(nc, io):
    k = Chip(nc, io)
    k.x_T = nc.dram_tensor("x_feature_major", [P, KD, TT], F32, kind="Internal").ap()
    k.gates = nc.dram_tensor("merge_gates", [P, 3 * KD, TT], F32, kind="Internal").ap()
    k.branch = nc.dram_tensor("branch_outputs", [3, P, H, TT], F32, kind="Internal").ap()
    w_in = io["w_in"].rearrange("l (k p) n -> p (l k) n", p=P)

    def group(col, out, scale=1.0, func=ACT.Copy):
        return dict(w=w_in, col=col, blocks=H, kb=KD, hi=k.x_hi, lo=k.x_lo, out=out, scale=scale, func=func)

    with ExitStack() as ctx:
        allocate(k, ctx)
        k.phase_sems = []
        constants(k)
        turn_states(k)
        normalise_input(k)
        with ExitStack() as part:
            s_T = k.sb(part, "s_T", [P, 3 * H, TT])

            def block_of(t, first):
                return lambda b: t[:, bass.ds(b + first, 1), :]

            project_groups(k, "sp", [group(C_SQ, block_of(s_T, 0), HD_SCALE), group(C_SK, block_of(s_T, H)),
                               group(C_SV, block_of(s_T, 2 * H))])
            stick_breaking_prompt(k, s_T)
            attention_decode(k, s_T)
        with ExitStack() as part:
            m_T = k.sb(part, "m_T", [P, 4 * H, TT])
            project_groups(k, "mp", [group(C_MQ, block_of(m_T, 0)), group(C_MK, block_of(m_T, H), HD_SCALE),
                               group(C_MV, block_of(m_T, 2 * H)),
                               group(C_MO, block_of(m_T, 3 * H), func=ACT.Sigmoid)], gates=range(5 * H, 6 * H))
            gate_terms(k)
            mlstm_prompt(k, m_T)
            mlstm_decode(k, m_T)
        k.retire_semaphores()
        h = k.sb(ctx, "h", [P, KD, TT])
        merge_branches(k, h)
        mix_out(k, h)
        normalise(k, h, k.g_mlp, "n1")
        feed_forward(k, h)
        k.p_hi = k.sb(ctx, "p_hi", [P, PLE // P, TT], F32R)
        k.p_lo = k.sb(ctx, "p_lo", [P, PLE // P, TT], F32R)
        k.ple_prod = k.sb(ctx, "ple_prod", [P, TT])
        turn_ple(k)
        normalise(k, h, k.g_ple, "n2")
        per_layer_embedding(k, h)
        final_norm(k, h)


_INS = ["x_prompt", "x_sample", "cache_k", "cache_v", "state_mlstm_C", "state_mlstm_n", "state_mlstm_m", "state_conv",
        "page_table", "p_prompt", "p_sample", "g_mix", "w_in", "b_if", "b_sb", "conv_w", "w_branch", "w_out", "g_mlp",
        "w_up", "w_down", "g_ple", "w_ple_gate", "w_ple", "g_final"]
_OUTS = [("y_prompt", (1, T, D)), ("y_sample", (B, 1, D)), ("k_prompt", (1, 1, T, H, P)), ("v_prompt", (1, 1, T, H, P)),
         ("C_prompt", (1, 1, H, P, P)), ("n_prompt", (1, 1, H, P)), ("m_prompt", (1, 1, H)), ("conv_prompt", (1, 1, 2, W)),
         ("k_sample", (1, B, 1, H, P)), ("v_sample", (1, B, 1, H, P)), ("C_sample", (1, B, H, P, P)),
         ("n_sample", (1, B, H, P)), ("m_sample", (1, B, H)), ("conv_sample", (1, B, 2, W))]


def kernel(**inputs):
    import numpy as _np
    import concourse.bacc as _bacc
    from concourse import mybir as _mybir
    from concourse.bass_utils import run_bass_kernel_spmd as _run

    nc = _bacc.Bacc("TRN2", target_bir_lowering=False, num_devices=1)
    arrays, io = {}, {}
    for name in _INS:
        a = _np.ascontiguousarray(inputs[name])
        arrays[f"in_{name}"] = a
        io[name] = nc.dram_tensor(f"in_{name}", a.shape, _mybir.dt.from_np(a.dtype), kind="ExternalInput").ap()
    for name, shape in _OUTS:
        io[name] = nc.dram_tensor(f"out_{name}", shape, _mybir.dt.float32, kind="ExternalOutput").ap()
    hybrid_layer(nc, io)
    r = _run(nc, [arrays], core_ids=[0])
    return tuple(r.results[0][f"out_{name}"] for name, _ in _OUTS)
```

```python
from contextlib import ExitStack

import concourse.bass as bass
from concourse import mybir
from concourse.alu_op_type import AluOpType as ALU

ACT = mybir.ActivationFunctionType
F32 = mybir.dt.float32
F32R = mybir.dt.float32r
I32 = mybir.dt.int32
AX = mybir.AxisListType

P = 128
D = 1024
KD = D // P
T = 1024
TB = T // P
B = 8
TT = T + B
NCH = 3
CW = TT // NCH
H = 4
W = H * P
PAGES = 8
N_PHYS = 80
FFN = 4 * D
PLE = 256
RING = 4
EPS = 1e-6
HD_SCALE = float(P) ** -0.5
BIG = 1e30
EXP_LN = "natural_log_exp_and_others"

C_MQ, C_MK, C_MV, C_MO, C_IF = 0, W, 2 * W, 3 * W, 4 * W
C_CB = 4 * W + 2 * H
C_CC, C_CX = C_CB + W, C_CB + 2 * W
C_SQ = C_CB + 3 * W
C_SK, C_SV = C_SQ + W, C_SQ + 2 * W
C_G = C_SQ + 3 * W
N_IN = C_G + 3 * D


class Chip:

    def __init__(self, nc, io):
        self.nc = nc
        self.io = io
        self.blocks = 0
        self.loads = 0
        self.phase_sems = []

    def sb(self, ctx, name, shape, dt=F32):
        return ctx.enter_context(self.nc.sbuf_tensor(name, shape, dt))

    def ps(self, ctx, name, shape, dt=F32):
        return ctx.enter_context(self.nc.psum_tensor(name, shape, dt))

    def sem(self, ctx, name):
        handle = self.nc.alloc_semaphore(name=name)
        self.phase_sems.append(handle)
        return handle

    def clear_semaphores(self, pool, sems):
        for sem in sems:
            pool.sem_clear(sem)
        self.cleared = sems

    def release_cleared(self):
        for sem in self.cleared:
            self.nc.release_semaphore(sem)



def load_weights(k, sp, n, par, src, kb=KD):
    sp.wait_ge(k.w_split, n + 1)
    sp.dma_start(k.w_raw[:, par, 0:kb, :], src).then_inc(k.w_landed[par], 16)


def split_weights(k, pool, n, par, pair, kb=KD):
    nc = k.nc
    pool.wait_ge(k.acc_ready, n * NCH + NCH)
    pool.sem_inc(k.pool_tick, 1)
    pool.wait_ge(k.w_landed[par], pair * 16 + 16)
    pool.sem_inc(k.pool_tick, 1)
    nc.gpsimd.tensor_scalar(k.w_hi[:, par, 0:kb, :], k.w_raw[:, par, 0:kb, :], 1.0, 1.0,
                            ALU.mult, ALU.mult).then_inc(k.w_rounded, 1)
    pool.wait_ge(k.w_rounded, n + 1)
    nc.gpsimd.tensor_tensor(k.w_lo[:, par, 0:kb, :], k.w_raw[:, par, 0:kb, :],
                            k.w_hi[:, par, 0:kb, :].bitcast(F32), ALU.subtract).then_inc(k.w_split, 1)


def each_ahead(eng, base, count, step):
    with eng.Fori(0, count // 2 - 1) as i:
        step(base + i * 2 + 1, 1, i * 2 + 1, base // 2 + i)
        step(base + i * 2 + 2, 0, i * 2 + 2, base // 2 + i + 1)
    step(base + count - 1, 1, count - 1, (base + count) // 2 - 1)


def split_ahead(k, pool, base, count, kb=KD, then_kb=KD):
    each_ahead(pool, base, count, lambda n, par, b, pair: split_weights(k, pool, n, par, pair, kb))
    split_weights(k, pool, base + count, 0, (base + count) // 2, then_kb)


def project_chunk(k, pe, n, par, c, x_hi, x_lo, kb=KD, k0=0):
    if c == 0:
        pe.wait_ge(k.w_split, n + 3)
    pe.wait_ge(k.acc_free, n * NCH + c + 1)
    cols = slice(c * CW, (c + 1) * CW)
    for i in range(kb):
        for j, (w, x) in enumerate(((k.w_hi, x_hi), (k.w_hi, x_lo), (k.w_lo, x_hi))):
            mm = k.nc.tensor.matmul(k.acc[:, c, 0:CW], w[:, par, i, :], x[:, k0 + i, cols],
                                    start=(i == 0 and j == 0), stop=(i == kb - 1 and j == 2))
    mm.then_inc(k.acc_ready, 1)


def acc_wait(k, eng, n, c):
    eng.wait_ge(k.acc_ready, n * NCH + c + 1 + 2 * NCH)


def constants(k):
    nc, io = k.nc, k.io
    with nc.Block() as block:
        @block.gpsimd
        def _(pool):
            nc.gpsimd.memset(k.ident[:, :], 0.0)
            nc.gpsimd.memset(k.ones[:, :], 1.0)
            nc.gpsimd.memset(k.neg_ones[:, :], -1.0)
            nc.gpsimd.memset(k.sum_to[:, :], 1.0)
            nc.gpsimd.memset(k.neg_from[:, :], -1.0)
            nc.gpsimd.memset(k.late_big[:, :], 0.0)
            nc.gpsimd.memset(k.late_neg[:, :], 0.0)
            nc.gpsimd.memset(k.eps[:, :], EPS)
            nc.gpsimd.memset(k.before[:, :], 1.0)
            nc.gpsimd.memset(k.two_idents[:, :], 0.0)
            pool.drain()
            nc.gpsimd.affine_select(out=k.two_idents[:, :], in_=k.two_idents[:, :], compare_op=ALU.not_equal, fill=1.0,
                                    base=0, pattern=[[-1, 2 * H]], channel_multiplier=1)
            pool.drain()
            nc.gpsimd.affine_select(out=k.two_idents[:, :], in_=k.two_idents[:, :], compare_op=ALU.not_equal, fill=1.0,
                                    base=-2 * H, pattern=[[-1, 2 * H]], channel_multiplier=1)
            nc.gpsimd.affine_select(out=k.before[:, :], in_=k.before[:, :], compare_op=ALU.is_gt, fill=0.0,
                                    base=0, pattern=[[1, P]], channel_multiplier=-1)
            nc.gpsimd.affine_select(out=k.ident[:, :], in_=k.ident[:, :], compare_op=ALU.not_equal, fill=1.0,
                                    base=0, pattern=[[-1, P]], channel_multiplier=1)
            nc.gpsimd.affine_select(out=k.sum_to[:, :], in_=k.sum_to[:, :], compare_op=ALU.is_ge, fill=0.0,
                                    base=0, pattern=[[1, P]], channel_multiplier=-1)
            nc.gpsimd.affine_select(out=k.neg_from[:, :], in_=k.neg_from[:, :], compare_op=ALU.is_ge, fill=0.0,
                                    base=0, pattern=[[-1, P]], channel_multiplier=1)
            nc.gpsimd.affine_select(out=k.late_big[:, :], in_=k.late_big[:, :], compare_op=ALU.is_ge, fill=BIG,
                                    base=0, pattern=[[1, P]], channel_multiplier=-1)
            nc.gpsimd.affine_select(out=k.late_neg[:, :], in_=k.late_neg[:, :], compare_op=ALU.is_ge, fill=-BIG,
                                    base=0, pattern=[[-1, P]], channel_multiplier=1)
            pool.sem_inc(k.w_split, 2)
            pool.sem_inc(k.acc_ready, 2 * NCH)
            pool.sem_inc(k.acc_free, NCH)

        @block.sync
        def _(sp):
            def column(dst, src):
                sp.dma_start(dst, src, allow_slow_non_contiguous=True).then_inc(k.params_in, 16)
            column(k.g_mix[:, :], io["g_mix"].rearrange("l (k p) -> p (l k)", p=P))
            column(k.g_mlp[:, :], io["g_mlp"].rearrange("l (k p) -> p (l k)", p=P))
            column(k.g_ple[:, :], io["g_ple"].rearrange("l (k p) -> p (l k)", p=P))
            column(k.b_if[:, :], io["b_if"].to_broadcast([P, 2 * H]))
            column(k.b_sb[:, :], io["b_sb"].to_broadcast([P, H]))
            for j in range(3):
                column(k.conv_w[:, j, :], io["conv_w"][0, j, :].rearrange("(k p) -> p k", p=P))
            sp.wait_ge(k.params_in, 8 * 16)


def normalise_input(k, then):
    nc, io = k.nc, k.io
    tiles = [(t * P, P) for t in range(TB)] + [(T, B)]
    with ExitStack() as ctx:
        rows = k.sb(ctx, "x_rows", [P, 3, D])
        squares = k.sb(ctx, "x_squares", [P, D])
        scales = k.sb(ctx, "x_scales", [P, 2, P])
        sums = k.sb(ctx, "x_sums", [P, len(tiles)])
        rstd = k.sb(ctx, "x_rstd", [P, len(tiles)])
        turned = k.sb(ctx, "x_turned", [P, 2, KD, P])
        gained = k.sb(ctx, "x_gained", [P, 2, KD, P])
        pt_x = k.ps(ctx, "pt_x", [P, KD, P])
        pt_s = k.ps(ctx, "pt_s", [P, KD, P])
        rows_in = [k.sem(ctx, f"rows_in{i}") for i in range(3)]
        x_out = [k.sem(ctx, f"x_out{i}") for i in range(2)]
        scaled_ok, turned_x, turned_s, x_read, s_read, rounded, split, rms = (
            k.sem(ctx, n) for n in ("scaled_ok", "turned_x", "turned_s", "x_read", "s_read",
                                    "rounded", "split", "rms"))
        x_p = io["x_prompt"].rearrange("b t d -> (b t) d")
        x_s = io["x_sample"].rearrange("b t d -> (b t) d")
        with nc.Block() as block:
            @block.sync
            def _(sp):
                def store(i):
                    t0, m = tiles[i]
                    sp.wait_ge(x_read, i + 1)
                    sp.dma_start(k.x_T[:, :, t0:t0 + m], turned[:, i % 2, :, 0:m]).then_inc(x_out[i % 2], 16)

                load_weights(k, sp, k.blocks, 0, then)
                for i, (t0, m) in enumerate(tiles):
                    if i >= 3:
                        sp.wait_ge(turned_s, i - 2)
                    src = x_p[t0:t0 + m, :] if t0 < T else x_s
                    sp.dma_start(rows[0:m, i % 3, :], src).then_inc(rows_in[i % 3], 16)
                    if i >= 2:
                        store(i - 2)
                store(len(tiles) - 2)
                store(len(tiles) - 1)
                for i in range(2):
                    sp.wait_ge(x_out[i], 16 * len(tiles[i::2]))

            @block.scalar
            def _(act):
                act.preload_act_table_set(EXP_LN)
                act.wait_ge(k.params_in, 8 * 16)

                def root(i):
                    t0, m = tiles[i]
                    act.wait_ge(rows_in[i % 3], 16 * (i // 3 + 1))
                    if i >= 2:
                        act.wait_ge(scaled_ok, i - 1)
                    nc.scalar.activation(squares[0:m, :], rows[0:m, i % 3, :], ACT.Square,
                                         accum_out=sums[0:m, i:i + 1])
                    act.drain()
                    nc.scalar.activation(rstd[0:m, i:i + 1], sums[0:m, i:i + 1], ACT.Ln,
                                         scale=1.0 / D, bias=k.eps[0:m, :])
                    act.drain()
                    nc.scalar.activation(rstd[0:m, i:i + 1], rstd[0:m, i:i + 1], ACT.Exp, scale=-0.5).then_inc(rms, 1)

                root(0)
                for i, (t0, m) in enumerate(tiles):
                    if i + 1 < len(tiles):
                        root(i + 1)
                    act.wait_ge(s_read, i + 1)
                    nc.scalar.activation(k.x_hi[:, :, t0:t0 + m], gained[:, i % 2, :, 0:m], ACT.Copy)\
                       .then_inc(rounded, 1)

            @block.vector
            def _(dve):
                for i, (t0, m) in enumerate(tiles):
                    dve.wait_ge(rms, i + 1)
                    if i >= 2:
                        dve.wait_ge(turned_s, i - 1)
                    nc.vector.tensor_scalar(scales[0:m, i % 2, 0:m], k.ident[0:m, 0:m], rstd[0:m, i:i + 1],
                                            None, ALU.mult).then_inc(scaled_ok, 1)
                    dve.wait_ge(turned_x, i + 1)
                    if i >= 2:
                        dve.wait_ge(x_out[i % 2], 16 * (i // 2))
                    nc.vector.tensor_copy(turned[:, i % 2, :, 0:m], pt_x[:, :, 0:m]).then_inc(x_read, 1)
                    dve.wait_ge(turned_s, i + 1)
                    if i >= 2:
                        dve.wait_ge(split, i - 1)
                    nc.vector.tensor_tensor(gained[:, i % 2, :, 0:m], pt_s[:, :, 0:m],
                                            k.g_mix[:, :].unsqueeze(2).to_broadcast([P, KD, m]),
                                            ALU.mult).then_inc(s_read, 1)

            @block.gpsimd
            def _(pool):
                split_weights(k, pool, k.blocks, 0, k.blocks // 2)
                for i, (t0, m) in enumerate(tiles):
                    pool.wait_ge(rounded, i + 1)
                    nc.gpsimd.tensor_tensor(k.x_lo[:, :, t0:t0 + m], gained[:, i % 2, :, 0:m],
                                            k.x_hi[:, :, t0:t0 + m].bitcast(F32), ALU.subtract).then_inc(split, 1)

            @block.tensor
            def _(pe):
                for i, (t0, m) in enumerate(tiles):
                    pe.wait_ge(rows_in[i % 3], 16 * (i // 3 + 1))
                    if i:
                        pe.wait_ge(x_read, i)
                    for b in range(KD):
                        tr = nc.tensor.transpose(pt_x[:, b, 0:m], rows[0:m, i % 3, b * P:(b + 1) * P],
                                                 k.ident[0:m, 0:m])
                    tr.then_inc(turned_x, 1)
                    pe.wait_ge(scaled_ok, i + 1)
                    if i:
                        pe.wait_ge(s_read, i)
                    for b in range(KD):
                        tr = nc.tensor.matmul(pt_s[:, b, 0:m], rows[0:m, i % 3, b * P:(b + 1) * P],
                                              scales[0:m, i % 2, 0:m], start=True, stop=True)
                    tr.then_inc(turned_s, 1)


def project_attention(k, groups, s_T, then):
    nc, io = k.nc, k.io
    base = k.blocks
    count = H * len(groups)
    part = ExitStack()
    turned = k.ps(part, "q_turned", [B, W])
    q_turned = k.sem(part, "q_turned")
    w_in = io["w_in"].rearrange("l (k p) n -> p (l k) n", p=P)
    with nc.Block() as block:
        @block.sync
        def _(sp):
            each_ahead(sp, base, count, lambda n, par, b, pair: load_weights(
                k, sp, n, par, w_in[:, :, bass.ds(b * P + groups[0]["col"], P)]))
            load_weights(k, sp, base + count, 0, then)

        @block.gpsimd
        def _(pool):
            split_ahead(k, pool, base, count)

        @block.tensor
        def _(pe):
            with pe.Fori(0, count // 2) as i:
                for par in range(2):
                    for c in range(NCH):
                        project_chunk(k, pe, base + i * 2 + par, par, c, k.x_hi, k.x_lo)
            pe.wait_ge(k.acc_free, (base + H) * NCH + NCH)
            for h in range(H):
                tr = nc.tensor.transpose(turned[:, h * P:(h + 1) * P], s_T[:, h, T:TT], k.ident[:, :])
            tr.then_inc(q_turned, 1)

        @block.vector
        def _(dve):
            dve.wait_ge(q_turned, 1)
            nc.vector.tensor_copy(k.q_tok[:, :], turned[:, :])

        @block.scalar
        def _(act):
            for gi, g in enumerate(groups):
                with act.Fori(0, H // 2) as i:
                    for par in range(2):
                        b = i * 2 + par
                        for c in range(NCH):
                            acc_wait(k, act, base + gi * H + b, c)
                            nc.scalar.activation(g["out"](b)[:, :, c * CW:(c + 1) * CW], k.acc[:, c:c + 1, 0:CW],
                                                 g["func"], scale=g["scale"]).then_inc(k.acc_free, 1)
    part.close()
    k.blocks = base + count


def turn_states(k):
    nc, io = k.nc, k.io
    with ExitStack() as ctx:
        conv_rows = k.sb(ctx, "conv_rows", [2 * B, W])
        n_rows = k.sb(ctx, "n_rows", [B * H, P])
        pt = k.ps(ctx, "pt_states", [P, 512])
        rows_in, turned = k.sem(ctx, "states_in"), k.sem(ctx, "states_turned")
        with nc.Block() as block:
            @block.sync
            def _(sp):
                sp.dma_start(conv_rows[:, :], io["state_conv"].rearrange("l b s c -> (l b s) c")).then_inc(rows_in, 16)
                sp.dma_start(n_rows[:, :], io["state_mlstm_n"].rearrange("l b h d -> (l b h) d")).then_inc(rows_in, 16)
                sp.dma_start(io["conv_sample"][0, :, 0, :], io["state_conv"][0, :, 1, :]).then_inc(rows_in, 16)
                sp.wait_ge(rows_in, 48)

            @block.tensor
            def _(pe):
                pe.wait_ge(rows_in, 48)
                for h in range(H):
                    nc.tensor.transpose(pt[:, h * 2 * B:(h + 1) * 2 * B], conv_rows[:, h * P:(h + 1) * P],
                                        k.ident[0:2 * B, 0:2 * B])
                nc.tensor.transpose(pt[:, 128:128 + B * H], n_rows[:, :], k.ident[0:B * H, 0:B * H]).then_inc(turned, 1)

            @block.vector
            def _(dve):
                dve.wait_ge(turned, 1)
                nc.vector.tensor_copy(k.conv_state[:, :, :], pt[:, 0:H * 2 * B].rearrange("p (h c) -> p h c", h=H))
                nc.vector.tensor_copy(k.n_old[:, :], pt[:, 128:128 + B * H])


UNITS = [(half, kb, max(0, kb * P - half * 512)) for half in range(2) for kb in range(4 * half + 3, -1, -1)]
NU = len(UNITS)


def unit_is_first(u):
    return u == 0 or UNITS[u][0] != UNITS[u - 1][0]


def unit_is_diagonal(u):
    return UNITS[u][1] >= 4 * UNITS[u][0]


NDIAG = sum(unit_is_diagonal(u) for u in range(NU))
DIAG_BEFORE = [sum(unit_is_diagonal(v) for v in range(u)) for u in range(NU + 1)]


def stick_breaking_prompt(k, s_T, then):
    nc, io = k.nc, k.io
    base = k.blocks
    NB = 4
    SLOTS = NB * NCH
    cols = (C_CC, C_CX, C_CB, C_G)
    w_in = io["w_in"].rearrange("l (k p) n -> p (l k) n", p=P)
    with ExitStack() as ctx:
        k_head = k.sb(ctx, "k_head", [P, TT])
        v_head = k.sb(ctx, "v_head", [P, TT])
        k_tok = k.sb(ctx, "k_tok", [P, TB, P])
        v_tok = k.sb(ctx, "v_tok", [P, TB, P])
        kv_dec = k.sb(ctx, "kv_dec", [B, 2, P])
        bias = k.sb(ctx, "sb_bias", [P, 1])
        z_abs = k.sb(ctx, "z_abs", [P, 2, 512])
        z_in = k.sb(ctx, "z_in", [P, 2, 512])
        sp_ = k.sb(ctx, "softplus", [P, 2, 512])
        later = k.sb(ctx, "sp_later", [P, 2, 512])
        prob = k.sb(ctx, "prob", [P, 2, 512])
        y_out = k.sb(ctx, "y_stick", [P, T])
        proj = k.sb(ctx, "proj_out", [P, NB, TT])
        cx = k.sb(ctx, "cx", [P, 2 + TT])
        conv = proj[:, 1, :]
        tails = k.sb(ctx, "cx_tails", [P, H, 2 + B])
        tail_rows = y_out[0:2 + B, 0:W]
        z = k.ps(ctx, "z", [P, 3, 512])
        y = k.ps(ctx, "y", [P, 2, 512])
        names = ("staged", "bias_ready", "kv_turned", "v_ready", "kv_ready", "z_ready", "abs_ready", "z_read", "exp_ready", "log_ready",
                 "sp_ready", "later_ready", "sums_added", "exp_done", "prob_ready", "av_done", "y_ready", "y_read",
                 "k_out", "v_out", "kd_out", "vd_out", "y_sent", "conv_sent", "gate_sent", "cx_ready", "conv_ready",
                 "tails_turned", "tails_ready", "tails_out", "gate_ready")
        s = {n: k.sem(ctx, "sb_" + n) for n in names}
        with nc.Block() as block:
            @block.sync
            def _(sp):
                def load(j, b):
                    load_weights(k, sp, base + j * NB + b, b % 2, w_in[:, :, bass.ds(j * P + cols[b], P)])

                with sp.Fori(0, H - 1) as j:
                    for b in range(1, NB):
                        load(j, b)
                    load_weights(k, sp, base + j * NB + NB, 0, w_in[:, :, bass.ds(j * P + (cols[0] + P), P)])
                for b in range(1, NB):
                    load(H - 1, b)
                load_weights(k, sp, base + H * NB, 0, then)
                sp.wait_ge(s["tails_ready"], 1)
                sp.dma_start(io["conv_prompt"][0, 0, :, :], tail_rows[0:2, :]).then_inc(s["tails_out"], 16)
                sp.dma_start(io["conv_sample"][0, :, 1, :], tail_rows[2:2 + B, :]).then_inc(s["tails_out"], 16)
                sp.wait_ge(s["tails_out"], 32)

            @block.tensor
            def _(pe):
                def turn_kv(j):
                    pe.wait_ge(s["staged"], j + 1)
                    pe.wait_ge(s["exp_done"], j * NU)
                    pe.wait_ge(s["y_read"], j * 2)
                    for tb in range(TB):
                        nc.tensor.transpose(z[:, tb // 4, (tb % 4) * P:(tb % 4 + 1) * P],
                                            v_head[:, tb * P:(tb + 1) * P], k.ident[:, :])
                    nc.tensor.transpose(z[0:B, 2, 0:P], v_head[:, T:TT], k.ident[:, :])
                    for tb in range(TB):
                        nc.tensor.transpose(y[:, tb // 4, (tb % 4) * P:(tb % 4 + 1) * P],
                                            k_head[:, tb * P:(tb + 1) * P], k.ident[:, :])
                    nc.tensor.transpose(z[0:B, 2, P:2 * P], k_head[:, T:TT], k.ident[:, :]).then_inc(s["kv_turned"], 1)

                def scores(j, u):
                    half, kb, first = UNITS[u]
                    if u == 0:
                        pe.wait_ge(s["v_ready"], j + 1)
                        pe.wait_ge(s["kv_ready"], j + 1)
                    if u >= 3:
                        pe.wait_ge(s["exp_done"], j * NU + u - 2)
                    nc.tensor.matmul(z[:, u % 3, first:512], k_head[:, kb * P:(kb + 1) * P],
                                     s_T[:, bass.ds(j, 1), half * 512 + first:(half + 1) * 512],
                                     start=True, stop=True).then_inc(s["z_ready"], 1)

                def sums(j, u):
                    half, kb, first = UNITS[u]
                    pe.wait_ge(s["sp_ready"], j * NU + u + 1)
                    mm = nc.tensor.matmul(z[:, u % 3, first:512], k.neg_from[:, :], sp_[:, u % 2, first:512],
                                          start=False, stop=True, skip_group_check=True)
                    if not unit_is_first(u):
                        pe.wait_ge(s["later_ready"], j * NU + u)
                        before = UNITS[u - 1][2]
                        mm = nc.tensor.matmul(z[:, u % 3, before:512], k.neg_ones[:, :], later[:, (u - 1) % 2, before:512],
                                              start=False, stop=True, skip_group_check=True)
                    mm.then_inc(s["sums_added"], 1)

                def values(j, u):
                    half, kb, first = UNITS[u]
                    pe.wait_ge(s["exp_done"], j * NU + u + 1)
                    if unit_is_diagonal(u):
                        pe.wait_ge(s["prob_ready"], j * NDIAG + DIAG_BEFORE[u] + 1)
                    nc.tensor.matmul(y[:, half, first:512], v_tok[:, kb, :], prob[:, u % 2, first:512],
                                     start=unit_is_first(u), stop=(kb == 0), skip_group_check=True)\
                        .then_inc(s["av_done"], 1)

                with pe.Fori(0, H) as j:
                    for slot in range(SLOTS + 3):
                        if slot < SLOTS:
                            b, c = divmod(slot, NCH)
                            project_chunk(k, pe, base + j * NB + b, b % 2, c, k.x_hi, k.x_lo)
                        if slot == 0:
                            turn_kv(j)
                        if 0 <= slot - 1 < NU:
                            scores(j, slot - 1)
                        if 0 <= slot - 2 < NU:
                            sums(j, slot - 2)
                        if 0 <= slot - 3 < NU:
                            values(j, slot - 3)
                pe.wait_ge(s["conv_ready"], H)
                for h in range(H):
                    tr = nc.tensor.transpose(z[0:2 + B, 0, h * P:(h + 1) * P], tails[:, h, :], k.ident[:, :])
                tr.then_inc(s["tails_turned"], 1)

            @block.scalar
            def _(act):
                act.preload_act_table_set(EXP_LN)

                def softplus_log(j, u):
                    _, _, first = UNITS[u]
                    act.wait_ge(s["z_read"], j * NU + u + 1)
                    act.wait_ge(s["sp_ready"], j * NU + max(u - 1, 0))
                    nc.scalar.activation(z_abs[:, u % 2, first:512], z_in[:, u % 2, first:512], ACT.Abs).then_inc(s["abs_ready"], 1)
                    act.wait_ge(s["abs_ready"], j * NU + u + 1)
                    nc.scalar.activation(z_abs[:, u % 2, first:512], z_abs[:, u % 2, first:512], ACT.Exp,
                                         scale=-1.0).then_inc(s["exp_ready"], 1)
                    act.wait_ge(s["exp_ready"], j * NU + u + 1)
                    nc.scalar.activation(z_abs[:, u % 2, first:512], z_abs[:, u % 2, first:512], ACT.Ln,
                                         bias=1.0).then_inc(s["log_ready"], 1)

                def probs(j, u):
                    _, _, first = UNITS[u]
                    act.wait_ge(s["sums_added"], j * NU + u + 1)
                    if u >= 2:
                        act.wait_ge(s["av_done"], j * NU + u - 1)
                    nc.scalar.activation(prob[:, u % 2, first:512], z[:, u % 3, first:512], ACT.Exp,
                                         bias=bias[:, :]).then_inc(s["exp_done"], 1)

                with act.Fori(0, H) as j:
                    act.wait_ge(s["z_ready"], j * NU)
                    nc.scalar.activation(k_head[:, :].unsqueeze(1), s_T[:, bass.ds(j + H, 1), :], ACT.Copy)
                    nc.scalar.activation(v_head[:, :].unsqueeze(1), s_T[:, bass.ds(j + 2 * H, 1), :], ACT.Copy)\
                      .then_inc(s["staged"], 1)
                    for slot in range(SLOTS + 2):
                        if slot < SLOTS:
                            b, c = divmod(slot, NCH)
                            if slot == 0:
                                act.wait_ge(s["cx_ready"], j)
                            if slot == NCH:
                                act.wait_ge(s["conv_sent"], j * 16)
                            if slot == 2 * NCH:
                                act.wait_ge(s["conv_ready"], j)
                            if slot == 3 * NCH:
                                act.wait_ge(s["gate_sent"], j * 16)
                            acc_wait(k, act, base + j * NB + b, c)
                            nc.scalar.activation(proj[:, b, c * CW:(c + 1) * CW], k.acc[:, c, 0:CW], ACT.Copy)\
                              .then_inc(k.acc_free, 1)
                        if slot == 0:
                            act.wait_ge(s["kv_turned"], j + 1)
                            act.wait_ge(s["v_out"], j * 16)
                            act.wait_ge(s["av_done"], j * NU)
                            nc.scalar.activation(v_tok[:, :, :], z[:, 0:2, :].rearrange("p a (b d) -> p (a b) d", d=P),
                                                 ACT.Copy).then_inc(s["v_ready"], 1)
                            act.wait_ge(s["v_ready"], j + 1)
                            act.dma_start(io["v_prompt"][0, 0, :, bass.ds(j, 1), :].rearrange("(b p) o d -> p (b o) d", p=P),
                                          v_tok[:, :, :]).then_inc(s["v_out"], 16)
                            act.wait_ge(s["kv_ready"], j + 1)
                            act.dma_start(io["k_prompt"][0, 0, :, bass.ds(j, 1), :].rearrange("(b p) o d -> p (b o) d", p=P),
                                          k_tok[:, :, :]).then_inc(s["k_out"], 16)
                            act.dma_start(io["v_sample"][0, :, 0, bass.ds(j, 1), :].rearrange("b o d -> b (o d)"),
                                          kv_dec[:, 0, :]).then_inc(s["vd_out"], 16)
                            act.dma_start(io["k_sample"][0, :, 0, bass.ds(j, 1), :].rearrange("b o d -> b (o d)"),
                                          kv_dec[:, 1, :]).then_inc(s["kd_out"], 16)
                        if 0 <= slot - 1 < NU:
                            softplus_log(j, slot - 1)
                        if 0 <= slot - 2 < NU:
                            probs(j, slot - 2)
                    act.wait_ge(k.acc_free, (base + j * NB + NB) * NCH + NCH)
                    act.dma_start(k.gates[:, bass.ds(j, 1), :], proj[:, 3:4, :]).then_inc(s["gate_sent"], 16)
                    act.wait_ge(s["conv_ready"], j + 1)
                    act.dma_start(k.branch[1, :, bass.ds(j, 1), :], proj[:, 1:2, :]).then_inc(s["conv_sent"], 16)
                    act.wait_ge(s["y_read"], j * 2 + 2)
                    act.dma_start(k.branch[2, :, bass.ds(j, 1), 0:T], y_out[:, :].unsqueeze(1)).then_inc(s["y_sent"], 16)
                for n in ("v_out", "k_out", "vd_out", "kd_out", "gate_sent", "conv_sent", "y_sent"):
                    act.wait_ge(s[n], 16 * H)

            @block.vector
            def _(dve):
                nc.vector.memset(cx[:, 0:2], 0.0)

                def softplus_parts(j, u):
                    _, _, first = UNITS[u]
                    dve.wait_ge(s["z_ready"], j * NU + u + 1)
                    nc.vector.tensor_scalar(z_in[:, u % 2, first:512], z[:, u % 3, first:512], bias[:, :], None,
                                            ALU.add).then_inc(s["z_read"], 1)

                def softplus_sum(j, u):
                    _, _, first = UNITS[u]
                    dve.wait_ge(s["log_ready"], j * NU + u + 1)
                    dve.wait_ge(s["z_read"], j * NU + u + 1)
                    if u >= 2:
                        dve.wait_ge(s["sums_added"], j * NU + u - 1)
                        dve.wait_ge(s["later_ready"], j * NU + u - 1)
                    if u == 0:
                        dve.wait_ge(s["later_ready"], j * NU)
                    nc.vector.scalar_tensor_tensor(out=sp_[:, u % 2, first:512], in0=z_in[:, u % 2, first:512], scalar=0.0,
                                                   in1=z_abs[:, u % 2, first:512], op0=ALU.max, op1=ALU.add)
                    if unit_is_diagonal(u):
                        dve.drain()
                        nc.vector.tensor_tensor(sp_[:, u % 2, first:first + P], sp_[:, u % 2, first:first + P],
                                                k.before[:, :], ALU.mult).then_inc(s["sp_ready"], 1)
                    else:
                        dve.drain().then_inc(s["sp_ready"], 1)

                def read_y(j, half):
                    u = 4 if half == 0 else NU
                    dve.wait_ge(s["av_done"], j * NU + u)
                    nc.vector.tensor_copy(y_out[:, half * 512:(half + 1) * 512], y[:, half, :]).then_inc(s["y_read"], 1)

                with dve.Fori(0, H) as j:
                    dve.wait_ge(s["exp_done"], j * NU)
                    nc.vector.tensor_copy(bias[:, :], k.b_sb[:, bass.ds(j, 1)]).then_inc(s["bias_ready"], 1)
                    dve.wait_ge(s["bias_ready"], j + 1)
                    dve.wait_ge(s["kv_turned"], j + 1)
                    dve.wait_ge(s["k_out"], j * 16)
                    dve.wait_ge(s["vd_out"], j * 16)
                    dve.wait_ge(s["kd_out"], j * 16)
                    nc.vector.tensor_copy(k_tok[:, :, :], y[:, :, :].rearrange("p a (b d) -> p (a b) d", d=P))
                    nc.vector.tensor_copy(kv_dec[:, :, :], z[0:B, 2, 0:2 * P].rearrange("p (a d) -> p a d", d=P))\
                      .then_inc(s["kv_ready"], 1)
                    for u in range(NU):
                        softplus_parts(j, u)
                        softplus_sum(j, u)
                        if u == 6:
                            dve.wait_ge(s["y_sent"], j * 16)
                            read_y(j, 0)
                        if u == 8:
                            dve.wait_ge(k.acc_free, (base + j * NB + 2) * NCH + NCH)
                            nc.vector.tensor_tensor(cx[:, 2:2 + TT], proj[:, 0, :], proj[:, 1, :],
                                                    ALU.mult).then_inc(s["cx_ready"], 1)
                    dve.wait_ge(k.acc_free, (base + j * NB + 3) * NCH + NCH)
                    dve.wait_ge(s["cx_ready"], j + 1)
                    nc.vector.tensor_scalar(conv[:, :], cx[:, 2:2 + TT], k.conv_w[:, 2, bass.ds(j, 1)], None, ALU.mult)
                    nc.vector.tensor_copy(tails[:, bass.ds(j, 1), :], cx[:, T:T + 2 + B].unsqueeze(1))
                    for tap in (1, 0):
                        dve.drain()
                        nc.vector.scalar_tensor_tensor(out=conv[:, 0:T], in0=cx[:, tap:tap + T],
                                                       scalar=k.conv_w[:, tap, bass.ds(j, 1)], in1=conv[:, 0:T],
                                                       op0=ALU.mult, op1=ALU.add)
                        nc.vector.scalar_tensor_tensor(out=conv[:, T:TT], in0=k.conv_state[:, bass.ds(j, 1), tap::2].squeeze(1),
                                                       scalar=k.conv_w[:, tap, bass.ds(j, 1)], in1=conv[:, T:TT],
                                                       op0=ALU.mult, op1=ALU.add)
                    dve.drain()
                    nc.vector.tensor_tensor(conv[:, :], conv[:, :], proj[:, 2, :], ALU.mult).then_inc(s["conv_ready"], 1)
                    read_y(j, 1)
                dve.wait_ge(s["tails_turned"], 1)
                dve.wait_ge(s["y_sent"], H * 16)
                nc.vector.tensor_copy(tail_rows[:, :], z[0:2 + B, 0, :]).then_inc(s["tails_ready"], 1)

            @block.gpsimd
            def _(pool):
                def add_later(j, u):
                    _, _, first = UNITS[u]
                    pool.wait_ge(s["sp_ready"], j * NU + u + 1)
                    if u >= 2:
                        pool.wait_ge(s["sums_added"], j * NU + u)
                    pool.wait_ge(s["later_ready"], j * NU + u)
                    before = 512 if unit_is_first(u) else UNITS[u - 1][2]
                    if first < before:
                        pool.sem_inc(k.pool_tick, 1)
                        op = nc.gpsimd.tensor_scalar(later[:, u % 2, first:before], sp_[:, u % 2, first:before], 1.0, 1.0,
                                                     ALU.mult, ALU.mult)
                    if before < 512:
                        op = nc.gpsimd.tensor_tensor(later[:, u % 2, before:512], later[:, (u - 1) % 2, before:512],
                                                     sp_[:, u % 2, before:512], ALU.add)
                    op.then_inc(s["later_ready"], 1)

                def mask_prob(j, u):
                    _, _, first = UNITS[u]
                    pool.wait_ge(s["exp_done"], j * NU + u + 1)
                    pool.sem_inc(k.pool_tick, 1)
                    nc.gpsimd.affine_select(out=prob[:, u % 2, first:first + P], in_=prob[:, u % 2, first:first + P],
                                            compare_op=ALU.is_gt, fill=0.0, base=0, pattern=[[1, P]],
                                            channel_multiplier=-1).then_inc(s["prob_ready"], 1)

                with pool.Fori(0, H) as j:
                    for slot in range(SLOTS + 2):
                        if slot % NCH == 0 and slot < SLOTS:
                            b = slot // NCH + 1
                            split_weights(k, pool, base + j * NB + b, b % 2, base // 2 + j * (NB // 2) + b // 2)
                        if 0 <= slot - 1 < NU:
                            add_later(j, slot - 1)
                        if 0 <= slot - 2 < NU and unit_is_diagonal(slot - 2):
                            mask_prob(j, slot - 2)
    k.blocks = base + H * NB


N_E = 4
E_STATE, E_NEGM, E_KEY, E_DECAY = range(N_E)
GATE_COLS = TB * H


def project_mlstm(k, m_T, groups, then):
    nc, io = k.nc, k.io
    base = k.blocks
    old_sems = list(k.phase_sems)
    N = B * PAGES * H
    HALF = PAGES // 2
    FIRST_GATE = 5 * H
    w_in = io["w_in"].rearrange("l (k p) n -> p (l k) n", p=P)
    with ExitStack() as ctx:
        gate_out = k.sb(ctx, "mp_gate_out", [P, 2, TT])
        table = k.sb(ctx, "pages", [1, B * PAGES], I32)
        page = k.sb(ctx, "page", [P, RING, W])
        q_own = k.sb(ctx, "q_own", [B, W])
        prod = k.sb(ctx, "qk_prod", [P, 2, W])
        z = k.sb(ctx, "dec_z", [P, B, PAGES, H])
        z_abs = k.sb(ctx, "dec_z_abs", [P, B, PAGES, H])
        sp_ = k.sb(ctx, "dec_sp", [P, B, PAGES, H])
        later = k.sb(ctx, "dec_later", [P, B, PAGES, H])
        q_row = k.ps(ctx, "q_row", [P, W])
        w_if = k.sb(ctx, "w_if", [P, KD, 2 * H])
        w_if2 = k.sb(ctx, "w_if2", [P, KD, 2, 2 * H], F32R)
        raw = k.sb(ctx, "if_raw", [P, TB + 1, 2 * H])
        f_abs = k.sb(ctx, "f_abs", [P, TB, H])
        log_f = k.sb(ctx, "log_f", [P, TB, H])
        total = k.sb(ctx, "log_f_total", [P, TB, H])
        b_sum = k.sb(ctx, "b_sum", [P, TB, H])
        spread = k.sb(ctx, "g_spread", [P, 2, H, P])
        junk = k.sb(ctx, "max_junk", [P, P])
        g_max = k.sb(ctx, "g_max", [P, TB, H])
        mu_last = k.sb(ctx, "mu_last", [P, TB, H])
        m_prev = k.sb(ctx, "m_prev", [P, TB + 1, H])
        sums = k.ps(ctx, "sums_ps", [P, 512])
        g_rows = k.ps(ctx, "g_rows", [P, 2, 512])
        by_gate = k.ps(ctx, "if_by_gate", [4 * H, 512])
        if_rows = k.sb(ctx, "if_rows", [4 * H, TT])
        gp = sums[:, 256:256 + (TB + 1) * 2 * H].rearrange("p (t g) -> p t g", g=2 * H)
        s = {n: k.sem(ctx, "mp_" + n) for n in (
            "table_in", "own_ready", "rows_ready", "multiplied", "reduced", "z_ready", "z_log_ready", "sp_ready",
            "z_summed", "arg_ready",
            "w_in", "w_ready", "if_ready", "if_read", "projected", "raw_ready", "log_ready", "log_f_ready", "summed", "spread_ready",
            "g_rows_ready", "g_rows_read", "exps_in", "m_out")}
        gate_sent = [k.sem(ctx, f"mp_gate_sent{b}") for b in range(2)]
        landed = [k.sem(ctx, f"k_page_landed{i}") for i in range(RING)]
        flat = "p b g h -> p (b g h)"
        MQ, MK, MV, MO, GATES = range(5)
        order = groups + [dict(col=C_G + FIRST_GATE * P, out=None, scale=1.0, func=ACT.Copy)]

        with nc.Block() as block:
            def walk(eng, step, after, straight=()):
                for gi, g in enumerate(order):
                    n = base + gi * H
                    if gi in straight:
                        for b in range(H):
                            step(gi, g, n + b, b % 2, (n + b) // 2, b, b // 2 + gi * 2)
                        after(gi)
                        continue
                    with eng.Fori(0, H // 2) as i:
                        for par in range(2):
                            step(gi, g, n + i * 2 + par, par, n // 2 + i, i * 2 + par, i + gi * 2)
                    after(gi)

            @block.sync
            def _(sp):
                sp.dma_start(table[:, :], io["page_table"].rearrange("b g -> (b g)").unsqueeze(0)).then_inc(s["table_in"], 16)
                sp.dma_start(w_if[:, :, :], w_in[:, :, C_IF:C_IF + 2 * H],
                             allow_slow_non_contiguous=True).then_inc(s["w_in"], 16)
                sp.wait_ge(s["table_in"], 16)

                def load(n, par, b, first=C_MQ):
                    load_weights(k, sp, n, par, w_in[:, :, bass.ds(b * P + first, P)])

                def pages(q, half):
                    load_pages(k, sp, table, q, half, io["cache_k"], page, s["multiplied"], landed)

                with sp.Fori(0, B - 1) as q:
                    load(base + q * 2 + 1, 1, q * 2 + 1)
                    pages(q, 0)
                    load(base + q * 2 + 2, 0, q * 2 + 2)
                    pages(q, 1)
                load(base + 2 * B - 1, 1, 2 * B - 1)
                pages(B - 1, 0)
                load(base + 2 * B, 0, 0, C_G + FIRST_GATE * P)
                pages(B - 1, 1)
                for b in range(1, H):
                    load(base + 2 * B + b, b % 2, b, C_G + FIRST_GATE * P)
                load_weights(k, sp, base + 5 * H, 0, then)
                sp.wait_ge(s["exps_in"], 1)
                sp.dma_start(io["m_prompt"].rearrange("l b h -> (l b) h"), m_prev[0:1, TB, :]).then_inc(s["m_out"], 16)
                sp.wait_ge(s["m_out"], 16)

            @block.gpsimd
            def _(pool):
                k.clear_semaphores(pool, old_sems)
                split_ahead(k, pool, base, 5 * H)

            @block.tensor
            def _(pe):
                def step(gi, g, n, par, pair, b, q):
                    for c in range(NCH):
                        project_chunk(k, pe, n, par, c, k.x_hi, k.x_lo)
                        if gi < GATES and par == 0 and c == 1:
                            pe.wait_ge(s["own_ready"], q + 1)
                            pe.wait_ge(s["multiplied"], q * PAGES + RING)
                            nc.tensor.matmul(q_row[:, :], k.ones[0:B, :], q_own[:, :], start=True, stop=True)\
                                .then_inc(s["rows_ready"], 1)
                        if gi == MO and c != 1:
                            t = b * 2 + c // 2
                            pe.wait_ge(s["spread_ready"], t + 1)
                            pe.wait_ge(s["g_rows_read"], t + 1)
                            nc.tensor.matmul(g_rows[:, c // 2, :], k.ones[:, :], spread[:, c // 2, :, :],
                                             start=True, stop=True).then_inc(s["g_rows_ready"], 1)

                def after(gi):
                    if gi == MQ:
                        pe.wait_ge(s["w_ready"], 1)
                        for c in range(NCH):
                            cols = slice(c * CW, (c + 1) * CW)
                            if c:
                                pe.wait_ge(s["if_read"], c)
                            for i in range(KD):
                                nc.tensor.matmul(by_gate[:, 0:CW], w_if2[:, i, :, :], k.x_hi[:, i, cols],
                                                 start=(i == 0), stop=False, skip_group_check=True)
                                mm = nc.tensor.matmul(by_gate[0:2 * H, 0:CW], w_if2[:, i, 0, :], k.x_lo[:, i, cols],
                                                      start=False, stop=(i == KD - 1), skip_group_check=True)
                            mm.then_inc(s["if_ready"], 1)
                        pe.wait_ge(s["if_read"], NCH)
                        for tb in range(TB + 1):
                            m = P if tb < TB else B
                            mm = nc.tensor.matmul(gp[0:m, tb, :], if_rows[:, tb * P:tb * P + m], k.two_idents[:, :],
                                                  start=True, stop=True)
                        mm.then_inc(s["projected"], 1)
                    if gi == MV:
                        pe.wait_ge(s["log_f_ready"], 1)
                        lf = log_f[:, :, :].rearrange("p c h -> p (c h)")
                        nc.tensor.matmul(sums[:, 0:GATE_COLS], k.sum_to[:, :], lf, start=True, stop=True)
                        nc.tensor.matmul(sums[:, GATE_COLS:2 * GATE_COLS], k.ones[:, :], lf, start=True, stop=True)\
                            .then_inc(s["summed"], 1)
                    if gi == GATES:
                        pe.wait_ge(s["sp_ready"], 1)
                        nc.tensor.matmul(sums[:, 0:N], k.neg_from[:, :], sp_[:, :, :, :].rearrange(flat), start=True, stop=False)
                        nc.tensor.matmul(sums[:, 0:N], k.neg_ones[:, :], later[:, :, :, :].rearrange(flat),
                                         start=False, stop=True).then_inc(s["z_summed"], 1)

                walk(pe, step, after)

            @block.scalar
            def _(act):
                def step(gi, g, n, par, pair, b, q):
                    to_dram = gi == GATES
                    if to_dram:
                        act.wait_ge(gate_sent[par], (b - par) * 8)
                    out = gate_out[:, par:par + 1, :] if to_dram else g["out"](b)
                    for c in range(NCH):
                        acc_wait(k, act, n, c)
                        nc.scalar.activation(out[:, :, c * CW:(c + 1) * CW], k.acc[:, c:c + 1, 0:CW],
                                             g["func"], scale=g["scale"]).then_inc(k.acc_free, 1)
                    if to_dram:
                        act.wait_ge(k.acc_free, (n + 1) * NCH + NCH)
                        act.dma_start(k.gates[:, bass.ds(b + FIRST_GATE, 1), :], out).then_inc(gate_sent[par], 16)

                def log_of(t):
                    for func, scale, bias in ((ACT.Abs, 1.0, 0.0), (ACT.Exp, -1.0, 0.0), (ACT.Ln, 1.0, 1.0)):
                        op = nc.scalar.activation(t[1], t[0] if func == ACT.Abs else t[1], func, scale=scale, bias=bias)
                        if func != ACT.Ln:
                            act.drain()
                    return op

                def after(gi):
                    if gi == MQ:
                        for c in range(NCH):
                            act.wait_ge(s["if_ready"], c + 1)
                            nc.scalar.activation(if_rows[:, c * CW:(c + 1) * CW], by_gate[:, 0:CW], ACT.Copy)\
                              .then_inc(s["if_read"], 1)
                    if gi == MK:
                        act.preload_act_table_set(EXP_LN)
                        act.wait_ge(s["raw_ready"], 1)
                        log_of((raw[:, 0:TB, H:2 * H], f_abs[:, :, :])).then_inc(s["log_ready"], 1)
                    if gi == MO:
                        act.preload_act_table_set(EXP_LN)
                        act.wait_ge(s["exps_in"], 1)
                        nc.scalar.activation(k.exps[:, :, :, :], k.exps[:, :, :, :], ACT.Exp)
                        act.wait_ge(s["z_ready"], 1)
                        log_of((z[:, :, :, :].rearrange(flat), z_abs[:, :, :, :].rearrange(flat))).then_inc(s["z_log_ready"], 1)
                    if gi == GATES:
                        act.wait_ge(s["arg_ready"], 1)
                        nc.scalar.activation(k.dec_prob[:, :, :, :].rearrange(flat), z_abs[:, :, :, :].rearrange(flat), ACT.Exp)

                walk(act, step, after)
                for par in range(2):
                    act.wait_ge(gate_sent[par], H // 2 * 16)

            @block.vector
            def _(dve):
                dve.sem_inc(s["multiplied"], RING)
                dve.sem_inc(s["g_rows_read"], 2)
                dve.wait_ge(s["w_in"], 16)
                nc.vector.tensor_copy(w_if2[:, :, 0, :], w_if[:, :, :])
                nc.vector.memset(m_prev[:, 0, :], 0.0)
                dve.drain()
                nc.vector.tensor_tensor(w_if2[:, :, 1, :], w_if[:, :, :], w_if2[:, :, 0, :].bitcast(F32),
                                        ALU.subtract).then_inc(s["w_ready"], 1)

                def spread_g(t, par):
                    nc.vector.tensor_tensor(spread[:, par, :, :], k.ident[:, :].unsqueeze(1).to_broadcast([P, H, P]),
                                            k.g_col[:, bass.ds(t, 1), :].squeeze(1).unsqueeze(2).to_broadcast([P, H, P]),
                                            ALU.mult).then_inc(s["spread_ready"], 1)

                def maxima(t, par):
                    dve.wait_ge(s["g_rows_ready"], t + 1)
                    rows = g_rows[:, par, :].rearrange("p (h t) -> p h t", h=H)
                    nc.vector.tensor_reduce(g_max[:, bass.ds(t, 1), :].squeeze(1), rows, AX.X, ALU.max)
                    for h in range(H):
                        dve.drain()
                        nc.vector.tensor_tensor_reduce(junk[:, :], rows[:, h, :], k.late_neg[:, :], 1.0, -3.0e38,
                                                       ALU.add, ALU.max, k.mu[:, t, h:h + 1])
                    dve.drain().then_inc(s["g_rows_read"], 1)

                def step(gi, g, n, par, pair, b, q):
                    if gi == GATES:
                        return
                    if par == 0:
                        dve.wait_ge(s["rows_ready"], q)
                        nc.vector.tensor_scalar(q_own[:, :], k.q_tok[:, :], k.ident[0:B, bass.ds(q, 1)], None, ALU.mult)\
                          .then_inc(s["own_ready"], 1)
                    if gi == MO:
                        for e in range(2):
                            spread_g(b * 2 + e, e)
                    if par == 0:
                        dve.wait_ge(s["rows_ready"], q + 1)
                    for j in range(HALF):
                        p_ = par * HALF + j
                        dve.wait_ge(landed[p_ % RING], q * (PAGES // RING * 16) + (p_ // RING + 1) * 16)
                        dve.wait_ge(s["reduced"], q * PAGES + max(p_ - 1, 0))
                        nc.vector.tensor_tensor(prod[:, p_ % 2, :], page[:, p_ % RING, :], q_row[:, :],
                                                ALU.mult).then_inc(s["multiplied"], 1)
                        dve.wait_ge(s["multiplied"], q * PAGES + p_ + 1 + RING)
                        nc.vector.tensor_reduce(z[:, bass.ds(q, 1), p_, :].squeeze(1),
                                                prod[:, p_ % 2, :].rearrange("p (h d) -> p h d", h=H), AX.X, ALU.add)\
                          .then_inc(s["reduced"], 1)
                        if gi == MO and j % 2 == 1:
                            maxima(b * 2 + j // 2, j // 2)

                def after(gi):
                    if gi == MK:
                        dve.wait_ge(s["projected"], 1)
                        nc.vector.tensor_tensor(raw[:, 0:TB, :], gp[:, 0:TB, :],
                                                k.b_if[:, :].unsqueeze(1).to_broadcast([P, TB, 2 * H]), ALU.add)
                        nc.vector.tensor_tensor(k.gates_dec[:, :], gp[0:B, TB, :], k.b_if[0:B, :], ALU.add)
                        dve.drain().then_inc(s["raw_ready"], 1)
                        nc.vector.tensor_scalar(total[:, :, :], raw[:, 0:TB, H:2 * H], -1.0, 0.0, ALU.mult, ALU.max)
                        dve.drain()
                        dve.wait_ge(s["log_ready"], 1)
                        nc.vector.scalar_tensor_tensor(out=log_f[:, :, :], in0=total[:, :, :], scalar=-1.0, in1=f_abs[:, :, :],
                                                       op0=ALU.mult, op1=ALU.subtract).then_inc(s["log_f_ready"], 1)
                    if gi == MV:
                        dve.wait_ge(s["summed"], 1)
                        dve.wait_ge(s["log_f_ready"], 1)
                        nc.vector.tensor_copy(b_sum[:, :, :], sums[:, 0:GATE_COLS].rearrange("p (c h) -> p c h", h=H))
                        nc.vector.tensor_copy(total[:, :, :], sums[:, GATE_COLS:2 * GATE_COLS].rearrange("p (c h) -> p c h", h=H))
                        dve.drain()
                        nc.vector.tensor_tensor(k.g_col[:, :, :], raw[:, 0:TB, 0:H], b_sum[:, :, :], ALU.subtract)
                        dve.drain()
                    if gi == MO:
                        for c in range(TB):
                            nc.vector.tensor_tensor(mu_last[:, c, :], m_prev[:, c, :], g_max[:, c, :], ALU.max)
                            dve.drain()
                            nc.vector.tensor_tensor(m_prev[:, c + 1, :], total[:, c, :], mu_last[:, c, :], ALU.add)
                            dve.drain()
                        nc.vector.tensor_tensor(k.mu[:, :, :], k.mu[:, :, :], m_prev[:, 0:TB, :], ALU.max)
                        dve.drain()
                        nc.vector.tensor_tensor(k.exps[:, E_STATE, :, :], m_prev[:, 0:TB, :], k.mu[:, :, :], ALU.subtract)
                        nc.vector.scalar_tensor_tensor(out=k.exps[:, E_NEGM, :, :], in0=b_sum[:, :, :], scalar=-1.0,
                                                       in1=k.mu[:, :, :], op0=ALU.mult, op1=ALU.subtract)
                        nc.vector.tensor_tensor(k.exps[:, E_KEY, :, :], k.g_col[:, :, :], mu_last[:, :, :], ALU.subtract)
                        nc.vector.tensor_tensor(k.exps[:, E_DECAY, :, :], m_prev[:, 0:TB, :], mu_last[:, :, :], ALU.subtract)
                        dve.drain().then_inc(s["exps_in"], 1)
                        dve.wait_ge(s["reduced"], B * PAGES)
                        bias = k.b_sb[:, :].unsqueeze(1).to_broadcast([P, B * PAGES, H])
                        zf = z[:, :, :, :].rearrange("p b g h -> p (b g) h")
                        nc.vector.tensor_tensor(zf, zf, bias, ALU.add).then_inc(s["z_ready"], 1)
                        dve.wait_ge(s["z_log_ready"], 1)
                        dve.wait_ge(s["z_ready"], 1)
                        fz, fs, fa = (t[:, :, :, :].rearrange(flat) for t in (z, sp_, z_abs))
                        nc.vector.scalar_tensor_tensor(out=fs, in0=fz, scalar=0.0, in1=fa, op0=ALU.max, op1=ALU.add)
                        nc.vector.memset(later[:, :, PAGES - 1, :], 0.0)
                        for g in range(PAGES - 2, -1, -1):
                            dve.drain()
                            nc.vector.tensor_tensor(later[:, :, g, :], later[:, :, g + 1, :], sp_[:, :, g + 1, :], ALU.add)
                        dve.drain().then_inc(s["sp_ready"], 1)
                        dve.wait_ge(s["z_summed"], 1)
                        nc.vector.tensor_tensor(fa, fz, sums[:, 0:N], ALU.add).then_inc(s["arg_ready"], 1)

                walk(dve, step, after, straight=(MO,))
    k.blocks = base + 5 * H
    k.release_cleared()


def load_pages(k, sp, table, q, half, cache, page, used, landed):
    for j in range(PAGES // 2):
        p_ = half * (PAGES // 2) + j
        number = sp.value_load(table[0:1, bass.ds(q * PAGES + p_, 1)], min_val=0, max_val=N_PHYS - 1)
        sp.wait_ge(used, q * PAGES + p_ + 1)
        sp.dma_start(page[:, p_ % RING, :], cache[0, bass.ds(number, 1), :, :, :].rearrange("a t h d -> (a t) (h d)"))\
          .then_inc(landed[p_ % RING], 16)


def mlstm_prompt(k, m_T, then):
    nc, io = k.nc, k.io
    base = k.blocks
    NB, FIRST_GATE = 2, H
    SLOTS = NB * NCH
    S_, M_, K_, V_, X_ = range(5)
    INTER, INTRA, STATE = (X_, K_), (M_, V_), (S_, X_)
    TURNED = K_
    w_in = io["w_in"].rearrange("l (k p) n -> p (l k) n", p=P)
    V1 = P + 1
    with ExitStack() as ctx:
        qkv = k.sb(ctx, "qkv", [P, 3, H, P])
        spread = k.sb(ctx, "mu_spread", [P, H, P])
        expo = k.sb(ctx, "expo", [P, H, P])
        w_T = k.sb(ctx, "w_T", [P, H, P])
        v_one = k.sb(ctx, "v_one", [P, H, V1])
        k_w = k.sb(ctx, "k_weighed", [P, H, P])
        inter = k.sb(ctx, "inter", [P, H, V1])
        num = k.sb(ctx, "num", [P, H, V1])
        den = k.sb(ctx, "den", [P, 3, H])
        h_tok = k.sb(ctx, "h_tok", [P, H, P])
        y_m = k.sb(ctx, "y_m", [P, H, P])
        state = k.sb(ctx, "state", [P, H, V1])
        gate_out = k.sb(ctx, "gate_out", [P, NB, TT])
        table = k.sb(ctx, "v_pages", [1, B * PAGES], I32)
        page = k.sb(ctx, "v_page", [P, RING, W])
        y_dec = k.sb(ctx, "y_dec_s", [P, H, B])
        v_sum = k.sb(ctx, "v_sum", [P, H, P])
        y = k.acc[:, 0, 512 - B * H:512].rearrange("p (b h) -> p b h", h=H)
        q = k.ps(ctx, "ml_ps", [P, 5, 512])
        s = {n: k.sem(ctx, "ml_" + n) for n in (
            "staged", "spread_ready", "pe1", "args_ready", "expo_ready", "weights_ready", "v_ready", "kw_ready", "pe2",
            "inter_ready", "num_ready", "h_ready", "pe3", "state_ready", "y_ready", "y_sent", "state_out",
            "table_in", "page_used", "weighed", "dec_summed", "dec_done", "dec_read", "dec_out")}
        landed = [k.sem(ctx, f"v_page_landed{i}") for i in range(RING)]
        gate_sent = [k.sem(ctx, f"gate_sent{b}") for b in range(NB)]

        def bank(i):
            return q[:, i, :].rearrange("p (h t) -> p h t", h=H)

        def pair(i):
            return q[:, i, 0:2 * V1].rearrange("p (h t) -> p h t", h=2)

        with nc.Block() as block:
            @block.sync
            def _(sp):
                sp.dma_start(table[:, :], io["page_table"].rearrange("b g -> (b g)").unsqueeze(0)).then_inc(s["table_in"], 16)
                sp.wait_ge(s["table_in"], 16)
                def pages(c, half):
                    load_pages(k, sp, table, c, half, io["cache_v"], page, s["page_used"], landed)

                def load(c, b, par):
                    load_weights(k, sp, base + c * NB + b, par, w_in[:, :, bass.ds((c * NB + b + FIRST_GATE) * P + C_G, P)])

                with sp.Fori(0, TB - 1) as c:
                    load(c, 1, 1)
                    pages(c, 0)
                    load(c, 2, 0)
                    pages(c, 1)
                load(TB - 1, 1, 1)
                pages(TB - 1, 0)
                load_weights(k, sp, base + TB * NB, 0, then, H)
                pages(TB - 1, 1)
                sp.wait_ge(s["dec_read"], 1)
                sp.dma_start(k.branch[2, :, :, T:TT], y_dec[:, :, :]).then_inc(s["dec_out"], 16)
                sp.wait_ge(s["dec_out"], 16)
                sp.wait_ge(s["state_ready"], TB + 1)
                sp.dma_start(io["C_prompt"][0, 0].rearrange("h d e -> d h e"), state[:, :, 0:P]).then_inc(s["state_out"], 16)
                sp.dma_start(io["n_prompt"][0, 0].rearrange("h d -> d h").unsqueeze(2), state[:, :, P:V1],
                             allow_slow_non_contiguous=True).then_inc(s["state_out"], 16)
                sp.wait_ge(s["state_out"], 32)

            @block.gpsimd
            def _(pool):
                split_ahead(k, pool, base, TB * NB, then_kb=H)

            @block.tensor
            def _(pe):
                def turn_and_score(c):
                    pe.wait_ge(s["staged"], c + 1)
                    pe.wait_ge(s["state_ready"], c + 1)
                    pe.wait_ge(s["y_ready"], c)
                    pe.wait_ge(s["num_ready"], c)
                    for h in range(H):
                        nc.tensor.matmul(bank(S_)[:, h, :], qkv[:, 1, h, :], qkv[:, 0, h, :], start=True, stop=True)
                    pe.wait_ge(s["spread_ready"], c + 1)
                    nc.tensor.matmul(q[:, M_, :], k.ones[:, :], spread[:, :, :], start=True, stop=True)
                    for h in range(H):
                        nc.tensor.transpose(bank(K_)[:, h, :], qkv[:, 1, h, :], k.ident[:, :])
                    for h in range(H):
                        tr = nc.tensor.transpose(bank(V_)[:, h, :], qkv[:, 2, h, :], k.ident[:, :])
                    tr.then_inc(s["pe1"], 1)

                def outputs(c):
                    pe.wait_ge(s["kw_ready"], c + 1)
                    for h in range(H):
                        nc.tensor.matmul(pair(INTER[h // 2])[:, h % 2, :], qkv[:, 0, h, :], state[:, h, :],
                                         start=True, stop=True)
                    pe.wait_ge(s["v_ready"], c + 1)
                    pe.wait_ge(s["weights_ready"], c + 1)
                    for h in range(H):
                        mm = nc.tensor.matmul(pair(INTRA[h // 2])[:, h % 2, :], w_T[:, h, :], v_one[:, h, :],
                                              start=True, stop=True)
                    mm.then_inc(s["pe2"], 1)

                def new_state(c):
                    pe.wait_ge(s["inter_ready"], c + 1)
                    for h in range(H):
                        nc.tensor.matmul(pair(STATE[h // 2])[:, h % 2, :], k_w[:, h, :], v_one[:, h, :],
                                         start=True, stop=True)
                    pe.wait_ge(s["h_ready"], c + 1)
                    for h in range(H):
                        tr = nc.tensor.transpose(bank(TURNED)[:, h, :], h_tok[:, h, :], k.ident[:, :])
                    tr.then_inc(s["pe3"], 1)

                def sum_values(c):
                    pe.wait_ge(s["weighed"], (c + 1) * PAGES)
                    pe.wait_ge(k.acc_free, (base + c * NB + 1) * NCH + 1)
                    for h in range(H):
                        mm = nc.tensor.matmul(y[:, bass.ds(c, 1), h], v_sum[:, h, :], k.ones[:, 0:1], start=True, stop=True)
                    mm.then_inc(s["dec_summed"], 1)

                with pe.Fori(0, TB) as c:
                    for slot in range(SLOTS):
                        b, ch = divmod(slot, NCH)
                        if slot == NCH:
                            sum_values(c)
                        project_chunk(k, pe, base + c * NB + b, b, ch, k.x_hi, k.x_lo)
                        if slot == 0:
                            turn_and_score(c)
                        if slot == 2:
                            outputs(c)
                        if slot == 4:
                            new_state(c)
                pe.drain().then_inc(s["dec_done"], 1)

            @block.scalar
            def _(act):
                act.preload_act_table_set(EXP_LN)
                with act.Fori(0, TB) as c:
                    act.wait_ge(s["pe2"], c)
                    nc.scalar.activation(qkv[:, :, :, :].rearrange("p a h t -> p (a h) t"),
                                         m_T[:, 0:3 * H, bass.ds(c * P, P)], ACT.Copy).then_inc(s["staged"], 1)
                    for slot in range(SLOTS):
                        b, ch = divmod(slot, NCH)
                        if ch == 0:
                            act.wait_ge(gate_sent[b], c * 16)
                        acc_wait(k, act, base + c * NB + b, ch)
                        nc.scalar.activation(gate_out[:, b, ch * CW:(ch + 1) * CW], k.acc[:, ch, 0:CW], ACT.Copy)\
                          .then_inc(k.acc_free, 1)
                        if ch == NCH - 1:
                            act.wait_ge(k.acc_free, (base + c * NB + b + 1) * NCH + NCH)
                            act.dma_start(k.gates[:, bass.ds(c * NB + b + FIRST_GATE, 1), :],
                                          gate_out[:, b:b + 1, :]).then_inc(gate_sent[b], 16)
                        if slot == 0:
                            act.wait_ge(s["pe1"], c + 1)
                            act.wait_ge(s["pe3"], c)
                            nc.scalar.activation(v_one[:, :, 0:P], bank(V_), ACT.Copy).then_inc(s["v_ready"], 1)
                            for h in range(H):
                                op = nc.scalar.activation(k_w[:, h:h + 1, :], bank(K_)[:, h:h + 1, :], ACT.Copy,
                                                          scale=k.exps[:, E_KEY, bass.ds(c, 1), h])
                            op.then_inc(s["kw_ready"], 1)
                            act.wait_ge(s["args_ready"], c + 1)
                            nc.scalar.activation(expo[:, :, :], expo[:, :, :], ACT.Exp, scale=-1.0)\
                              .then_inc(s["expo_ready"], 1)
                        if slot == 2:
                            act.wait_ge(s["pe2"], c + 1)
                            act.wait_ge(s["num_ready"], c)
                            for h in range(H):
                                op = nc.scalar.activation(inter[:, h, :], pair(INTER[h // 2])[:, h % 2, :], ACT.Copy,
                                                          scale=k.exps[:, E_STATE, bass.ds(c, 1), h])
                            op.then_inc(s["inter_ready"], 1)
                    act.wait_ge(s["y_ready"], c + 1)
                    act.dma_start(k.branch[0, :, :, bass.ds(c * P, P)], y_m[:, :, :]).then_inc(s["y_sent"], 16)
                act.wait_ge(s["y_sent"], TB * 16)
                for b in range(NB):
                    act.wait_ge(gate_sent[b], TB * 16)

            @block.vector
            def _(dve):
                nc.vector.memset(state[:, :, :], 0.0)
                nc.vector.memset(v_one[:, :, P:V1], 1.0)
                dve.drain().then_inc(s["state_ready"], 1)
                dve.sem_inc(s["page_used"], RING)

                def weigh_pages(c, half):
                    for g in range(half * (PAGES // 2), (half + 1) * (PAGES // 2)):
                        dve.wait_ge(landed[g % RING], c * (PAGES // RING * 16) + (g // RING + 1) * 16)
                        if g == 0:
                            dve.wait_ge(s["dec_summed"], c)
                        for h in range(H):
                            values = page[:, g % RING, h * P:(h + 1) * P].unsqueeze(1)
                            weight = k.dec_prob[:, bass.ds(c, 1), g, h]
                            if g == 0:
                                nc.vector.tensor_scalar(v_sum[:, h:h + 1, :], values, weight, None, ALU.mult)
                            else:
                                nc.vector.scalar_tensor_tensor(out=v_sum[:, h:h + 1, :], in0=values, scalar=weight,
                                                               in1=v_sum[:, h:h + 1, :], op0=ALU.mult, op1=ALU.add)
                        dve.drain().then_inc(s["page_used"], 1)
                    dve.sem_inc(s["weighed"], PAGES // 2)

                with dve.Fori(0, TB) as c:
                    dve.wait_ge(s["pe1"], c)
                    nc.vector.tensor_tensor(spread[:, :, :], k.ident[:, :].unsqueeze(1).to_broadcast([P, H, P]),
                                            k.mu[:, bass.ds(c, 1), :].squeeze(1).unsqueeze(2).to_broadcast([P, H, P]),
                                            ALU.mult).then_inc(s["spread_ready"], 1)
                    weigh_pages(c, 0)
                    dve.wait_ge(s["pe1"], c + 1)
                    dve.wait_ge(s["expo_ready"], c)
                    for h in range(H):
                        op = nc.vector.scalar_tensor_tensor(out=expo[:, h, :], in0=bank(M_)[:, h, :],
                                                            scalar=k.g_col[:, bass.ds(c, 1), h], in1=k.late_big[:, :],
                                                            op0=ALU.subtract, op1=ALU.max)
                    op.then_inc(s["args_ready"], 1)
                    dve.wait_ge(s["expo_ready"], c + 1)
                    dve.wait_ge(s["pe2"], c)
                    nc.vector.tensor_tensor(w_T[:, :, :], expo[:, :, :], bank(S_), ALU.mult).then_inc(s["weights_ready"], 1)
                    weigh_pages(c, 1)
                    dve.wait_ge(s["inter_ready"], c + 1)
                    for i in range(2):
                        op = nc.vector.tensor_tensor(num[:, 2 * i:2 * i + 2, :], inter[:, 2 * i:2 * i + 2, :],
                                                     pair(INTRA[i]), ALU.add)
                    dve.drain().then_inc(s["num_ready"], 1)
                    nc.vector.scalar_tensor_tensor(out=den[:, 0, :], in0=num[:, :, P], scalar=-1.0, in1=num[:, :, P],
                                                   op0=ALU.mult, op1=ALU.max)
                    dve.drain()
                    nc.vector.tensor_tensor(den[:, 1, :], den[:, 0, :], k.exps[:, E_NEGM, bass.ds(c, 1), :].squeeze(1), ALU.max)
                    dve.drain()
                    nc.vector.reciprocal(den[:, 2, :], den[:, 1, :])
                    dve.drain()
                    dve.wait_ge(s["pe3"], c)
                    nc.vector.tensor_tensor(h_tok[:, :, :], num[:, :, 0:P],
                                            den[:, 2, :].unsqueeze(2).to_broadcast([P, H, P]), ALU.mult)\
                      .then_inc(s["h_ready"], 1)
                    dve.wait_ge(s["pe3"], c + 1)
                    for h in range(H):
                        op = nc.vector.scalar_tensor_tensor(out=state[:, h, :], in0=state[:, h, :],
                                                            scalar=k.exps[:, E_DECAY, bass.ds(c, 1), h],
                                                            in1=pair(STATE[h // 2])[:, h % 2, :], op0=ALU.mult, op1=ALU.add)
                    op.then_inc(s["state_ready"], 1)
                    dve.wait_ge(s["y_sent"], c * 16)
                    nc.vector.tensor_tensor(y_m[:, :, :], bank(TURNED), m_T[:, 3 * H:4 * H, bass.ds(c * P, P)],
                                            ALU.mult).then_inc(s["y_ready"], 1)
                dve.wait_ge(s["dec_done"], 1)
                dve.wait_ge(k.acc_free, (base + TB * NB) * NCH + NCH)
                nc.vector.tensor_copy(y_dec[:, :, :], y.rearrange("p b h -> p h b")).then_inc(s["dec_read"], 1)
    k.blocks = base + TB * NB


def mlstm_decode(k, m_T):
    nc, io = k.nc, k.io
    N = B * H
    dec = slice(T, TT)
    with ExitStack() as ctx:
        spread = k.sb(ctx, "dec_spread", [B, B, 2 * H])
        m_old = k.sb(ctx, "m_old", [P, N])
        gate = k.sb(ctx, "dec_gate", [P, B, 2 * H])
        f_abs = k.sb(ctx, "dec_f_abs", [P, B, H])
        f_pos = k.sb(ctx, "dec_f_pos", [P, B, H])
        m_new = k.sb(ctx, "m_new", [P, B, H])
        terms = k.sb(ctx, "dec_terms", [P, 3, B, H])
        kv = k.sb(ctx, "dec_kv", [B, 2, H, P])
        own = k.sb(ctx, "dec_own", [B, B, H])
        v_own = k.sb(ctx, "dec_v_own", [B, 2, B, P])
        old = k.sb(ctx, "C_old", [P, 2, B, P])
        new = k.sb(ctx, "C_new", [P, 2, B, P])
        n_new = k.sb(ctx, "n_new", [P, B, H])
        n_add = k.sb(ctx, "n_add", [P, B, H])
        n_rows = k.sb(ctx, "n_new_rows", [N, P])
        dot = k.sb(ctx, "dec_dot", [P, B, H])
        den = k.sb(ctx, "dec_den", [P, B, H])
        y_d = k.sb(ctx, "y_dec", [P, H, B])
        reps = k.ps(ctx, "dec_reps", [P, 512])
        turned = k.ps(ctx, "dec_turned", [B, 2, 512])
        outer = k.ps(ctx, "dec_outer", [P, B, P])
        s = {n: k.sem(ctx, "md_" + n) for n in (
            "m_in", "spread_ready", "gates_ready", "gate_ready", "log_ready", "terms_in", "terms_ready", "kv_turned",
            "kv_ready", "own_ready", "outer_ready", "new_ready", "dot_ready", "dots", "nums", "n_ready", "n_turned",
            "n_rows_ready", "y_ready", "sent")}
        old_in = [k.sem(ctx, f"C_old_in{i}") for i in range(2)]
        new_out = [k.sem(ctx, f"C_new_out{i}") for i in range(2)]
        qd = m_T[:, 0:H, dec]
        flat = "p b h -> p (b h)"
        with nc.Block() as block:
            @block.sync
            def _(sp):
                sp.dma_start(m_old[:, :], io["state_mlstm_m"].rearrange("l b h -> l (b h)").to_broadcast([P, N]),
                             allow_slow_non_contiguous=True).then_inc(s["m_in"], 16)
                for h in range(H):
                    if h >= 2:
                        sp.wait_ge(s["new_ready"], h - 1)
                    sp.dma_start(old[:, h % 2, :, :], io["state_mlstm_C"][0, :, h].rearrange("b d e -> d b e"))\
                      .then_inc(old_in[h % 2], 16)
                for h in range(H):
                    sp.wait_ge(s["new_ready"], h + 1)
                    sp.dma_start(io["C_sample"][0, :, h].rearrange("b d e -> d b e"), new[:, h % 2, :, :])\
                      .then_inc(new_out[h % 2], 16)
                sp.wait_ge(s["terms_in"], 1)
                sp.dma_start(io["m_sample"].rearrange("l b h -> l (b h)"), m_new[0:1, :, :].rearrange(flat)).then_inc(s["sent"], 16)
                sp.wait_ge(s["n_rows_ready"], 1)
                sp.dma_start(io["n_sample"].rearrange("l b h d -> (l b h) d"), n_rows[:, :]).then_inc(s["sent"], 16)
                sp.wait_ge(s["y_ready"], 1)
                sp.dma_start(k.branch[0, :, :, dec], y_d[:, :, :]).then_inc(s["sent"], 16)
                sp.wait_ge(s["sent"], 48)
                for i in range(2):
                    sp.wait_ge(new_out[i], 32)

            @block.tensor
            def _(pe):
                for a in range(2):
                    for h in range(H):
                        tr = nc.tensor.transpose(turned[:, a, h * P:(h + 1) * P], m_T[:, (a + 1) * H + h, dec], k.ident[:, :])
                tr.then_inc(s["kv_turned"], 1)
                pe.wait_ge(s["spread_ready"], 1)
                nc.tensor.matmul(reps[:, 0:B * 2 * H], k.ones[0:B, :], spread[:, :, :].rearrange("p b g -> p (b g)"),
                                 start=True, stop=True).then_inc(s["gates_ready"], 1)
                for h in range(H):
                    pe.wait_ge(s["own_ready"], h + 1)
                    if h:
                        pe.wait_ge(s["new_ready"], h)
                    for half in range(2):
                        mm = nc.tensor.matmul(outer[:, 4 * half:4 * half + 4, :], kv[:, 0, h, :],
                                              v_own[:, h % 2, 4 * half:4 * half + 4, :], start=True, stop=True)
                    mm.then_inc(s["outer_ready"], 1)
                    pe.wait_ge(s["new_ready"], h + 1)
                    for b in range(B):
                        mm = nc.tensor.matmul(reps[:, 128 + h * B + b:129 + h * B + b], new[:, h % 2, b, :],
                                              m_T[:, h, T + b:T + b + 1], start=True, stop=True)
                    mm.then_inc(s["nums"], 1)
                pe.wait_ge(s["dot_ready"], 1)
                nc.tensor.matmul(reps[:, 256:256 + N], k.ones[:, :], dot[:, :, :].rearrange(flat), start=True, stop=True)\
                    .then_inc(s["dots"], 1)
                pe.wait_ge(s["kv_ready"], 1)
                nc.tensor.transpose(outer[0:N, 0, :], n_new[:, :, :].rearrange(flat),
                                    k.ident[:, :]).then_inc(s["n_turned"], 1)

            @block.scalar
            def _(act):
                act.preload_act_table_set(EXP_LN)
                act.wait_ge(s["gate_ready"], 1)
                nc.scalar.activation(f_abs[:, :, :], gate[:, :, H:2 * H], ACT.Abs)
                act.drain()
                nc.scalar.activation(f_abs[:, :, :], f_abs[:, :, :], ACT.Exp, scale=-1.0)
                act.drain()
                nc.scalar.activation(f_abs[:, :, :], f_abs[:, :, :], ACT.Ln, bias=1.0).then_inc(s["log_ready"], 1)
                act.wait_ge(s["terms_in"], 1)
                nc.scalar.activation(terms[:, :, :, :], terms[:, :, :, :], ACT.Exp).then_inc(s["terms_ready"], 1)

            @block.vector
            def _(dve):
                nc.vector.tensor_tensor(spread[:, :, :], k.ident[0:B, 0:B].unsqueeze(2).to_broadcast([B, B, 2 * H]),
                                        k.gates_dec[:, :].unsqueeze(1).to_broadcast([B, B, 2 * H]),
                                        ALU.mult).then_inc(s["spread_ready"], 1)
                dve.wait_ge(s["kv_turned"], 1)
                nc.vector.tensor_copy(kv[:, :, :, :].rearrange("p a h d -> p a (h d)"), turned[:, :, :]).then_inc(s["kv_ready"], 1)
                dve.wait_ge(s["gates_ready"], 1)
                nc.vector.tensor_copy(gate[:, :, :].rearrange("p b g -> p (b g)"), reps[:, 0:B * 2 * H])\
                  .then_inc(s["gate_ready"], 1)
                dve.wait_ge(s["gate_ready"], 1)
                nc.vector.tensor_scalar(f_pos[:, :, :], gate[:, :, H:2 * H], -1.0, 0.0, ALU.mult, ALU.max)
                dve.drain()
                dve.wait_ge(s["log_ready"], 1)
                nc.vector.scalar_tensor_tensor(out=f_pos[:, :, :], in0=f_pos[:, :, :], scalar=-1.0, in1=f_abs[:, :, :],
                                               op0=ALU.mult, op1=ALU.subtract)
                dve.drain()
                dve.wait_ge(s["m_in"], 16)
                nc.vector.tensor_tensor(f_pos[:, :, :], f_pos[:, :, :], m_old[:, :].rearrange("p (b h) -> p b h", h=H), ALU.add)
                dve.drain()
                nc.vector.tensor_tensor(m_new[:, :, :], f_pos[:, :, :], gate[:, :, 0:H], ALU.max)
                dve.drain()
                nc.vector.tensor_tensor(terms[:, 0, :, :], f_pos[:, :, :], m_new[:, :, :], ALU.subtract)
                nc.vector.tensor_tensor(terms[:, 1, :, :], gate[:, :, 0:H], m_new[:, :, :], ALU.subtract)
                nc.vector.tensor_scalar(terms[:, 2, :, :], m_new[:, :, :], -1.0, None, ALU.mult)
                dve.drain().then_inc(s["terms_in"], 1)
                dve.wait_ge(s["terms_ready"], 1)
                nc.vector.tensor_tensor(own[:, :, :], k.ident[0:B, 0:B].unsqueeze(2).to_broadcast([B, B, H]),
                                        terms[0:B, 1, :, :], ALU.mult)
                nc.vector.tensor_tensor(n_new[:, :, :], k.n_old[:, :].rearrange("p (b h) -> p b h", h=H), terms[:, 0, :, :], ALU.mult)
                nc.vector.tensor_tensor(n_add[:, :, :], m_T[:, H:2 * H, dec].rearrange("p h b -> p b h"), terms[:, 1, :, :], ALU.mult)
                dve.drain()
                nc.vector.tensor_tensor(n_new[:, :, :], n_new[:, :, :], n_add[:, :, :], ALU.add)
                dve.drain()
                nc.vector.tensor_tensor(dot[:, :, :], n_new[:, :, :], qd.rearrange("p h b -> p b h"), ALU.mult).then_inc(s["dot_ready"], 1)
                for h in range(H):
                    nc.vector.tensor_tensor(v_own[:, h % 2, :, :], kv[:, 1, h, :].unsqueeze(1).to_broadcast([B, B, P]),
                                            own[:, :, h].unsqueeze(2).to_broadcast([B, B, P]), ALU.mult).then_inc(s["own_ready"], 1)
                    dve.wait_ge(old_in[h % 2], 16 * (h // 2 + 1))
                    nc.vector.tensor_tensor(old[:, h % 2, :, :], old[:, h % 2, :, :],
                                            terms[:, 0, :, h].unsqueeze(2).to_broadcast([P, B, P]), ALU.mult)
                    dve.drain()
                    dve.wait_ge(s["outer_ready"], h + 1)
                    if h >= 2:
                        dve.wait_ge(new_out[h % 2], 16)
                        dve.wait_ge(s["nums"], h - 1)
                    nc.vector.tensor_tensor(new[:, h % 2, :, :], old[:, h % 2, :, :], outer[:, :, :], ALU.add)\
                      .then_inc(s["new_ready"], 1)
                dve.wait_ge(s["dots"], 1)
                nc.vector.tensor_copy(den[:, :, :].rearrange(flat), reps[:, 256:256 + N])
                dve.drain()
                nc.vector.scalar_tensor_tensor(out=dot[:, :, :], in0=den[:, :, :], scalar=-1.0, in1=den[:, :, :],
                                               op0=ALU.mult, op1=ALU.max)
                dve.drain()
                nc.vector.tensor_tensor(den[:, :, :], dot[:, :, :], terms[:, 2, :, :], ALU.max)
                dve.drain()
                nc.vector.reciprocal(dot[:, :, :], den[:, :, :])
                dve.wait_ge(s["nums"], H)
                nc.vector.tensor_tensor(y_d[:, :, :], reps[:, 128:128 + N].rearrange("p (h b) -> p h b", h=H),
                                        m_T[:, 3 * H:4 * H, dec], ALU.mult)
                dve.drain()
                nc.vector.tensor_tensor(y_d[:, :, :], y_d[:, :, :], dot[:, :, :].rearrange("p b h -> p h b"), ALU.mult)\
                  .then_inc(s["y_ready"], 1)
                dve.wait_ge(s["n_turned"], 1)
                nc.vector.tensor_copy(n_rows[:, :], outer[0:N, 0, :]).then_inc(s["n_rows_ready"], 1)



def merge_branches(k, merged, then):
    nc, io = k.nc, k.io
    base = k.blocks
    NBR = 3
    with ExitStack() as ctx:
        y_raw = k.sb(ctx, "y_raw", [P, H, TT])
        y_hi = k.sb(ctx, "y_hi", [P, H, TT], F32R)
        y_lo = k.sb(ctx, "y_lo", [P, H, TT], F32R)
        gate = k.sb(ctx, "merge_gate", [P, 2, TT])
        part = k.sb(ctx, "merge_part", [P, TT])
        s = {n: k.sem(ctx, "mb_" + n) for n in ("y_in", "y_rounded", "y_split", "sigmoid", "part_ready", "merged", "hi_ready")}
        gate_in = [k.sem(ctx, f"gate_in{i}") for i in range(2)]
        with nc.Block() as block:
            @block.sync
            def _(sp):
                def weights(r):
                    return io["w_branch"][0, r].rearrange("(k p) n -> p k n", p=P)

                def load_gate(r, m, par):
                    sp.wait_ge(s["merged"], r * KD + m + 1)
                    sp.dma_start(gate[:, par:par + 1, :], k.gates[:, bass.ds(m + r * KD, 1), :]).then_inc(gate_in[par], 16)

                sp.dma_start(y_raw[:, :, :], k.branch[0]).then_inc(s["y_in"], 16)
                for r in range(NBR):
                    w = weights(r)
                    load_gate(r, 0, 0)
                    with sp.Fori(0, KD // 2 - 1) as i:
                        for m, par in ((i * 2 + 1, 1), (i * 2 + 2, 0)):
                            load_weights(k, sp, base + r * KD + m, par, w[:, :, bass.ds(m * P, P)], H)
                            load_gate(r, m, par)
                    load_weights(k, sp, base + r * KD + KD - 1, 1, w[:, :, D - P:D], H)
                    if r < NBR - 1:
                        load_weights(k, sp, base + r * KD + KD, 0, weights(r + 1)[:, :, 0:P], H)
                        sp.wait_ge(s["y_split"], r + 1)
                        sp.dma_start(y_raw[:, :, :], k.branch[r + 1]).then_inc(s["y_in"], 16)
                    else:
                        load_weights(k, sp, base + NBR * KD, 0, then)
                    load_gate(r, KD - 1, 1)

            @block.gpsimd
            def _(pool):
                split_ahead(k, pool, base, NBR * KD, kb=H)

            @block.tensor
            def _(pe):
                for r in range(NBR):
                    pe.wait_ge(s["y_split"], r + 1)
                    with pe.Fori(0, KD // 2) as i:
                        for par in range(2):
                            for c in range(NCH):
                                project_chunk(k, pe, base + r * KD + i * 2 + par, par, c, y_hi[:, :, :], y_lo[:, :, :], H)

            @block.scalar
            def _(act):
                act.preload_act_table_set("sigmoid_and_others")
                for r in range(NBR):
                    act.wait_ge(s["y_in"], 16 * (r + 1))
                    if r:
                        act.wait_ge(k.acc_ready, (base + r * KD) * NCH + 2 * NCH)
                    nc.scalar.activation(y_hi[:, :, :], y_raw[:, :, :], ACT.Copy).then_inc(s["y_rounded"], 1)
                    with act.Fori(0, KD // 2) as i:
                        for par in range(2):
                            m = i * 2 + par
                            act.wait_ge(gate_in[par], (i + r * (KD // 2) + 1) * 16)
                            nc.scalar.activation(gate[:, par, :], gate[:, par, :], ACT.Sigmoid).then_inc(s["sigmoid"], 1)
                            if r == NBR - 1:
                                act.wait_ge(s["merged"], r * KD + m + 1 + 2)
                                nc.scalar.activation(k.x_hi[:, bass.ds(m, 1), :], merged[:, bass.ds(m, 1), :], ACT.Copy)\
                                  .then_inc(s["hi_ready"], 1)

            @block.vector
            def _(dve):
                dve.sem_inc(s["merged"], 2)
                for r in range(NBR):
                    dve.wait_ge(s["y_rounded"], r + 1)
                    nc.vector.tensor_tensor(y_lo[:, :, :], y_raw[:, :, :], y_hi[:, :, :].bitcast(F32), ALU.subtract)\
                      .then_inc(s["y_split"], 1)
                    with dve.Fori(0, KD // 2) as i:
                        for par in range(2):
                            m = i * 2 + par
                            n = base + r * KD + m
                            dve.wait_ge(s["sigmoid"], r * KD + m + 1)
                            if r:
                                dve.wait_ge(s["merged"], r * KD + m + 2)
                            for c in range(NCH):
                                acc_wait(k, dve, n, c)
                                cols = slice(c * CW, (c + 1) * CW)
                                out = merged[:, bass.ds(m, 1), cols] if r == 0 else part[:, cols].unsqueeze(1)
                                nc.vector.tensor_tensor(out, k.acc[:, c:c + 1, 0:CW], gate[:, par:par + 1, cols],
                                                        ALU.mult).then_inc(k.acc_free, 1)
                            if r == 0:
                                dve.drain().then_inc(s["merged"], 1)
                            else:
                                dve.wait_ge(k.acc_free, (n + 1) * NCH + NCH)
                                nc.vector.tensor_tensor(merged[:, bass.ds(m, 1), :], merged[:, bass.ds(m, 1), :],
                                                        part[:, :].unsqueeze(1), ALU.add).then_inc(s["merged"], 1)
                            if r == NBR - 1:
                                dve.wait_ge(s["hi_ready"], m + 1)
                                nc.vector.tensor_tensor(k.x_lo[:, bass.ds(m, 1), :], merged[:, bass.ds(m, 1), :],
                                                        k.x_hi[:, bass.ds(m, 1), :].bitcast(F32), ALU.subtract)
    k.blocks = base + NBR * KD


def mix_out(k, h, then):
    nc, io = k.nc, k.io
    base = k.blocks
    w = io["w_out"][0].rearrange("(k p) n -> p k n", p=P)
    with ExitStack() as ctx:
        h_in = k.sem(ctx, "h_in")
        s = {n: k.sem(ctx, "mo_" + n) for n in SQUARES}
        squares = k.sb(ctx, "h_squares", [P, TT])[:, :]
        with nc.Block() as block:
            @block.sync
            def _(sp):
                sp.dma_start(h[:, :, :], k.x_T).then_inc(h_in, 16)
                each_ahead(sp, base, KD, lambda n, par, b, pair: load_weights(k, sp, n, par, w[:, :, bass.ds(b * P, P)]))
                load_weights(k, sp, base + KD, 0, then)

            @block.gpsimd
            def _(pool):
                split_ahead(k, pool, base, KD)

            @block.tensor
            def _(pe):
                with pe.Fori(0, KD // 2) as i:
                    for par in range(2):
                        for c in range(NCH):
                            project_chunk(k, pe, base + i * 2 + par, par, c, k.x_hi, k.x_lo)

            @block.scalar
            def _(act):
                with act.Fori(0, KD // 2) as i:
                    for par in range(2):
                        square_block(k, act, h, i * 2 + par, squares, s)

            @block.vector
            def _(dve):
                dve.wait_ge(h_in, 16)
                nc.vector.memset(k.sq_sum[:, :], 0.0)
                with dve.Fori(0, KD // 2) as i:
                    for par in range(2):
                        b = i * 2 + par
                        for c in range(NCH):
                            add_chunk(k, dve, base + b, c, h[:, bass.ds(b, 1), :])
                        dve.drain().then_inc(s["h_ready"], 1)
                        add_square(k, dve, b, squares, s)
    k.blocks = base + KD


def add_chunk(k, dve, n, c, out):
    cols = slice(c * CW, (c + 1) * CW)
    acc_wait(k, dve, n, c)
    k.nc.vector.tensor_tensor(out[:, :, cols], k.acc[:, c:c + 1, 0:CW], out[:, :, cols], ALU.add).then_inc(k.acc_free, 1)


SQUARES = ("h_ready", "sq_ready", "sq_added")

def square_block(k, act, h, b, squares, s):
    act.wait_ge(s["h_ready"], b + 1)
    act.wait_ge(s["sq_added"], b)
    k.nc.scalar.activation(squares.unsqueeze(1), h[:, bass.ds(b, 1), :], ACT.Square).then_inc(s["sq_ready"], 1)


def add_square(k, dve, b, squares, s):
    dve.wait_ge(s["sq_ready"], b + 1)
    dve.wait_ge(s["sq_added"], b)
    k.nc.vector.tensor_tensor(k.sq_sum[:, :], k.sq_sum[:, :], squares, ALU.add).then_inc(s["sq_added"], 1)


class Norm:
    POOL_BLOCKS = (2, 4, 6)

    def __init__(self, k, ctx, h, gain, places, name):
        self.k, self.h, self.gain = k, h, gain
        self.places = places
        self.sums = k.ps(ctx, name + "_sums", [P, NCH, 512])
        self.rstd = k.sq_sum
        self.summed, self.log_ready, self.rstd_ready, self.x_ready, self.hi_ready, self.lo_dve, self.lo_pool = (
            k.sem(ctx, f"{name}_{n}") for n in ("summed", "log_ready", "rstd_ready", "x_ready", "hi_ready", "lo_dve", "lo_pool"))

    def place(self, c, m):
        return self.places[(c * KD + m) % len(self.places)]

    def sum(self, pe):
        for c in range(NCH):
            self.k.nc.tensor.matmul(self.sums[:, c, 0:CW], self.k.ones[:, :], self.k.sq_sum[:, c * CW:(c + 1) * CW],
                                    start=True, stop=True).then_inc(self.summed, 1)

    def wait(self, eng, c):
        eng.wait_ge(self.lo_dve, (c + 1) * (KD - len(self.POOL_BLOCKS)))
        eng.wait_ge(self.lo_pool, (c + 1) * len(self.POOL_BLOCKS))

    def scale(self, dve):
        k, nc = self.k, self.k.nc
        for c in range(NCH):
            cols = slice(c * CW, (c + 1) * CW)

            def low(m):
                dve.wait_ge(self.hi_ready, c * KD + m + 1)
                nc.vector.tensor_tensor(k.x_lo[:, m, cols], self.place(c, m),
                                        k.x_hi[:, m, cols].bitcast(F32), ALU.subtract).then_inc(self.lo_dve, 1)

            dve.wait_ge(self.rstd_ready, c + 1)
            for m in range(KD):
                last = c * KD + m - len(self.places)
                if last >= 0:
                    done = [j % KD in self.POOL_BLOCKS for j in range(last + 1)]
                    dve.wait_ge(self.lo_pool if done[-1] else self.lo_dve, done.count(done[-1]))
                nc.vector.scalar_tensor_tensor(out=self.place(c, m), in0=self.h[:, m, cols],
                                               scalar=self.gain[:, m:m + 1], in1=self.rstd[:, cols],
                                               op0=ALU.mult, op1=ALU.mult).then_inc(self.x_ready, 1)
                if m and m - 1 not in self.POOL_BLOCKS:
                    low(m - 1)
            low(KD - 1)
        self.wait(dve, NCH - 1)

    def round(self, act):
        act.preload_act_table_set(EXP_LN)
        for c in range(NCH):
            cols = slice(c * CW, (c + 1) * CW)
            act.wait_ge(self.summed, c + 1)
            self.k.nc.scalar.activation(self.rstd[:, cols], self.sums[:, c, 0:CW], ACT.Ln, scale=1.0 / D,
                                        bias=self.k.eps[:, :]).then_inc(self.log_ready, 1)
            act.wait_ge(self.log_ready, c + 1)
            self.k.nc.scalar.activation(self.rstd[:, cols], self.rstd[:, cols], ACT.Exp, scale=-0.5)\
                .then_inc(self.rstd_ready, 1)
        for c in range(NCH):
            cols = slice(c * CW, (c + 1) * CW)
            for m in range(KD):
                act.wait_ge(self.x_ready, c * KD + m + 1)
                self.k.nc.scalar.activation(self.k.x_hi[:, m, cols], self.place(c, m), ACT.Copy).then_inc(self.hi_ready, 1)

    def low(self, pool):
        k = self.k
        for c in range(NCH):
            cols = slice(c * CW, (c + 1) * CW)
            for m in self.POOL_BLOCKS:
                pool.wait_ge(self.hi_ready, c * KD + m + 1)
                k.nc.gpsimd.tensor_tensor(k.x_lo[:, m, cols], self.place(c, m),
                                          k.x_hi[:, m, cols].bitcast(F32), ALU.subtract).then_inc(self.lo_pool, 1)


def feed_forward(k, h, then):
    nc, io = k.nc, k.io
    base = k.blocks
    G = FFN // D
    w_up = io["w_up"][0].rearrange("(k p) n -> p k n", p=P)
    w_down = io["w_down"][0].rearrange("(g k p) n -> p g k n", p=P, k=KD)
    with ExitStack() as ctx:
        u_hi = k.sb(ctx, "u_hi", [P, KD, TT], F32R)
        u_lo = k.sb(ctx, "u_lo", [P, KD, TT], F32R)
        relu = k.sb(ctx, "relu", [P, 3, CW])
        square = k.sb(ctx, "relu_sq", [P, 3, CW])
        squares = relu[:, :, :].rearrange("p c n -> p (c n)")
        s = {n: k.sem(ctx, "ff_" + n) for n in ("relu_ready", "squared", "rounded", "split") + SQUARES}
        norm = Norm(k, ctx, h, k.g_mlp, [t[:, c, :] for t in (relu, square) for c in range(NCH)], "n1")
        PG = KD * NCH
        with nc.Block() as block:
            @block.sync
            def _(sp):
                def up(g, b, par):
                    load_weights(k, sp, base + g * (2 * KD) + b, par, w_up[:, :, bass.ds(g * D + b * P, P)])

                def down(g, b, par):
                    load_weights(k, sp, base + g * (2 * KD) + KD + b, par,
                                 w_down[:, bass.ds(g, 1), :, bass.ds(b * P, P)].squeeze(1))

                def group(g):
                    with sp.Fori(0, KD // 2 - 1) as i:
                        up(g, i * 2 + 1, 1)
                        up(g, i * 2 + 2, 0)
                    up(g, KD - 1, 1)
                    down(g, 0, 0)
                    with sp.Fori(0, KD // 2 - 1) as i:
                        down(g, i * 2 + 1, 1)
                        down(g, i * 2 + 2, 0)
                    down(g, KD - 1, 1)

                with sp.Fori(0, G - 1) as g:
                    group(g)
                    load_weights(k, sp, base + g * (2 * KD) + 2 * KD, 0, w_up[:, :, bass.ds(g * D + D, P)])
                group(G - 1)
                load_weights(k, sp, base + G * 2 * KD, 0, then)

            @block.gpsimd
            def _(pool):
                norm.low(pool)
                split_ahead(k, pool, base, G * 2 * KD)

            @block.tensor
            def _(pe):
                norm.sum(pe)
                with pe.Fori(0, G) as g:
                    n0 = base + g * (2 * KD)
                    with pe.Fori(0, KD // 2) as i:
                        for par in range(2):
                            for c in range(NCH):
                                if par == 0:
                                    norm.wait(pe, c)
                                project_chunk(k, pe, n0 + i * 2 + par, par, c, k.x_hi, k.x_lo)
                    for par in range(2):
                        for c in range(NCH):
                            if par == 0:
                                pe.wait_ge(s["split"], g * PG + (KD - 1) * NCH + c + 1)
                            project_chunk(k, pe, n0 + KD + par, par, c, u_hi, u_lo)
                    with pe.Fori(1, KD // 2) as i:
                        for par in range(2):
                            for c in range(NCH):
                                project_chunk(k, pe, n0 + KD + i * 2 + par, par, c, u_hi, u_lo)

            @block.vector
            def _(dve):
                norm.scale(dve)
                dve.drain()
                nc.vector.memset(k.sq_sum[:, :], 0.0)

                def up(g, n0):
                    with dve.Fori(0, KD // 2) as i:
                        def finish(e):
                            par, c = divmod(e, NCH)
                            t = g * PG + i * (2 * NCH) + e
                            dve.wait_ge(s["rounded"], t + 1)
                            nc.vector.tensor_tensor(u_lo[:, bass.ds(i * 2 + par, 1), c * CW:(c + 1) * CW],
                                                    square[:, c:c + 1, :],
                                                    u_hi[:, bass.ds(i * 2 + par, 1), c * CW:(c + 1) * CW].bitcast(F32),
                                                    ALU.subtract).then_inc(s["split"], 1)
                        for e in range(2 * NCH):
                            par, c = divmod(e, NCH)
                            acc_wait(k, dve, n0 + i * 2 + par, c)
                            if e >= NCH:
                                dve.wait_ge(s["rounded"], g * PG + i * (2 * NCH) + e - NCH + 1)
                            nc.vector.tensor_scalar(relu[:, c, :], k.acc[:, c, 0:CW], 0.0, None, ALU.max)\
                              .then_inc(k.acc_free, 1)
                            dve.drain().then_inc(s["relu_ready"], 1)
                            if e:
                                finish(e - 1)
                        finish(2 * NCH - 1)

                def down(n0, last):
                    with dve.Fori(0, KD // 2) as i:
                        for par in range(2):
                            b = i * 2 + par
                            for c in range(NCH):
                                add_chunk(k, dve, n0 + KD + b, c, h[:, bass.ds(b, 1), :])
                            if last:
                                dve.drain().then_inc(s["h_ready"], 1)
                                add_square(k, dve, b, squares, s)

                with dve.Fori(0, G - 1) as g:
                    up(g, base + g * (2 * KD))
                    down(base + g * (2 * KD), False)
                up(G - 1, base + (G - 1) * 2 * KD)
                down(base + (G - 1) * 2 * KD, True)

            @block.scalar
            def _(act):
                norm.round(act)
                with act.Fori(0, G) as g:
                    with act.Fori(0, KD // 2) as i:
                        for e in range(2 * NCH):
                            par, c = divmod(e, NCH)
                            t = g * PG + i * (2 * NCH) + e
                            act.wait_ge(s["relu_ready"], t + 1)
                            act.wait_ge(s["split"], t - NCH + 1 if e >= NCH else g * PG + i * (2 * NCH))
                            nc.scalar.activation(square[:, c, :], relu[:, c, :], ACT.Square).then_inc(s["squared"], 1)
                            nc.scalar.activation(u_hi[:, bass.ds(i * 2 + par, 1), c * CW:(c + 1) * CW], relu[:, c:c + 1, :],
                                                 ACT.Square).then_inc(s["rounded"], 1)
                with act.Fori(0, KD // 2) as i:
                    for par in range(2):
                        square_block(k, act, h, i * 2 + par, squares, s)
    k.blocks = base + G * 2 * KD


def per_layer_embedding(k, h):
    nc, io = k.nc, k.io
    base = k.blocks
    KP = PLE // P
    w_gate = io["w_ple_gate"][0].rearrange("(k p) n -> p k n", p=P)
    w_ple = io["w_ple"][0].rearrange("(k p) n -> p k n", p=P)
    with ExitStack() as ctx:
        rows = k.sb(ctx, "p_rows", [P, TB + 1, PLE])
        p_hi = k.sb(ctx, "p_hi", [P, KP, TT], F32R)
        p_lo = k.sb(ctx, "p_lo", [P, KP, TT], F32R)
        p_raw = k.sb(ctx, "p_raw", [P, 2, KP, P])
        pt = k.ps(ctx, "p_turned", [P, 2, 4, P])
        prod = k.sb(ctx, "ple_prod", [P, TT])
        gate = k.sb(ctx, "ple_gate", [P, TT])
        emb = k.sb(ctx, "ple_emb", [P, TT])
        squares = k.sb(ctx, "h_squares3", [P, TT])[:, :]
        s = {n: k.sem(ctx, "pl_" + n) for n in ("product",
            "rows_in", "turned", "rounded", "split") + SQUARES}
        norm = Norm(k, ctx, h, k.g_ple, [t[:, c * CW:(c + 1) * CW] for t in (gate, emb) for c in range(NCH)], "n2")
        with nc.Block() as block:
            @block.sync
            def _(sp):
                sp.dma_start(rows[:, 0:TB, :], io["p_prompt"][0, 0].rearrange("(b p) c -> p b c", p=P)).then_inc(s["rows_in"], 16)
                sp.dma_start(rows[0:B, TB, :], io["p_sample"][0, :, 0, :]).then_inc(s["rows_in"], 16)
                with sp.Fori(0, KD - 1) as m:
                    load_weights(k, sp, base + m * 2 + 1, 1, w_ple[:, :, bass.ds(m * P, P)], KP)
                    load_weights(k, sp, base + m * 2 + 2, 0, w_gate[:, :, bass.ds(m * P + P, P)])
                load_weights(k, sp, base + KD * 2 - 1, 1, w_ple[:, :, D - P:D], KP)

            @block.gpsimd
            def _(pool):
                norm.low(pool)
                split_weights(k, pool, base + 1, 1, base // 2, KP)
                for t in range(TB + 1):
                    m = P if t < TB else B
                    pool.wait_ge(s["rounded"], t + 1)
                    nc.gpsimd.tensor_tensor(p_lo[:, :, t * P:t * P + m], p_raw[:, t % 2, :, 0:m],
                                            p_hi[:, :, t * P:t * P + m].bitcast(F32), ALU.subtract).then_inc(s["split"], 1)
                with pool.Fori(1, KD) as m:
                    split_weights(k, pool, base + m * 2, 0, base // 2 + m)
                    split_weights(k, pool, base + m * 2 + 1, 1, base // 2 + m, KP)

            @block.tensor
            def _(pe):
                norm.sum(pe)
                for c in range(NCH):
                    norm.wait(pe, c)
                    project_chunk(k, pe, base, 0, c, k.x_hi, k.x_lo)
                pe.wait_ge(s["rows_in"], 32)
                for t in range(TB + 1):
                    m = P if t < TB else B
                    if t >= 2:
                        pe.wait_ge(s["rounded"], t - 1)
                    for i in range(KP):
                        tr = nc.tensor.transpose(pt[:, t % 2, i, 0:m], rows[0:m, t, i * P:(i + 1) * P], k.ident[0:m, 0:m])
                    tr.then_inc(s["turned"], 1)
                pe.wait_ge(s["split"], TB + 1)
                for c in range(NCH):
                    project_chunk(k, pe, base + 1, 1, c, p_hi, p_lo, KP)
                with pe.Fori(1, KD) as m:
                    for c in range(NCH):
                        project_chunk(k, pe, base + m * 2, 0, c, k.x_hi, k.x_lo)
                    for c in range(NCH):
                        project_chunk(k, pe, base + m * 2 + 1, 1, c, p_hi, p_lo, KP)

            @block.scalar
            def _(act):
                norm.round(act)
                for t in range(TB + 1):
                    m = P if t < TB else B
                    act.wait_ge(s["turned"], t + 1)
                    if t >= 2:
                        act.wait_ge(s["split"], t - 1)
                    nc.scalar.activation(p_raw[:, t % 2, :, 0:m], pt[:, t % 2, 0:KP, 0:m], ACT.Copy)
                    nc.scalar.activation(p_hi[:, :, t * P:t * P + m], pt[:, t % 2, 0:KP, 0:m], ACT.Copy).then_inc(s["rounded"], 1)
                norm.wait(act, NCH - 1)
                act.preload_act_table_set("sigmoid_and_others")
                with act.Fori(0, KD) as m:
                    for half, (out, func) in enumerate(((gate, ACT.Sigmoid), (emb, ACT.Copy))):
                        for c in range(NCH):
                            acc_wait(k, act, base + m * 2 + half, c)
                            if half == 0 and c == 0:
                                act.wait_ge(s["product"], m)
                            nc.scalar.activation(out[:, c * CW:(c + 1) * CW], k.acc[:, c, 0:CW], func).then_inc(k.acc_free, 1)
                    square_block(k, act, h, m, squares, s)

            @block.vector
            def _(dve):
                norm.scale(dve)
                nc.vector.memset(k.sq_sum[:, :], 0.0)
                with dve.Fori(0, KD) as m:
                    dve.wait_ge(k.acc_free, (base + m * 2 + 2) * NCH + NCH)
                    dve.wait_ge(s["h_ready"], m)
                    nc.vector.tensor_tensor(prod[:, :], gate[:, :], emb[:, :], ALU.mult).then_inc(s["product"], 1)
                    dve.wait_ge(s["product"], m + 1)
                    nc.vector.tensor_tensor(h[:, bass.ds(m, 1), :], h[:, bass.ds(m, 1), :], prod[:, :].unsqueeze(1),
                                            ALU.add).then_inc(s["h_ready"], 1)
                    add_square(k, dve, m, squares, s)
    k.blocks = base + KD * 2


def final_norm(k, h):
    nc, io = k.nc, k.io
    tiles = [(t * P, P) for t in range(TB)] + [(T, B)]
    NT = len(tiles)
    with ExitStack() as ctx:
        gain = k.sb(ctx, "g_final_rows", [P, D])
        rstd = k.sb(ctx, "fn_rstd", [P, NT])
        y = k.sb(ctx, "fn_y", [P, 3, D])
        sums = k.ps(ctx, "fn_sums", [P, NT])
        pt = k.ps(ctx, "fn_pt", [P, 2, D])
        s = {n: k.sem(ctx, "fn_" + n) for n in ("gain_in", "summed", "turned", "rstd_ready", "y_ready")}
        sent = [k.sem(ctx, f"y_sent{i}") for i in range(3)]
        y_p = io["y_prompt"].rearrange("b t d -> (b t) d")
        y_s = io["y_sample"].rearrange("b t d -> (b t) d")
        with nc.Block() as block:
            @block.sync
            def _(sp):
                sp.dma_start(gain[:, :], io["g_final"].unsqueeze(0).to_broadcast([P, D])).then_inc(s["gain_in"], 16)
                for i, (t0, m) in enumerate(tiles):
                    sp.wait_ge(s["y_ready"], i + 1)
                    sp.dma_start(y_p[t0:t0 + m, :] if t0 < T else y_s, y[0:m, i % 3, :]).then_inc(sent[i % 3], 16)
                for i in range(3):
                    sp.wait_ge(sent[i], 16 * len(tiles[i::3]))

            @block.tensor
            def _(pe):
                for i, (t0, m) in enumerate(tiles):
                    mm = nc.tensor.matmul(sums[0:m, i:i + 1], k.sq_sum[:, t0:t0 + m], k.ones[:, 0:1], start=True, stop=True)
                mm.then_inc(s["summed"], 1)
                for i, (t0, m) in enumerate(tiles):
                    if i >= 2:
                        pe.wait_ge(s["y_ready"], i - 1)
                    for b in range(KD):
                        tr = nc.tensor.transpose(pt[0:m, i % 2, b * P:(b + 1) * P], h[:, b, t0:t0 + m], k.ident[:, :])
                    tr.then_inc(s["turned"], 1)

            @block.scalar
            def _(act):
                act.preload_act_table_set(EXP_LN)
                act.wait_ge(s["summed"], 1)
                for cols, m in ((slice(0, TB), P), (slice(TB, NT), B)):
                    nc.scalar.activation(rstd[0:m, cols], sums[0:m, cols], ACT.Ln, scale=1.0 / D, bias=k.eps[0:m, :])
                    act.drain()
                    op = nc.scalar.activation(rstd[0:m, cols], rstd[0:m, cols], ACT.Exp, scale=-0.5)
                op.then_inc(s["rstd_ready"], 1)

            @block.vector
            def _(dve):
                dve.wait_ge(s["gain_in"], 16)
                dve.wait_ge(s["rstd_ready"], 1)
                for i, (t0, m) in enumerate(tiles):
                    dve.wait_ge(s["turned"], i + 1)
                    if i >= 3:
                        dve.wait_ge(sent[i % 3], 16 * (i // 3))
                    nc.vector.scalar_tensor_tensor(out=y[0:m, i % 3, :], in0=pt[0:m, i % 2, :], scalar=rstd[0:m, i:i + 1],
                                                   in1=gain[0:m, :], op0=ALU.mult, op1=ALU.mult).then_inc(s["y_ready"], 1)

def allocate(k, ctx):
    k.x_hi = k.sb(ctx, "x_hi", [P, KD, TT], F32R)
    k.x_lo = k.sb(ctx, "x_lo", [P, KD, TT], F32R)
    k.w_raw = k.sb(ctx, "w_raw", [P, 2, KD, P])
    k.w_hi = k.sb(ctx, "w_hi", [P, 2, KD, P], F32R)
    k.w_lo = k.sb(ctx, "w_lo", [P, 2, KD, P], F32R)
    k.ident, k.ones, k.neg_ones, k.sum_to, k.neg_from, k.late_big, k.late_neg = (
        k.sb(ctx, name, [P, P])
        for name in ("ident", "ones", "neg_ones", "sum_to", "neg_from", "late_big", "late_neg"))
    k.eps = k.sb(ctx, "eps", [P, 1])
    k.g_mix, k.g_mlp, k.g_ple = (k.sb(ctx, name, [P, KD]) for name in ("g_mix_c", "g_mlp_c", "g_ple_c"))
    k.b_if = k.sb(ctx, "b_if_c", [P, 2 * H])
    k.b_sb = k.sb(ctx, "b_sb_c", [P, H])
    k.conv_w = k.sb(ctx, "conv_w_c", [P, 3, H])
    k.acc = k.ps(ctx, "acc", [P, NCH, 512])
    k.w_landed = [k.sem(ctx, f"w_landed{i}") for i in range(2)]
    k.w_rounded, k.w_split, k.acc_ready, k.acc_free, k.pool_tick, k.params_in = (
        k.sem(ctx, name) for name in ("w_rounded", "w_split", "acc_ready", "acc_free", "pool_tick", "params_in"))
    k.before = k.sb(ctx, "before", [P, P])
    k.conv_state = k.sb(ctx, "conv_state", [P, H, 2 * B])
    k.n_old = k.sb(ctx, "n_old", [P, B * H])
    k.g_col = k.sb(ctx, "g_col", [P, TB, H])
    k.mu = k.sb(ctx, "mu", [P, TB, H])
    k.exps = k.sb(ctx, "exps", [P, N_E, TB, H])
    k.gates_dec = k.sb(ctx, "gates_dec", [B, 2 * H])
    k.q_tok = k.sb(ctx, "q_tok", [B, W])
    k.two_idents = k.sb(ctx, "two_idents", [4 * H, 2 * H])


def hybrid_layer(nc, io):
    k = Chip(nc, io)
    k.x_T = nc.dram_tensor("x_feature_major", [P, KD, TT], F32, kind="Internal").ap()
    k.gates = nc.dram_tensor("merge_gates", [P, 3 * KD, TT], F32, kind="Internal").ap()
    k.branch = nc.dram_tensor("branch_outputs", [3, P, H, TT], F32, kind="Internal").ap()
    w_in = io["w_in"].rearrange("l (k p) n -> p (l k) n", p=P)

    w_branch = io["w_branch"][0, 0].rearrange("(k p) n -> p k n", p=P)
    w_out, w_up, w_ple_gate = (io[n][0].rearrange("(k p) n -> p k n", p=P) for n in ("w_out", "w_up", "w_ple_gate"))

    def group(col, out, scale=1.0, func=ACT.Copy):
        return dict(col=col, out=out, scale=scale, func=func)

    def block_of(t, first):
        return lambda b: t[:, bass.ds(b + first, 1), :]

    with ExitStack() as ctx:
        allocate(k, ctx)
        k.phase_sems = []
        constants(k)
        turn_states(k)
        normalise_input(k, w_in[:, :, C_SQ:C_SQ + P])
        with ExitStack() as part:
            s_T = k.sb(part, "s_T", [P, 3 * H, TT])
            project_attention(k, [group(C_SQ, block_of(s_T, 0), HD_SCALE), group(C_SK, block_of(s_T, H)),
                                  group(C_SV, block_of(s_T, 2 * H))], s_T, w_in[:, :, C_CC:C_CC + P])
            stick_breaking_prompt(k, s_T, w_in[:, :, C_MQ:C_MQ + P])
        with ExitStack() as part:
            m_T = k.sb(part, "m_T", [P, 4 * H, TT])
            k.dec_prob = k.sb(part, "dec_prob", [P, B, PAGES, H])
            project_mlstm(k, m_T, [group(C_MQ, block_of(m_T, 0)), group(C_MK, block_of(m_T, H), HD_SCALE),
                                   group(C_MV, block_of(m_T, 2 * H)),
                                   group(C_MO, block_of(m_T, 3 * H), func=ACT.Sigmoid)],
                          w_in[:, :, C_G + H * P:C_G + H * P + P])
            mlstm_prompt(k, m_T, w_branch[:, :, 0:P])
            mlstm_decode(k, m_T)
        h = k.sb(ctx, "h", [P, KD, TT])
        k.sq_sum = k.sb(ctx, "sq_sum", [P, TT])
        merge_branches(k, h, w_out[:, :, 0:P])
        mix_out(k, h, w_up[:, :, 0:P])
        feed_forward(k, h, w_ple_gate[:, :, 0:P])
        per_layer_embedding(k, h)
        final_norm(k, h)


_INS = ["x_prompt", "x_sample", "cache_k", "cache_v", "state_mlstm_C", "state_mlstm_n", "state_mlstm_m", "state_conv",
        "page_table", "p_prompt", "p_sample", "g_mix", "w_in", "b_if", "b_sb", "conv_w", "w_branch", "w_out", "g_mlp",
        "w_up", "w_down", "g_ple", "w_ple_gate", "w_ple", "g_final"]
_OUTS = [("y_prompt", (1, T, D)), ("y_sample", (B, 1, D)), ("k_prompt", (1, 1, T, H, P)), ("v_prompt", (1, 1, T, H, P)),
         ("C_prompt", (1, 1, H, P, P)), ("n_prompt", (1, 1, H, P)), ("m_prompt", (1, 1, H)), ("conv_prompt", (1, 1, 2, W)),
         ("k_sample", (1, B, 1, H, P)), ("v_sample", (1, B, 1, H, P)), ("C_sample", (1, B, H, P, P)),
         ("n_sample", (1, B, H, P)), ("m_sample", (1, B, H)), ("conv_sample", (1, B, 2, W))]


def kernel(**inputs):
    import numpy as _np
    import concourse.bacc as _bacc
    from concourse import mybir as _mybir
    from concourse.bass_utils import run_bass_kernel_spmd as _run

    nc = _bacc.Bacc("TRN2", target_bir_lowering=False, num_devices=1)
    arrays, io = {}, {}
    for name in _INS:
        a = _np.ascontiguousarray(inputs[name])
        arrays[f"in_{name}"] = a
        io[name] = nc.dram_tensor(f"in_{name}", a.shape, _mybir.dt.from_np(a.dtype), kind="ExternalInput").ap()
    for name, shape in _OUTS:
        io[name] = nc.dram_tensor(f"out_{name}", shape, _mybir.dt.float32, kind="ExternalOutput").ap()
    hybrid_layer(nc, io)
    r = _run(nc, [arrays], core_ids=[0])
    return tuple(r.results[0][f"out_{name}"] for name, _ in _OUTS)
```

```python
from contextlib import ExitStack

import concourse.bass as bass
from concourse import mybir
from concourse.alu_op_type import AluOpType as ALU

ACT = mybir.ActivationFunctionType
F32 = mybir.dt.float32
F32R = mybir.dt.float32r
I32 = mybir.dt.int32
AX = mybir.AxisListType

P = 128
D = 1024
KD = D // P
T = 1024
TB = T // P
B = 8
TT = T + B
NCH = 3
CW = TT // NCH
CHUNKS = [slice(c * CW, (c + 1) * CW) for c in range(NCH)]
H = 4
W = H * P
PAGES = 8
N_PHYS = 80
FFN = 4 * D
PLE = 256
RING = 4
EPS = 1e-6
HD_SCALE = float(P) ** -0.5
BIG = 1e30
EXP_LN = "natural_log_exp_and_others"

C_MQ, C_MK, C_MV, C_MO, C_IF = 0, W, 2 * W, 3 * W, 4 * W
C_CB = 4 * W + 2 * H
C_CC, C_CX = C_CB + W, C_CB + 2 * W
C_SQ = C_CB + 3 * W
C_SK, C_SV = C_SQ + W, C_SQ + 2 * W
C_G = C_SQ + 3 * W
N_IN = C_G + 3 * D


class Chip:

    def __init__(self, nc, io):
        self.nc = nc
        self.io = io
        self.blocks = 0
        self.phase_sems = []

    def sb(self, ctx, name, shape, dt=F32):
        return ctx.enter_context(self.nc.sbuf_tensor(name, shape, dt))

    def ps(self, ctx, name, shape, dt=F32):
        return ctx.enter_context(self.nc.psum_tensor(name, shape, dt))

    def sem(self, ctx, name):
        handle = self.nc.alloc_semaphore(name=name)
        self.phase_sems.append(handle)
        return handle

    def clear_semaphores(self, pool, sems):
        for sem in sems:
            pool.sem_clear(sem)
        self.cleared = sems

    def release_cleared(self):
        for sem in self.cleared:
            self.nc.release_semaphore(sem)



def load_weights(k, sp, n, par, src, kb=KD):
    sp.wait_ge(k.w_split, n + 1)
    sp.dma_start(k.w_raw[:, par, 0:kb, :], src).then_inc(k.w_landed[par], 16)


def split_weights(k, pool, n, par, pair, kb=KD):
    nc = k.nc
    pool.wait_ge(k.acc_ready, n * NCH + NCH)
    pool.sem_inc(k.pool_tick, 1)
    pool.wait_ge(k.w_landed[par], pair * 16 + 16)
    pool.sem_inc(k.pool_tick, 1)
    nc.gpsimd.tensor_scalar(k.w_hi[:, par, 0:kb, :], k.w_raw[:, par, 0:kb, :], 1.0, 1.0,
                            ALU.mult, ALU.mult).then_inc(k.w_rounded, 1)
    pool.wait_ge(k.w_rounded, n + 1)
    nc.gpsimd.tensor_tensor(k.w_lo[:, par, 0:kb, :], k.w_raw[:, par, 0:kb, :],
                            k.w_hi[:, par, 0:kb, :].bitcast(F32), ALU.subtract).then_inc(k.w_split, 1)


def each_ahead(eng, base, count, step):
    with eng.Fori(0, count // 2 - 1) as i:
        step(base + i * 2 + 1, 1, i * 2 + 1, base // 2 + i)
        step(base + i * 2 + 2, 0, i * 2 + 2, base // 2 + i + 1)
    step(base + count - 1, 1, count - 1, (base + count) // 2 - 1)


def split_ahead(k, pool, base, count, kb=KD, then_kb=KD):
    each_ahead(pool, base, count, lambda n, par, b, pair: split_weights(k, pool, n, par, pair, kb))
    split_weights(k, pool, base + count, 0, (base + count) // 2, then_kb)


def project_chunk(k, pe, n, par, c, x_hi, x_lo, kb=KD):
    if c == 0:
        pe.wait_ge(k.w_split, n + 3)
    pe.wait_ge(k.acc_free, n * NCH + c + 1)
    cols = slice(c * CW, (c + 1) * CW)
    for i in range(kb):
        for j, (w, x) in enumerate(((k.w_hi, x_hi), (k.w_hi, x_lo), (k.w_lo, x_hi))):
            mm = k.nc.tensor.matmul(k.acc[:, c, 0:CW], w[:, par, i, :], x[:, i, cols],
                                    start=(i == 0 and j == 0), stop=(i == kb - 1 and j == 2))
    mm.then_inc(k.acc_ready, 1)


def acc_wait(k, eng, n, c):
    eng.wait_ge(k.acc_ready, n * NCH + c + 1 + 2 * NCH)


def make_constants(k, pool):
    nc = k.nc
    nc.gpsimd.memset(k.ident[:, :], 0.0)
    nc.gpsimd.memset(k.ones[:, :], 1.0)
    nc.gpsimd.memset(k.neg_ones[:, :], -1.0)
    nc.gpsimd.memset(k.sum_to[:, :], 1.0)
    nc.gpsimd.memset(k.neg_from[:, :], -1.0)
    nc.gpsimd.memset(k.late_big[:, :], 0.0)
    nc.gpsimd.memset(k.late_neg[:, :], 0.0)
    nc.gpsimd.memset(k.eps[:, :], EPS)
    nc.gpsimd.memset(k.before[:, :], 1.0)
    nc.gpsimd.memset(k.two_idents[:, :], 0.0)
    pool.drain()
    nc.gpsimd.affine_select(out=k.two_idents[:, :], in_=k.two_idents[:, :], compare_op=ALU.not_equal, fill=1.0,
                            base=0, pattern=[[-1, 2 * H]], channel_multiplier=1)
    pool.drain()
    nc.gpsimd.affine_select(out=k.two_idents[:, :], in_=k.two_idents[:, :], compare_op=ALU.not_equal, fill=1.0,
                            base=-2 * H, pattern=[[-1, 2 * H]], channel_multiplier=1)
    nc.gpsimd.affine_select(out=k.before[:, :], in_=k.before[:, :], compare_op=ALU.is_gt, fill=0.0,
                            base=0, pattern=[[1, P]], channel_multiplier=-1)
    nc.gpsimd.affine_select(out=k.ident[:, :], in_=k.ident[:, :], compare_op=ALU.not_equal, fill=1.0,
                            base=0, pattern=[[-1, P]], channel_multiplier=1)
    nc.gpsimd.affine_select(out=k.sum_to[:, :], in_=k.sum_to[:, :], compare_op=ALU.is_ge, fill=0.0,
                            base=0, pattern=[[1, P]], channel_multiplier=-1)
    nc.gpsimd.affine_select(out=k.neg_from[:, :], in_=k.neg_from[:, :], compare_op=ALU.is_ge, fill=0.0,
                            base=0, pattern=[[-1, P]], channel_multiplier=1)
    nc.gpsimd.affine_select(out=k.late_big[:, :], in_=k.late_big[:, :], compare_op=ALU.is_ge, fill=BIG,
                            base=0, pattern=[[1, P]], channel_multiplier=-1)
    nc.gpsimd.affine_select(out=k.late_neg[:, :], in_=k.late_neg[:, :], compare_op=ALU.is_ge, fill=-BIG,
                            base=0, pattern=[[-1, P]], channel_multiplier=1)
    pool.drain().then_inc(k.consts_ready, 1)
    pool.sem_inc(k.w_split, 2)
    pool.sem_inc(k.acc_ready, 2 * NCH)
    pool.sem_inc(k.acc_free, NCH)


def load_parameters(k, sp):
    io = k.io

    def column(dst, src):
        sp.dma_start(dst, src, allow_slow_non_contiguous=True).then_inc(k.params_in, 16)
    column(k.g_mix[:, :], io["g_mix"].rearrange("l (k p) -> p (l k)", p=P))
    column(k.g_mlp[:, :], io["g_mlp"].rearrange("l (k p) -> p (l k)", p=P))
    column(k.g_ple[:, :], io["g_ple"].rearrange("l (k p) -> p (l k)", p=P))
    column(k.b_if[:, :], io["b_if"].to_broadcast([P, 2 * H]))
    column(k.b_sb[:, :], io["b_sb"].to_broadcast([P, H]))
    for j in range(3):
        column(k.conv_w[:, j, :], io["conv_w"][0, j, :].rearrange("(k p) -> p k", p=P))


def normalise_input(k, then):
    nc, io = k.nc, k.io
    tiles = [(t * P, P) for t in range(TB)] + [(T, B)]
    with ExitStack() as ctx:
        rows = k.sb(ctx, "x_rows", [P, 3, D])
        conv_rows = k.sb(ctx, "conv_rows", [2 * B, W])
        n_rows = k.sb(ctx, "n_rows", [B * H, P])
        pt_states = k.ps(ctx, "pt_states", [P, 512])
        squares = k.sb(ctx, "x_squares", [P, D])
        scales = k.sb(ctx, "x_scales", [P, 2, P])
        sums = k.sb(ctx, "x_sums", [P, len(tiles)])
        rstd = k.sb(ctx, "x_rstd", [P, len(tiles)])
        turned = k.sb(ctx, "x_turned", [P, 2, KD, P])
        gained = k.sb(ctx, "x_gained", [P, 2, KD, P])
        pt_x = k.ps(ctx, "pt_x", [P, KD, P])
        pt_s = k.ps(ctx, "pt_s", [P, KD, P])
        rows_in = [k.sem(ctx, f"rows_in{i}") for i in range(3)]
        x_out = [k.sem(ctx, f"x_out{i}") for i in range(2)]
        states_in, states_turned = k.sem(ctx, "states_in"), k.sem(ctx, "states_turned")
        scaled_ok, turned_x, turned_s, x_read, s_read, rounded, split, rms = (
            k.sem(ctx, n) for n in ("scaled_ok", "turned_x", "turned_s", "x_read", "s_read",
                                    "rounded", "split", "rms"))
        x_p = io["x_prompt"].rearrange("b t d -> (b t) d")
        x_s = io["x_sample"].rearrange("b t d -> (b t) d")
        with nc.Block() as block:
            @block.sync
            def _(sp):
                def store(i):
                    t0, m = tiles[i]
                    sp.wait_ge(x_read, i + 1)
                    sp.dma_start(k.x_T[:, :, t0:t0 + m], turned[:, i % 2, :, 0:m]).then_inc(x_out[i % 2], 16)

                for i, (t0, m) in enumerate(tiles):
                    if i == 2:
                        load_parameters(k, sp)
                        load_weights(k, sp, k.blocks, 0, then)
                    if i >= 3:
                        sp.wait_ge(turned_s, i - 2)
                    src = x_p[t0:t0 + m, :] if t0 < T else x_s
                    sp.dma_start(rows[0:m, i % 3, :], src).then_inc(rows_in[i % 3], 16)
                    if i >= 2:
                        store(i - 2)
                sp.dma_start(conv_rows[:, :], io["state_conv"].rearrange("l b s c -> (l b s) c")).then_inc(states_in, 16)
                sp.dma_start(n_rows[:, :], io["state_mlstm_n"].rearrange("l b h d -> (l b h) d")).then_inc(states_in, 16)
                sp.dma_start(io["conv_sample"][0, :, 0, :], io["state_conv"][0, :, 1, :]).then_inc(states_in, 16)
                sp.wait_ge(states_in, 48)
                store(len(tiles) - 2)
                store(len(tiles) - 1)
                for i in range(2):
                    sp.wait_ge(x_out[i], 16 * len(tiles[i::2]))

            @block.scalar
            def _(act):
                act.preload_act_table_set(EXP_LN)
                act.wait_ge(k.consts_ready, 1)

                def root(i):
                    t0, m = tiles[i]
                    act.wait_ge(rows_in[i % 3], 16 * (i // 3 + 1))
                    if i >= 2:
                        act.wait_ge(scaled_ok, i - 1)
                    nc.scalar.activation(squares[0:m, :], rows[0:m, i % 3, :], ACT.Square,
                                         accum_out=sums[0:m, i:i + 1])
                    act.drain()
                    nc.scalar.activation(rstd[0:m, i:i + 1], sums[0:m, i:i + 1], ACT.Ln,
                                         scale=1.0 / D, bias=k.eps[0:m, :])
                    act.drain()
                    nc.scalar.activation(rstd[0:m, i:i + 1], rstd[0:m, i:i + 1], ACT.Exp, scale=-0.5).then_inc(rms, 1)

                root(0)
                for i, (t0, m) in enumerate(tiles):
                    if i + 1 < len(tiles):
                        root(i + 1)
                    act.wait_ge(s_read, i + 1)
                    nc.scalar.activation(k.x_hi[:, :, t0:t0 + m], gained[:, i % 2, :, 0:m], ACT.Copy)\
                       .then_inc(rounded, 1)

            @block.vector
            def _(dve):
                dve.wait_ge(k.consts_ready, 1)
                for i, (t0, m) in enumerate(tiles):
                    dve.wait_ge(rms, i + 1)
                    if i >= 2:
                        dve.wait_ge(turned_s, i - 1)
                    nc.vector.tensor_scalar(scales[0:m, i % 2, 0:m], k.ident[0:m, 0:m], rstd[0:m, i:i + 1],
                                            None, ALU.mult).then_inc(scaled_ok, 1)
                    dve.wait_ge(turned_x, i + 1)
                    if i >= 2:
                        dve.wait_ge(x_out[i % 2], 16 * (i // 2))
                    nc.vector.tensor_copy(turned[:, i % 2, :, 0:m], pt_x[:, :, 0:m]).then_inc(x_read, 1)
                    dve.wait_ge(k.params_in, 8 * 16)
                    dve.wait_ge(turned_s, i + 1)
                    if i >= 2:
                        dve.wait_ge(split, i - 1)
                    nc.vector.tensor_tensor(gained[:, i % 2, :, 0:m], pt_s[:, :, 0:m],
                                            k.g_mix[:, :].unsqueeze(2).to_broadcast([P, KD, m]),
                                            ALU.mult).then_inc(s_read, 1)
                dve.wait_ge(states_turned, 1)
                nc.vector.tensor_copy(k.conv_state[:, :, :], pt_states[:, 0:H * 2 * B].rearrange("p (h c) -> p h c", h=H))
                nc.vector.tensor_copy(k.n_old[:, :], pt_states[:, 128:128 + B * H])

            @block.gpsimd
            def _(pool):
                make_constants(k, pool)
                split_weights(k, pool, k.blocks, 0, k.blocks // 2)
                for i, (t0, m) in enumerate(tiles):
                    pool.wait_ge(rounded, i + 1)
                    nc.gpsimd.tensor_tensor(k.x_lo[:, :, t0:t0 + m], gained[:, i % 2, :, 0:m],
                                            k.x_hi[:, :, t0:t0 + m].bitcast(F32), ALU.subtract).then_inc(split, 1)

            @block.tensor
            def _(pe):
                pe.wait_ge(k.consts_ready, 1)
                for i, (t0, m) in enumerate(tiles):
                    pe.wait_ge(rows_in[i % 3], 16 * (i // 3 + 1))
                    if i:
                        pe.wait_ge(x_read, i)
                    for b in range(KD):
                        tr = nc.tensor.transpose(pt_x[:, b, 0:m], rows[0:m, i % 3, b * P:(b + 1) * P],
                                                 k.ident[0:m, 0:m])
                    tr.then_inc(turned_x, 1)
                    pe.wait_ge(scaled_ok, i + 1)
                    if i:
                        pe.wait_ge(s_read, i)
                    for b in range(KD):
                        tr = nc.tensor.matmul(pt_s[:, b, 0:m], rows[0:m, i % 3, b * P:(b + 1) * P],
                                              scales[0:m, i % 2, 0:m], start=True, stop=True)
                    tr.then_inc(turned_s, 1)
                pe.wait_ge(states_in, 48)
                for h in range(H):
                    nc.tensor.transpose(pt_states[:, h * 2 * B:(h + 1) * 2 * B], conv_rows[:, h * P:(h + 1) * P],
                                        k.ident[0:2 * B, 0:2 * B])
                nc.tensor.transpose(pt_states[:, 128:128 + B * H], n_rows[:, :], k.ident[0:B * H, 0:B * H])\
                    .then_inc(states_turned, 1)


def project_attention(k, groups, s_T, then):
    nc, io = k.nc, k.io
    base = k.blocks
    count = H * len(groups)
    part = ExitStack()
    turned = k.ps(part, "q_turned", [B, W])
    q_turned = k.sem(part, "q_turned")
    w_in = io["w_in"].rearrange("l (k p) n -> p (l k) n", p=P)
    with nc.Block() as block:
        @block.sync
        def _(sp):
            each_ahead(sp, base, count, lambda n, par, b, pair: load_weights(
                k, sp, n, par, w_in[:, :, bass.ds(b * P + groups[0]["col"], P)]))
            load_weights(k, sp, base + count, 0, then)

        @block.gpsimd
        def _(pool):
            split_ahead(k, pool, base, count)

        @block.tensor
        def _(pe):
            with pe.Fori(0, count // 2) as i:
                for par in range(2):
                    for c in range(NCH):
                        project_chunk(k, pe, base + i * 2 + par, par, c, k.x_hi, k.x_lo)
            pe.wait_ge(k.acc_free, (base + H) * NCH + NCH)
            for h in range(H):
                tr = nc.tensor.transpose(turned[:, h * P:(h + 1) * P], s_T[:, h, T:TT], k.ident[:, :])
            tr.then_inc(q_turned, 1)

        @block.vector
        def _(dve):
            dve.wait_ge(q_turned, 1)
            nc.vector.tensor_copy(k.q_tok[:, :], turned[:, :])

        @block.scalar
        def _(act):
            for gi, g in enumerate(groups):
                with act.Fori(0, H // 2) as i:
                    for par in range(2):
                        b = i * 2 + par
                        for c in range(NCH):
                            acc_wait(k, act, base + gi * H + b, c)
                            nc.scalar.activation(g["out"](b)[:, :, c * CW:(c + 1) * CW], k.acc[:, c:c + 1, 0:CW],
                                                 g["func"], scale=g["scale"]).then_inc(k.acc_free, 1)
    part.close()
    k.blocks = base + count


UNITS = [(half, kb, max(0, kb * P - half * 512)) for half in range(2) for kb in range(4 * half + 3, -1, -1)]
NU = len(UNITS)


def unit_is_first(u):
    return u == 0 or UNITS[u][0] != UNITS[u - 1][0]


def unit_is_diagonal(u):
    return UNITS[u][1] >= 4 * UNITS[u][0]


NDIAG = sum(unit_is_diagonal(u) for u in range(NU))
DIAG_BEFORE = [sum(unit_is_diagonal(v) for v in range(u)) for u in range(NU + 1)]


HAS_NEXT = [u + 1 < NU and not unit_is_first(u + 1) for u in range(NU)]
NPARTS = sum(HAS_NEXT)
PARTS_BEFORE = [sum(HAS_NEXT[:u]) for u in range(NU)]


def stick_breaking_prompt(k, s_T, then):
    nc, io = k.nc, k.io
    base = k.blocks
    NB = 4
    SLOTS = NB * NCH
    cols = (C_CC, C_CX, C_CB, C_G)
    w_in = io["w_in"].rearrange("l (k p) n -> p (l k) n", p=P)
    with ExitStack() as ctx:
        k_head = k.sb(ctx, "k_head", [P, TT])
        k_tok = k.sb(ctx, "k_tok", [P, TB, P])
        v_tok = k.sb(ctx, "v_tok", [P, TB, P])
        kv_dec = k.sb(ctx, "kv_dec", [B, 2, P])
        bias = k.sb(ctx, "sb_bias", [P, 1])
        z_abs = k.sb(ctx, "z_abs", [P, 2, 512])
        z_pos = k.sb(ctx, "z_pos", [P, 512])
        sp_ = z_abs
        sp_hi = k.sb(ctx, "sp_hi", [P, 2, 512], F32R)
        sp_lo = k.sb(ctx, "sp_lo", [P, 2, 512], F32R)
        later_hi = k.sb(ctx, "later_hi", [P, 512], F32R)
        later_lo = k.sb(ctx, "later_lo", [P, 512], F32R)
        neg_from = k.sb(ctx, "neg_from_r", [P, P], F32R)
        neg_ones = k.sb(ctx, "neg_ones_r", [P, P], F32R)
        later = k.sb(ctx, "sp_later", [P, 512])
        prob = k.sb(ctx, "prob", [P, 2, 512])
        y_out = k.sb(ctx, "y_stick", [P, T])
        proj = k.sb(ctx, "proj_out", [P, NB, TT])
        cx = k.sb(ctx, "cx", [P, 2 + TT])
        v_head = cx[:, 2:2 + TT]
        conv = proj[:, 1, :]
        tails = k.sb(ctx, "cx_tails", [P, H, 2 + B])
        tail_rows = prob[0:2 + B, 0, :]
        z = k.ps(ctx, "z", [P, 3, 512])
        y = k.ps(ctx, "y", [P, 2, 512])
        names = ("staged", "bias_ready", "kv_turned", "v_ready", "kv_ready", "z_ready", "abs_ready", "z_read", "exp_ready", "log_ready",
                 "sp_ready", "sp_rounded", "sp_split", "later_ready", "later_rounded", "later_split", "consts_ready", "sums_added", "exp_done", "prob_ready", "av_done", "y_read",
                 "k_out", "v_out", "kd_out", "vd_out", "y_sent", "conv_sent", "gate_sent", "cx_ready", "conv_ready",
                 "tails_turned", "tails_ready", "tails_out")
        s = {n: k.sem(ctx, "sb_" + n) for n in names}
        with nc.Block() as block:
            @block.sync
            def _(sp):
                def load(j, b):
                    load_weights(k, sp, base + j * NB + b, b % 2, w_in[:, :, bass.ds(j * P + cols[b], P)])

                with sp.Fori(0, H - 1) as j:
                    for b in range(1, NB):
                        load(j, b)
                    load_weights(k, sp, base + j * NB + NB, 0, w_in[:, :, bass.ds(j * P + (cols[0] + P), P)])
                for b in range(1, NB):
                    load(H - 1, b)
                load_weights(k, sp, base + H * NB, 0, then)
                sp.wait_ge(s["tails_ready"], 1)
                sp.dma_start(io["conv_prompt"][0, 0, :, :], tail_rows[0:2, :]).then_inc(s["tails_out"], 16)
                sp.dma_start(io["conv_sample"][0, :, 1, :], tail_rows[2:2 + B, :]).then_inc(s["tails_out"], 16)
                sp.wait_ge(s["tails_out"], 32)

            @block.tensor
            def _(pe):
                pe.sem_inc(s["z_ready"], 1)
                pe.sem_inc(s["av_done"], 1)
                def turn_kv(j):
                    pe.wait_ge(s["staged"], j + 1)
                    pe.wait_ge(s["exp_done"], j * NU + 1)
                    pe.wait_ge(s["y_read"], j * 2 + 1)
                    for tb in range(TB):
                        nc.tensor.transpose(z[:, tb // 4, (tb % 4) * P:(tb % 4 + 1) * P],
                                            v_head[:, tb * P:(tb + 1) * P], k.ident[:, :])
                    nc.tensor.transpose(z[0:B, 2, 0:P], v_head[:, T:TT], k.ident[:, :])
                    for tb in range(TB):
                        nc.tensor.transpose(y[:, tb // 4, (tb % 4) * P:(tb % 4 + 1) * P],
                                            k_head[:, tb * P:(tb + 1) * P], k.ident[:, :])
                    nc.tensor.transpose(z[0:B, 2, P:2 * P], k_head[:, T:TT], k.ident[:, :]).then_inc(s["kv_turned"], 1)

                def scores(j, u):
                    half, kb, first = UNITS[u]
                    if u == 0:
                        pe.wait_ge(s["v_ready"], j + 1)
                        pe.wait_ge(s["kv_ready"], j + 1)
                    if u >= 3:
                        pe.wait_ge(s["exp_done"], j * NU + u - 2 + 1)
                    nc.tensor.matmul(z[:, u % 3, first:512], k_head[:, kb * P:(kb + 1) * P],
                                     s_T[:, bass.ds(j, 1), half * 512 + first:(half + 1) * 512],
                                     start=True, stop=True).then_inc(s["z_ready"], 1)

                def sums(j, u):
                    half, kb, first = UNITS[u]
                    pe.wait_ge(s["sp_split"], j * NU + u + 1)
                    for part in (sp_hi, sp_lo):
                        mm = nc.tensor.matmul(z[:, u % 3, first:512], neg_from[:, :], part[:, u % 2, first:512],
                                              start=False, stop=True, skip_group_check=True)
                    if not unit_is_first(u):
                        pe.wait_ge(s["later_split"], j * NPARTS + PARTS_BEFORE[u])
                        before = UNITS[u - 1][2]
                        for part in (later_hi, later_lo):
                            mm = nc.tensor.matmul(z[:, u % 3, before:512], neg_ones[:, :], part[:, before:512],
                                                  start=False, stop=True, skip_group_check=True)
                    mm.then_inc(s["sums_added"], 1)

                def values(j, u):
                    half, kb, first = UNITS[u]
                    pe.wait_ge(s["exp_done"], j * NU + u + 1 + 1)
                    if unit_is_diagonal(u):
                        pe.wait_ge(s["prob_ready"], j * NDIAG + DIAG_BEFORE[u] + 1)
                    nc.tensor.matmul(y[:, half, first:512], v_tok[:, kb, :], prob[:, u % 2, first:512],
                                     start=unit_is_first(u), stop=(kb == 0), skip_group_check=True)\
                        .then_inc(s["av_done"], 1)

                pe.wait_ge(s["consts_ready"], 1)
                with pe.Fori(0, H) as j:
                    for slot in range(SLOTS + 3):
                        if slot < SLOTS:
                            b, c = divmod(slot, NCH)
                            project_chunk(k, pe, base + j * NB + b, b % 2, c, k.x_hi, k.x_lo)
                        if slot == 0:
                            turn_kv(j)
                        if 0 <= slot - 1 < NU:
                            scores(j, slot - 1)
                        if 0 <= slot - 2 < NU:
                            sums(j, slot - 2)
                        if 0 <= slot - 3 < NU:
                            values(j, slot - 3)
                pe.wait_ge(s["conv_ready"], H + 1)
                for h in range(H):
                    tr = nc.tensor.transpose(z[0:2 + B, 0, h * P:(h + 1) * P], tails[:, h, :], k.ident[:, :])
                tr.then_inc(s["tails_turned"], 1)

            @block.scalar
            def _(act):
                act.sem_inc(s["exp_done"], 1)
                for n in ("v_out", "k_out", "vd_out", "kd_out", "gate_sent", "conv_sent", "y_sent"):
                    act.sem_inc(s[n], 16)
                act.preload_act_table_set(EXP_LN)

                def softplus_log(j, u):
                    _, _, first = UNITS[u]
                    act.wait_ge(s["z_ready"], j * NU + u + 1 + 1)
                    if u >= 2:
                        act.wait_ge(s["sp_split"], j * NU + u - 1)
                        act.wait_ge(s["later_ready"], j * NU + u)
                    else:
                        act.wait_ge(s["later_ready"], j * NU + 1)
                    nc.scalar.activation(z_abs[:, u % 2, first:512], z[:, u % 3, first:512], ACT.Abs,
                                         bias=bias[:, :]).then_inc(s["abs_ready"], 1)
                    act.wait_ge(s["abs_ready"], j * NU + u + 1)
                    nc.scalar.activation(z_abs[:, u % 2, first:512], z_abs[:, u % 2, first:512], ACT.Exp,
                                         scale=-1.0).then_inc(s["exp_ready"], 1)
                    act.wait_ge(s["exp_ready"], j * NU + u + 1)
                    nc.scalar.activation(z_abs[:, u % 2, first:512], z_abs[:, u % 2, first:512], ACT.Ln,
                                         bias=1.0).then_inc(s["log_ready"], 1)

                def probs(j, u):
                    _, _, first = UNITS[u]
                    act.wait_ge(s["sums_added"], j * NU + u + 1)
                    if u >= 2:
                        act.wait_ge(s["av_done"], j * NU + u - 1 + 1)
                    nc.scalar.activation(prob[:, u % 2, first:512], z[:, u % 3, first:512], ACT.Exp,
                                         bias=bias[:, :]).then_inc(s["exp_done"], 1)

                with act.Fori(0, H) as j:
                    act.wait_ge(s["z_ready"], j * NU + 1)
                    nc.scalar.activation(k_head[:, :].unsqueeze(1), s_T[:, bass.ds(j + H, 1), :], ACT.Copy)
                    act.wait_ge(s["conv_ready"], j + 1)
                    nc.scalar.activation(v_head[:, :].unsqueeze(1), s_T[:, bass.ds(j + 2 * H, 1), :], ACT.Copy)\
                      .then_inc(s["staged"], 1)
                    for slot in range(SLOTS + 2):
                        if slot < SLOTS:
                            b, c = divmod(slot, NCH)
                            if slot == 0:
                                act.wait_ge(s["cx_ready"], j + 1)
                            if slot == NCH:
                                act.wait_ge(s["conv_sent"], j * 16 + 16)
                            if slot == 2 * NCH:
                                act.wait_ge(s["conv_ready"], j + 1)
                            if slot == 3 * NCH:
                                act.wait_ge(s["gate_sent"], j * 16 + 16)
                            acc_wait(k, act, base + j * NB + b, c)
                            nc.scalar.activation(proj[:, b, c * CW:(c + 1) * CW], k.acc[:, c, 0:CW], ACT.Copy)\
                              .then_inc(k.acc_free, 1)
                        if slot == 0:
                            act.wait_ge(s["kv_turned"], j + 1)
                            act.wait_ge(s["v_out"], j * 16 + 16)
                            act.wait_ge(s["av_done"], j * NU + 1)
                            nc.scalar.activation(v_tok[:, :, :], z[:, 0:2, :].rearrange("p a (b d) -> p (a b) d", d=P),
                                                 ACT.Copy).then_inc(s["v_ready"], 1)
                            act.wait_ge(s["v_ready"], j + 1)
                            act.dma_start(io["v_prompt"][0, 0, :, bass.ds(j, 1), :].rearrange("(b p) o d -> p (b o) d", p=P),
                                          v_tok[:, :, :]).then_inc(s["v_out"], 16)
                            act.wait_ge(s["kv_ready"], j + 1)
                            act.dma_start(io["k_prompt"][0, 0, :, bass.ds(j, 1), :].rearrange("(b p) o d -> p (b o) d", p=P),
                                          k_tok[:, :, :]).then_inc(s["k_out"], 16)
                            act.dma_start(io["v_sample"][0, :, 0, bass.ds(j, 1), :].rearrange("b o d -> b (o d)"),
                                          kv_dec[:, 0, :]).then_inc(s["vd_out"], 16)
                            act.dma_start(io["k_sample"][0, :, 0, bass.ds(j, 1), :].rearrange("b o d -> b (o d)"),
                                          kv_dec[:, 1, :]).then_inc(s["kd_out"], 16)
                        if 0 <= slot - 1 < NU:
                            softplus_log(j, slot - 1)
                        if 0 <= slot - 2 < NU:
                            probs(j, slot - 2)
                    act.wait_ge(k.acc_free, (base + j * NB + NB) * NCH + NCH)
                    act.dma_start(k.gates[:, bass.ds(j, 1), :], proj[:, 3:4, :]).then_inc(s["gate_sent"], 16)
                    act.wait_ge(s["conv_ready"], j + 1 + 1)
                    act.dma_start(k.branch[1, :, bass.ds(j, 1), :], proj[:, 1:2, :]).then_inc(s["conv_sent"], 16)
                    act.wait_ge(s["y_read"], j * 2 + 2 + 1)
                    act.dma_start(k.branch[2, :, bass.ds(j, 1), 0:T], y_out[:, :].unsqueeze(1)).then_inc(s["y_sent"], 16)
                for n in ("v_out", "k_out", "vd_out", "kd_out", "gate_sent", "conv_sent", "y_sent"):
                    act.wait_ge(s[n], 16 * H + 16)

            @block.vector
            def _(dve):
                dve.sem_inc(s["y_read"], 1)
                dve.sem_inc(s["sp_ready"], 1)
                dve.sem_inc(s["cx_ready"], 1)
                dve.sem_inc(s["conv_ready"], 1)
                nc.vector.memset(cx[:, 0:2], 0.0)
                nc.vector.tensor_copy(neg_from[:, :], k.neg_from[:, :])
                nc.vector.tensor_copy(neg_ones[:, :], k.neg_ones[:, :]).then_inc(s["consts_ready"], 1)

                def softplus_parts(j, u):
                    _, _, first = UNITS[u]
                    dve.wait_ge(s["abs_ready"], j * NU + u + 1)
                    nc.vector.tensor_scalar(z_pos[:, first:512], z[:, u % 3, first:512], bias[:, :], 0.0,
                                            ALU.add, ALU.max).then_inc(s["z_read"], 1)

                def softplus_sum(j, u):
                    _, _, first = UNITS[u]
                    dve.wait_ge(s["log_ready"], j * NU + u + 1)
                    dve.wait_ge(s["z_read"], j * NU + u + 1)
                    nc.vector.tensor_tensor(sp_[:, u % 2, first:512], z_pos[:, first:512], z_abs[:, u % 2, first:512],
                                            ALU.add)
                    if unit_is_diagonal(u):
                        dve.drain()
                        nc.vector.tensor_tensor(sp_[:, u % 2, first:first + P], sp_[:, u % 2, first:first + P],
                                                k.before[:, :], ALU.mult).then_inc(s["sp_ready"], 1)
                    else:
                        dve.drain().then_inc(s["sp_ready"], 1)

                def split_softplus(j, u):
                    _, _, first = UNITS[u]
                    if u >= 2:
                        dve.wait_ge(s["sums_added"], j * NU + u - 1)
                    dve.wait_ge(s["sp_ready"], j * NU + u + 1 + 1)
                    nc.vector.tensor_copy(sp_hi[:, u % 2, first:512], sp_[:, u % 2, first:512]).then_inc(s["sp_rounded"], 1)
                    dve.wait_ge(s["sp_rounded"], j * NU + u + 1)
                    nc.vector.tensor_tensor(sp_lo[:, u % 2, first:512], sp_[:, u % 2, first:512],
                                            sp_hi[:, u % 2, first:512].bitcast(F32), ALU.subtract).then_inc(s["sp_split"], 1)

                def convolve(j, tap):
                    weight = k.conv_w[:, tap, bass.ds(j, 1)]
                    if tap == 2:
                        dve.wait_ge(s["cx_ready"], j + 1 + 1)
                        nc.vector.tensor_scalar(conv[:, :], cx[:, 2:2 + TT], weight, None, ALU.mult)
                        nc.vector.tensor_copy(tails[:, bass.ds(j, 1), :], cx[:, T:T + 2 + B].unsqueeze(1))
                    else:
                        nc.vector.scalar_tensor_tensor(out=conv[:, 0:T], in0=cx[:, tap:tap + T], scalar=weight,
                                                       in1=conv[:, 0:T], op0=ALU.mult, op1=ALU.add)
                        nc.vector.scalar_tensor_tensor(out=conv[:, T:TT], in0=k.conv_state[:, bass.ds(j, 1), tap::2].squeeze(1),
                                                       scalar=weight, in1=conv[:, T:TT], op0=ALU.mult, op1=ALU.add)
                    dve.drain()

                def read_y(j, half):
                    u = 4 if half == 0 else NU
                    dve.wait_ge(s["av_done"], j * NU + u + 1)
                    nc.vector.tensor_copy(y_out[:, half * 512:(half + 1) * 512], y[:, half, :]).then_inc(s["y_read"], 1)

                with dve.Fori(0, H) as j:
                    dve.wait_ge(s["exp_done"], j * NU + 1)
                    nc.vector.tensor_copy(bias[:, :], k.b_sb[:, bass.ds(j, 1)]).then_inc(s["bias_ready"], 1)
                    dve.wait_ge(s["bias_ready"], j + 1)
                    dve.wait_ge(s["kv_turned"], j + 1)
                    dve.wait_ge(s["k_out"], j * 16 + 16)
                    dve.wait_ge(s["vd_out"], j * 16 + 16)
                    dve.wait_ge(s["kd_out"], j * 16 + 16)
                    nc.vector.tensor_copy(k_tok[:, :, :], y[:, :, :].rearrange("p a (b d) -> p (a b) d", d=P))
                    nc.vector.tensor_copy(kv_dec[:, :, :], z[0:B, 2, 0:2 * P].rearrange("p (a d) -> p a d", d=P))\
                      .then_inc(s["kv_ready"], 1)
                    for u in range(NU):
                        softplus_parts(j, u)
                        softplus_sum(j, u)
                        split_softplus(j, u)
                        if u == 6:
                            dve.wait_ge(s["y_sent"], j * 16 + 16)
                            read_y(j, 0)
                        if u == 8:
                            dve.wait_ge(k.acc_free, (base + j * NB + 2) * NCH + NCH)
                            nc.vector.tensor_tensor(cx[:, 2:2 + TT], proj[:, 0, :], proj[:, 1, :],
                                                    ALU.mult).then_inc(s["cx_ready"], 1)
                        if u > 8:
                            convolve(j, 11 - u)
                    dve.wait_ge(k.acc_free, (base + j * NB + 3) * NCH + NCH)
                    nc.vector.tensor_tensor(conv[:, :], conv[:, :], proj[:, 2, :], ALU.mult).then_inc(s["conv_ready"], 1)
                    read_y(j, 1)
                dve.wait_ge(s["tails_turned"], 1)
                dve.wait_ge(s["av_done"], H * NU + 1)
                nc.vector.tensor_copy(tail_rows[:, :], z[0:2 + B, 0, :]).then_inc(s["tails_ready"], 1)

            @block.gpsimd
            def _(pool):
                pool.sem_inc(s["later_ready"], 1)
                def add_later(j, u):
                    _, _, first = UNITS[u]
                    pool.wait_ge(s["sp_ready"], j * NU + u + 1 + 1)
                    pool.wait_ge(s["later_ready"], j * NU + u + 1)
                    before = 512 if unit_is_first(u) else UNITS[u - 1][2]
                    if first < before:
                        pool.sem_inc(k.pool_tick, 1)
                        op = nc.gpsimd.tensor_scalar(later[:, first:before], sp_[:, u % 2, first:before], 1.0, 1.0,
                                                     ALU.mult, ALU.mult)
                    if before < 512:
                        op = nc.gpsimd.tensor_tensor(later[:, before:512], later[:, before:512],
                                                     sp_[:, u % 2, before:512], ALU.add)
                    op.then_inc(s["later_ready"], 1)

                def split_later(j, u):
                    _, _, first = UNITS[u]
                    if HAS_NEXT[u]:
                        pool.wait_ge(s["later_ready"], j * NU + u + 1 + 1)
                        if u == 0:
                            pool.wait_ge(s["av_done"], j * NU + 1)
                        else:
                            pool.wait_ge(s["sums_added"], j * NU + (u if unit_is_first(u) else u + 1))
                        pool.sem_inc(k.pool_tick, 1)
                        nc.gpsimd.tensor_scalar(later_hi[:, first:512], later[:, first:512], 1.0, 1.0,
                                                ALU.mult, ALU.mult).then_inc(s["later_rounded"], 1)
                        pool.drain()
                        nc.gpsimd.tensor_tensor(later_lo[:, first:512], later[:, first:512],
                                                later_hi[:, first:512].bitcast(F32), ALU.subtract).then_inc(s["later_split"], 1)

                def mask_prob(j, u):
                    _, _, first = UNITS[u]
                    pool.wait_ge(s["exp_done"], j * NU + u + 1 + 1)
                    pool.sem_inc(k.pool_tick, 1)
                    nc.gpsimd.affine_select(out=prob[:, u % 2, first:first + P], in_=prob[:, u % 2, first:first + P],
                                            compare_op=ALU.is_gt, fill=0.0, base=0, pattern=[[1, P]],
                                            channel_multiplier=-1).then_inc(s["prob_ready"], 1)

                with pool.Fori(0, H) as j:
                    for slot in range(SLOTS + 2):
                        if slot % NCH == 0 and slot < SLOTS:
                            b = slot // NCH + 1
                            split_weights(k, pool, base + j * NB + b, b % 2, base // 2 + j * (NB // 2) + b // 2)
                        if 0 <= slot - 1 < NU:
                            add_later(j, slot - 1)
                        if 0 <= slot - 2 < NU and unit_is_diagonal(slot - 2):
                            mask_prob(j, slot - 2)
                        if 0 <= slot - 1 < NU:
                            split_later(j, slot - 1)
    k.blocks = base + H * NB


N_E = 4
E_STATE, E_NEGM, E_KEY, E_DECAY = range(N_E)
GATE_COLS = TB * H


def project_mlstm(k, m_T, groups, then):
    nc, io = k.nc, k.io
    base = k.blocks
    old_sems = list(k.phase_sems)
    N = B * PAGES * H
    HALF = PAGES // 2
    FIRST_GATE = 5 * H
    w_in = io["w_in"].rearrange("l (k p) n -> p (l k) n", p=P)
    with ExitStack() as ctx:
        gate_out = k.sb(ctx, "mp_gate_out", [P, 2, TT])
        table = k.sb(ctx, "pages", [1, B * PAGES], I32)
        page = k.sb(ctx, "page", [P, RING, W])
        q_own = k.sb(ctx, "q_own", [B, W])
        prod = k.sb(ctx, "qk_prod", [P, 2, W])
        z = k.sb(ctx, "dec_z", [P, B, PAGES, H])
        z_abs = k.sb(ctx, "dec_z_abs", [P, B, PAGES, H])
        sp_ = k.sb(ctx, "dec_sp", [P, B, PAGES, H])
        later = k.sb(ctx, "dec_later", [P, B, PAGES, H])
        q_row = k.ps(ctx, "q_row", [P, W])
        w_if = k.sb(ctx, "w_if", [P, KD, 2 * H])
        w_if2 = k.sb(ctx, "w_if2", [P, KD, 2, 2 * H], F32R)
        raw = k.sb(ctx, "if_raw", [P, TB + 1, 2 * H])
        f_abs = k.sb(ctx, "f_abs", [P, TB, H])
        log_f = k.sb(ctx, "log_f", [P, TB, H])
        total = k.sb(ctx, "log_f_total", [P, TB, H])
        b_sum = k.sb(ctx, "b_sum", [P, TB, H])
        spread = k.sb(ctx, "g_spread", [P, 2, H, P])
        junk = k.sb(ctx, "max_junk", [P, P])
        g_max = k.sb(ctx, "g_max", [P, TB, H])
        mu_last = k.sb(ctx, "mu_last", [P, TB, H])
        m_prev = k.sb(ctx, "m_prev", [P, TB + 1, H])
        sums = k.ps(ctx, "sums_ps", [P, 512])
        g_rows = k.ps(ctx, "g_rows", [P, 2, 512])
        by_gate = k.ps(ctx, "if_by_gate", [4 * H, 512])
        if_rows = k.sb(ctx, "if_rows", [4 * H, TT])
        gp = sums[:, 256:256 + (TB + 1) * 2 * H].rearrange("p (t g) -> p t g", g=2 * H)
        s = {n: k.sem(ctx, "mp_" + n) for n in (
            "table_in", "own_ready", "rows_ready", "multiplied", "reduced", "z_ready", "z_log_ready", "sp_ready",
            "z_summed", "arg_ready",
            "w_in", "w_ready", "if_ready", "if_read", "projected", "raw_ready", "log_ready", "log_f_ready", "summed", "spread_ready",
            "g_rows_ready", "g_rows_read", "exps_in", "m_out")}
        gate_sent = [k.sem(ctx, f"mp_gate_sent{b}") for b in range(2)]
        landed = [k.sem(ctx, f"k_page_landed{i}") for i in range(RING)]
        flat = "p b g h -> p (b g h)"
        MQ, MK, MV, MO, GATES = range(5)
        order = groups + [dict(col=C_G + FIRST_GATE * P, out=None, scale=1.0, func=ACT.Copy)]

        with nc.Block() as block:
            def walk(eng, step, after, straight=()):
                for gi, g in enumerate(order):
                    n = base + gi * H
                    if gi in straight:
                        for b in range(H):
                            step(gi, g, n + b, b % 2, (n + b) // 2, b, b // 2 + gi * 2)
                        after(gi)
                        continue
                    with eng.Fori(0, H // 2) as i:
                        for par in range(2):
                            step(gi, g, n + i * 2 + par, par, n // 2 + i, i * 2 + par, i + gi * 2)
                    after(gi)

            @block.sync
            def _(sp):
                sp.dma_start(table[:, :], io["page_table"].rearrange("b g -> (b g)").unsqueeze(0)).then_inc(s["table_in"], 16)
                sp.dma_start(w_if[:, :, :], w_in[:, :, C_IF:C_IF + 2 * H],
                             allow_slow_non_contiguous=True).then_inc(s["w_in"], 16)
                sp.wait_ge(s["table_in"], 16)

                def load(n, par, b, first=C_MQ):
                    load_weights(k, sp, n, par, w_in[:, :, bass.ds(b * P + first, P)])

                def pages(q, half):
                    load_pages(k, sp, table, q, half, io["cache_k"], page, s["multiplied"], landed)

                with sp.Fori(0, B - 1) as q:
                    load(base + q * 2 + 1, 1, q * 2 + 1)
                    pages(q, 0)
                    load(base + q * 2 + 2, 0, q * 2 + 2)
                    pages(q, 1)
                load(base + 2 * B - 1, 1, 2 * B - 1)
                pages(B - 1, 0)
                load(base + 2 * B, 0, 0, C_G + FIRST_GATE * P)
                pages(B - 1, 1)
                for b in range(1, H):
                    load(base + 2 * B + b, b % 2, b, C_G + FIRST_GATE * P)
                load_weights(k, sp, base + 5 * H, 0, then)
                sp.wait_ge(s["exps_in"], 1)
                sp.dma_start(io["m_prompt"].rearrange("l b h -> (l b) h"), m_prev[0:1, TB, :]).then_inc(s["m_out"], 16)
                sp.wait_ge(s["m_out"], 16)

            @block.gpsimd
            def _(pool):
                k.clear_semaphores(pool, old_sems)
                split_ahead(k, pool, base, 5 * H)

            @block.tensor
            def _(pe):
                pe.sem_inc(s["rows_ready"], 1)
                def step(gi, g, n, par, pair, b, q):
                    for c in range(NCH):
                        project_chunk(k, pe, n, par, c, k.x_hi, k.x_lo)
                        if gi < GATES and par == 0 and c == 1:
                            pe.wait_ge(s["own_ready"], q + 1)
                            pe.wait_ge(s["multiplied"], q * PAGES + RING)
                            nc.tensor.matmul(q_row[:, :], k.ones[0:B, :], q_own[:, :], start=True, stop=True)\
                                .then_inc(s["rows_ready"], 1)
                        if gi == MO and c != 1:
                            t = b * 2 + c // 2
                            pe.wait_ge(s["spread_ready"], t + 1)
                            pe.wait_ge(s["g_rows_read"], t + 1)
                            nc.tensor.matmul(g_rows[:, c // 2, :], k.ones[:, :], spread[:, c // 2, :, :],
                                             start=True, stop=True).then_inc(s["g_rows_ready"], 1)

                def after(gi):
                    if gi == MQ:
                        pe.wait_ge(s["w_ready"], 1)
                        for c in range(NCH):
                            cols = slice(c * CW, (c + 1) * CW)
                            if c:
                                pe.wait_ge(s["if_read"], c)
                            for i in range(KD):
                                nc.tensor.matmul(by_gate[:, 0:CW], w_if2[:, i, :, :], k.x_hi[:, i, cols],
                                                 start=(i == 0), stop=False, skip_group_check=True)
                                mm = nc.tensor.matmul(by_gate[0:2 * H, 0:CW], w_if2[:, i, 0, :], k.x_lo[:, i, cols],
                                                      start=False, stop=(i == KD - 1), skip_group_check=True)
                            mm.then_inc(s["if_ready"], 1)
                        pe.wait_ge(s["if_read"], NCH)
                        for tb in range(TB + 1):
                            m = P if tb < TB else B
                            mm = nc.tensor.matmul(gp[0:m, tb, :], if_rows[:, tb * P:tb * P + m], k.two_idents[:, :],
                                                  start=True, stop=True)
                        mm.then_inc(s["projected"], 1)
                    if gi == MV:
                        pe.wait_ge(s["log_f_ready"], 1)
                        lf = log_f[:, :, :].rearrange("p c h -> p (c h)")
                        nc.tensor.matmul(sums[:, 0:GATE_COLS], k.sum_to[:, :], lf, start=True, stop=True)
                        nc.tensor.matmul(sums[:, GATE_COLS:2 * GATE_COLS], k.ones[:, :], lf, start=True, stop=True)\
                            .then_inc(s["summed"], 1)
                    if gi == GATES:
                        pe.wait_ge(s["sp_ready"], 1)
                        nc.tensor.matmul(sums[:, 0:N], k.neg_from[:, :], sp_[:, :, :, :].rearrange(flat), start=True, stop=False)
                        nc.tensor.matmul(sums[:, 0:N], k.neg_ones[:, :], later[:, :, :, :].rearrange(flat),
                                         start=False, stop=True).then_inc(s["z_summed"], 1)

                walk(pe, step, after)

            @block.scalar
            def _(act):
                for par in range(2):
                    act.sem_inc(gate_sent[par], 16)

                def step(gi, g, n, par, pair, b, q):
                    to_dram = gi == GATES
                    if to_dram:
                        act.wait_ge(gate_sent[par], (b - par) * 8 + 16)
                    out = gate_out[:, par:par + 1, :] if to_dram else g["out"](b)
                    for c in range(NCH):
                        acc_wait(k, act, n, c)
                        nc.scalar.activation(out[:, :, c * CW:(c + 1) * CW], k.acc[:, c:c + 1, 0:CW],
                                             g["func"], scale=g["scale"]).then_inc(k.acc_free, 1)
                    if to_dram:
                        act.wait_ge(k.acc_free, (n + 1) * NCH + NCH)
                        act.dma_start(k.gates[:, bass.ds(b + FIRST_GATE, 1), :], out).then_inc(gate_sent[par], 16)

                def log_of(t):
                    for func, scale, bias in ((ACT.Abs, 1.0, 0.0), (ACT.Exp, -1.0, 0.0), (ACT.Ln, 1.0, 1.0)):
                        op = nc.scalar.activation(t[1], t[0] if func == ACT.Abs else t[1], func, scale=scale, bias=bias)
                        if func != ACT.Ln:
                            act.drain()
                    return op

                def after(gi):
                    if gi == MQ:
                        for c in range(NCH):
                            act.wait_ge(s["if_ready"], c + 1)
                            nc.scalar.activation(if_rows[:, c * CW:(c + 1) * CW], by_gate[:, 0:CW], ACT.Copy)\
                              .then_inc(s["if_read"], 1)
                    if gi == MK:
                        act.preload_act_table_set(EXP_LN)
                        act.wait_ge(s["raw_ready"], 1)
                        log_of((raw[:, 0:TB, H:2 * H], f_abs[:, :, :])).then_inc(s["log_ready"], 1)
                    if gi == MO:
                        act.preload_act_table_set(EXP_LN)
                        act.wait_ge(s["exps_in"], 1)
                        nc.scalar.activation(k.exps[:, :, :, :], k.exps[:, :, :, :], ACT.Exp)
                        act.wait_ge(s["z_ready"], 1)
                        log_of((z[:, :, :, :].rearrange(flat), z_abs[:, :, :, :].rearrange(flat))).then_inc(s["z_log_ready"], 1)
                    if gi == GATES:
                        act.wait_ge(s["arg_ready"], 1)
                        nc.scalar.activation(k.dec_prob[:, :, :, :].rearrange(flat), z_abs[:, :, :, :].rearrange(flat), ACT.Exp)

                walk(act, step, after)
                for par in range(2):
                    act.wait_ge(gate_sent[par], H // 2 * 16 + 16)

            @block.vector
            def _(dve):
                dve.sem_inc(s["reduced"], 1)
                dve.sem_inc(s["multiplied"], RING)
                dve.sem_inc(s["g_rows_read"], 2)
                dve.wait_ge(s["w_in"], 16)
                nc.vector.tensor_copy(w_if2[:, :, 0, :], w_if[:, :, :])
                nc.vector.memset(m_prev[:, 0, :], 0.0)
                dve.drain()
                nc.vector.tensor_tensor(w_if2[:, :, 1, :], w_if[:, :, :], w_if2[:, :, 0, :].bitcast(F32),
                                        ALU.subtract).then_inc(s["w_ready"], 1)

                def spread_g(t, par):
                    nc.vector.tensor_tensor(spread[:, par, :, :], k.ident[:, :].unsqueeze(1).to_broadcast([P, H, P]),
                                            k.g_col[:, bass.ds(t, 1), :].squeeze(1).unsqueeze(2).to_broadcast([P, H, P]),
                                            ALU.mult).then_inc(s["spread_ready"], 1)

                def maxima(t, par):
                    dve.wait_ge(s["g_rows_ready"], t + 1)
                    rows = g_rows[:, par, :].rearrange("p (h t) -> p h t", h=H)
                    nc.vector.tensor_reduce(g_max[:, bass.ds(t, 1), :].squeeze(1), rows, AX.X, ALU.max)
                    for h in range(H):
                        dve.drain()
                        nc.vector.tensor_tensor_reduce(junk[:, :], rows[:, h, :], k.late_neg[:, :], 1.0, -3.0e38,
                                                       ALU.add, ALU.max, k.mu[:, t, h:h + 1])
                    dve.drain().then_inc(s["g_rows_read"], 1)

                def step(gi, g, n, par, pair, b, q):
                    if gi == GATES:
                        return
                    if par == 0:
                        dve.wait_ge(s["rows_ready"], q + 1)
                        nc.vector.tensor_scalar(q_own[:, :], k.q_tok[:, :], k.ident[0:B, bass.ds(q, 1)], None, ALU.mult)\
                          .then_inc(s["own_ready"], 1)
                    if gi == MO:
                        for e in range(2):
                            spread_g(b * 2 + e, e)
                    if par == 0:
                        dve.wait_ge(s["rows_ready"], q + 1 + 1)
                    for j in range(HALF):
                        p_ = par * HALF + j
                        dve.wait_ge(landed[p_ % RING], q * (PAGES // RING * 16) + (p_ // RING + 1) * 16)
                        dve.wait_ge(s["reduced"], q * PAGES + max(p_ - 1, 0) + 1)
                        nc.vector.tensor_tensor(prod[:, p_ % 2, :], page[:, p_ % RING, :], q_row[:, :],
                                                ALU.mult).then_inc(s["multiplied"], 1)
                        dve.wait_ge(s["multiplied"], q * PAGES + p_ + 1 + RING)
                        nc.vector.tensor_reduce(z[:, bass.ds(q, 1), p_, :].squeeze(1),
                                                prod[:, p_ % 2, :].rearrange("p (h d) -> p h d", h=H), AX.X, ALU.add)\
                          .then_inc(s["reduced"], 1)
                        if gi == MO and j % 2 == 1:
                            maxima(b * 2 + j // 2, j // 2)

                def after(gi):
                    if gi == MK:
                        dve.wait_ge(s["projected"], 1)
                        nc.vector.tensor_tensor(raw[:, 0:TB, :], gp[:, 0:TB, :],
                                                k.b_if[:, :].unsqueeze(1).to_broadcast([P, TB, 2 * H]), ALU.add)
                        nc.vector.tensor_tensor(k.gates_dec[:, :], gp[0:B, TB, :], k.b_if[0:B, :], ALU.add)
                        dve.drain().then_inc(s["raw_ready"], 1)
                        nc.vector.tensor_scalar(total[:, :, :], raw[:, 0:TB, H:2 * H], -1.0, 0.0, ALU.mult, ALU.max)
                        dve.drain()
                        dve.wait_ge(s["log_ready"], 1)
                        nc.vector.scalar_tensor_tensor(out=log_f[:, :, :], in0=total[:, :, :], scalar=-1.0, in1=f_abs[:, :, :],
                                                       op0=ALU.mult, op1=ALU.subtract).then_inc(s["log_f_ready"], 1)
                    if gi == MV:
                        dve.wait_ge(s["summed"], 1)
                        dve.wait_ge(s["log_f_ready"], 1)
                        nc.vector.tensor_copy(b_sum[:, :, :], sums[:, 0:GATE_COLS].rearrange("p (c h) -> p c h", h=H))
                        nc.vector.tensor_copy(total[:, :, :], sums[:, GATE_COLS:2 * GATE_COLS].rearrange("p (c h) -> p c h", h=H))
                        dve.drain()
                        nc.vector.tensor_tensor(k.g_col[:, :, :], raw[:, 0:TB, 0:H], b_sum[:, :, :], ALU.subtract)
                        dve.drain()
                    if gi == MO:
                        for c in range(TB):
                            nc.vector.tensor_tensor(mu_last[:, c, :], m_prev[:, c, :], g_max[:, c, :], ALU.max)
                            dve.drain()
                            nc.vector.tensor_tensor(m_prev[:, c + 1, :], total[:, c, :], mu_last[:, c, :], ALU.add)
                            dve.drain()
                        nc.vector.tensor_tensor(k.mu[:, :, :], k.mu[:, :, :], m_prev[:, 0:TB, :], ALU.max)
                        dve.drain()
                        nc.vector.tensor_tensor(k.exps[:, E_STATE, :, :], m_prev[:, 0:TB, :], k.mu[:, :, :], ALU.subtract)
                        nc.vector.scalar_tensor_tensor(out=k.exps[:, E_NEGM, :, :], in0=b_sum[:, :, :], scalar=-1.0,
                                                       in1=k.mu[:, :, :], op0=ALU.mult, op1=ALU.subtract)
                        nc.vector.tensor_tensor(k.exps[:, E_KEY, :, :], k.g_col[:, :, :], mu_last[:, :, :], ALU.subtract)
                        nc.vector.tensor_tensor(k.exps[:, E_DECAY, :, :], m_prev[:, 0:TB, :], mu_last[:, :, :], ALU.subtract)
                        dve.drain().then_inc(s["exps_in"], 1)
                        dve.wait_ge(s["reduced"], B * PAGES + 1)
                        bias = k.b_sb[:, :].unsqueeze(1).to_broadcast([P, B * PAGES, H])
                        zf = z[:, :, :, :].rearrange("p b g h -> p (b g) h")
                        nc.vector.tensor_tensor(zf, zf, bias, ALU.add).then_inc(s["z_ready"], 1)
                        dve.wait_ge(s["z_log_ready"], 1)
                        dve.wait_ge(s["z_ready"], 1)
                        fz, fs, fa = (t[:, :, :, :].rearrange(flat) for t in (z, sp_, z_abs))
                        nc.vector.scalar_tensor_tensor(out=fs, in0=fz, scalar=0.0, in1=fa, op0=ALU.max, op1=ALU.add)
                        nc.vector.memset(later[:, :, PAGES - 1, :], 0.0)
                        for g in range(PAGES - 2, -1, -1):
                            dve.drain()
                            nc.vector.tensor_tensor(later[:, :, g, :], later[:, :, g + 1, :], sp_[:, :, g + 1, :], ALU.add)
                        dve.drain().then_inc(s["sp_ready"], 1)
                        dve.wait_ge(s["z_summed"], 1)
                        nc.vector.tensor_tensor(fa, fz, sums[:, 0:N], ALU.add).then_inc(s["arg_ready"], 1)

                walk(dve, step, after, straight=(MO,))
    k.blocks = base + 5 * H
    k.release_cleared()


def load_pages(k, sp, table, q, half, cache, page, used, landed):
    for j in range(PAGES // 2):
        p_ = half * (PAGES // 2) + j
        number = sp.value_load(table[0:1, bass.ds(q * PAGES + p_, 1)], min_val=0, max_val=N_PHYS - 1)
        sp.wait_ge(used, q * PAGES + p_ + 1)
        sp.dma_start(page[:, p_ % RING, :], cache[0, bass.ds(number, 1), :, :, :].rearrange("a t h d -> (a t) (h d)"))\
          .then_inc(landed[p_ % RING], 16)


def mlstm_prompt(k, m_T, then):
    nc, io = k.nc, k.io
    base = k.blocks
    NB, FIRST_GATE = 2, H
    SLOTS = NB * NCH
    S_, M_, K_, V_, X_ = range(5)
    INTER, INTRA, STATE = (X_, K_), (M_, V_), (S_, X_)
    TURNED = K_
    w_in = io["w_in"].rearrange("l (k p) n -> p (l k) n", p=P)
    V1 = P + 1
    with ExitStack() as ctx:
        qkv = k.sb(ctx, "qkv", [P, 3, H, P])
        spread = k.sb(ctx, "mu_spread", [P, H, P])
        expo = k.sb(ctx, "expo", [P, H, P])
        w_T = k.sb(ctx, "w_T", [P, H, P])
        v_one = k.sb(ctx, "v_one", [P, H, V1])
        k_w = k.sb(ctx, "k_weighed", [P, H, P])
        inter = k.sb(ctx, "inter", [P, H, V1])
        num = k.sb(ctx, "num", [P, H, V1])
        den = k.sb(ctx, "den", [P, 3, H])
        h_tok = k.sb(ctx, "h_tok", [P, H, P])
        y_m = k.sb(ctx, "y_m", [P, H, P])
        state = k.sb(ctx, "state", [P, H, V1])
        gate_out = k.sb(ctx, "gate_out", [P, NB, TT])
        table = k.sb(ctx, "v_pages", [1, B * PAGES], I32)
        page = k.sb(ctx, "v_page", [P, RING, W])
        y_dec = k.sb(ctx, "y_dec_s", [P, H, B])
        v_sum = k.sb(ctx, "v_sum", [P, H, P])
        y = k.acc[:, 0, 512 - B * H:512].rearrange("p (b h) -> p b h", h=H)
        q = k.ps(ctx, "ml_ps", [P, 5, 512])
        s = {n: k.sem(ctx, "ml_" + n) for n in (
            "staged", "spread_ready", "pe1", "args_ready", "expo_ready", "weights_ready", "v_ready", "kw_ready", "pe2",
            "inter_ready", "num_ready", "h_ready", "pe3", "state_ready", "y_ready", "y_sent", "state_out",
            "table_in", "page_used", "weighed", "dec_summed", "dec_done", "dec_read", "dec_out")}
        landed = [k.sem(ctx, f"v_page_landed{i}") for i in range(RING)]
        gate_sent = [k.sem(ctx, f"gate_sent{b}") for b in range(NB)]

        def bank(i):
            return q[:, i, :].rearrange("p (h t) -> p h t", h=H)

        def pair(i):
            return q[:, i, 0:2 * V1].rearrange("p (h t) -> p h t", h=2)

        with nc.Block() as block:
            @block.sync
            def _(sp):
                sp.dma_start(table[:, :], io["page_table"].rearrange("b g -> (b g)").unsqueeze(0)).then_inc(s["table_in"], 16)
                sp.wait_ge(s["table_in"], 16)
                def pages(c, half):
                    load_pages(k, sp, table, c, half, io["cache_v"], page, s["page_used"], landed)

                def load(c, b, par):
                    load_weights(k, sp, base + c * NB + b, par, w_in[:, :, bass.ds((c * NB + b + FIRST_GATE) * P + C_G, P)])

                with sp.Fori(0, TB - 1) as c:
                    load(c, 1, 1)
                    pages(c, 0)
                    load(c, 2, 0)
                    pages(c, 1)
                load(TB - 1, 1, 1)
                pages(TB - 1, 0)
                load_weights(k, sp, base + TB * NB, 0, then, H)
                pages(TB - 1, 1)
                sp.wait_ge(s["dec_read"], 1)
                sp.dma_start(k.branch[2, :, :, T:TT], y_dec[:, :, :]).then_inc(s["dec_out"], 16)
                sp.wait_ge(s["state_ready"], TB + 1)
                sp.dma_start(io["C_prompt"][0, 0].rearrange("h d e -> d h e"), state[:, :, 0:P]).then_inc(s["state_out"], 16)
                sp.dma_start(io["n_prompt"][0, 0].rearrange("h d -> d h").unsqueeze(2), state[:, :, P:V1],
                             allow_slow_non_contiguous=True).then_inc(s["state_out"], 16)
                sp.wait_ge(s["state_out"], 32)
                sp.wait_ge(s["dec_out"], 16)

            @block.gpsimd
            def _(pool):
                split_ahead(k, pool, base, TB * NB, then_kb=H)

            @block.tensor
            def _(pe):
                pe.sem_inc(s["pe1"], 1)
                pe.sem_inc(s["pe2"], 1)
                pe.sem_inc(s["pe3"], 1)
                pe.sem_inc(s["dec_summed"], 1)
                def turn_and_score(c):
                    pe.wait_ge(s["staged"], c + 1)
                    pe.wait_ge(s["state_ready"], c + 1)
                    pe.wait_ge(s["y_ready"], c + 1)
                    pe.wait_ge(s["num_ready"], c + 1)
                    for h in range(H):
                        nc.tensor.matmul(bank(S_)[:, h, :], qkv[:, 1, h, :], qkv[:, 0, h, :], start=True, stop=True)
                    pe.wait_ge(s["spread_ready"], c + 1)
                    nc.tensor.matmul(q[:, M_, :], k.ones[:, :], spread[:, :, :], start=True, stop=True)
                    for h in range(H):
                        nc.tensor.transpose(bank(K_)[:, h, :], qkv[:, 1, h, :], k.ident[:, :])
                    for h in range(H):
                        tr = nc.tensor.transpose(bank(V_)[:, h, :], qkv[:, 2, h, :], k.ident[:, :])
                    tr.then_inc(s["pe1"], 1)

                def outputs(c):
                    pe.wait_ge(s["kw_ready"], c + 1)
                    for h in range(H):
                        nc.tensor.matmul(pair(INTER[h // 2])[:, h % 2, :], qkv[:, 0, h, :], state[:, h, :],
                                         start=True, stop=True)
                    pe.wait_ge(s["v_ready"], c + 1)
                    pe.wait_ge(s["weights_ready"], c + 1)
                    for h in range(H):
                        mm = nc.tensor.matmul(pair(INTRA[h // 2])[:, h % 2, :], w_T[:, h, :], v_one[:, h, :],
                                              start=True, stop=True)
                    mm.then_inc(s["pe2"], 1)

                def new_state(c):
                    pe.wait_ge(s["inter_ready"], c + 1)
                    for h in range(H):
                        nc.tensor.matmul(pair(STATE[h // 2])[:, h % 2, :], k_w[:, h, :], v_one[:, h, :],
                                         start=True, stop=True)
                    pe.wait_ge(s["h_ready"], c + 1)
                    for h in range(H):
                        tr = nc.tensor.transpose(bank(TURNED)[:, h, :], h_tok[:, h, :], k.ident[:, :])
                    tr.then_inc(s["pe3"], 1)

                def sum_values(c):
                    pe.wait_ge(s["weighed"], (c + 1) * PAGES)
                    pe.wait_ge(k.acc_free, (base + c * NB + 1) * NCH + 1)
                    for h in range(H):
                        mm = nc.tensor.matmul(y[:, bass.ds(c, 1), h], v_sum[:, h, :], k.ones[:, 0:1], start=True, stop=True)
                    mm.then_inc(s["dec_summed"], 1)

                with pe.Fori(0, TB) as c:
                    for slot in range(SLOTS):
                        b, ch = divmod(slot, NCH)
                        if slot == NCH:
                            sum_values(c)
                        project_chunk(k, pe, base + c * NB + b, b, ch, k.x_hi, k.x_lo)
                        if slot == 0:
                            turn_and_score(c)
                        if slot == 2:
                            outputs(c)
                        if slot == 4:
                            new_state(c)
                pe.drain().then_inc(s["dec_done"], 1)

            @block.scalar
            def _(act):
                act.sem_inc(s["expo_ready"], 1)
                act.sem_inc(s["y_sent"], 16)
                for b in range(NB):
                    act.sem_inc(gate_sent[b], 16)
                act.preload_act_table_set(EXP_LN)
                with act.Fori(0, TB) as c:
                    act.wait_ge(s["pe2"], c + 1)
                    nc.scalar.activation(qkv[:, :, :, :].rearrange("p a h t -> p (a h) t"),
                                         m_T[:, 0:3 * H, bass.ds(c * P, P)], ACT.Copy).then_inc(s["staged"], 1)
                    for slot in range(SLOTS):
                        b, ch = divmod(slot, NCH)
                        if ch == 0:
                            act.wait_ge(gate_sent[b], c * 16 + 16)
                        acc_wait(k, act, base + c * NB + b, ch)
                        nc.scalar.activation(gate_out[:, b, ch * CW:(ch + 1) * CW], k.acc[:, ch, 0:CW], ACT.Copy)\
                          .then_inc(k.acc_free, 1)
                        if ch == NCH - 1:
                            act.wait_ge(k.acc_free, (base + c * NB + b + 1) * NCH + NCH)
                            act.dma_start(k.gates[:, bass.ds(c * NB + b + FIRST_GATE, 1), :],
                                          gate_out[:, b:b + 1, :]).then_inc(gate_sent[b], 16)
                        if slot == 0:
                            act.wait_ge(s["pe1"], c + 1 + 1)
                            act.wait_ge(s["pe3"], c + 1)
                            nc.scalar.activation(v_one[:, :, 0:P], bank(V_), ACT.Copy).then_inc(s["v_ready"], 1)
                            for h in range(H):
                                op = nc.scalar.activation(k_w[:, h:h + 1, :], bank(K_)[:, h:h + 1, :], ACT.Copy,
                                                          scale=k.exps[:, E_KEY, bass.ds(c, 1), h])
                            op.then_inc(s["kw_ready"], 1)
                            act.wait_ge(s["args_ready"], c + 1)
                            nc.scalar.activation(expo[:, :, :], expo[:, :, :], ACT.Exp, scale=-1.0)\
                              .then_inc(s["expo_ready"], 1)
                        if slot == 2:
                            act.wait_ge(s["pe2"], c + 1 + 1)
                            act.wait_ge(s["num_ready"], c + 1)
                            for h in range(H):
                                op = nc.scalar.activation(inter[:, h, :], pair(INTER[h // 2])[:, h % 2, :], ACT.Copy,
                                                          scale=k.exps[:, E_STATE, bass.ds(c, 1), h])
                            op.then_inc(s["inter_ready"], 1)
                    act.wait_ge(s["y_ready"], c + 1 + 1)
                    act.dma_start(k.branch[0, :, :, bass.ds(c * P, P)], y_m[:, :, :]).then_inc(s["y_sent"], 16)
                act.wait_ge(s["y_sent"], TB * 16 + 16)
                for b in range(NB):
                    act.wait_ge(gate_sent[b], TB * 16 + 16)

            @block.vector
            def _(dve):
                dve.sem_inc(s["y_ready"], 1)
                dve.sem_inc(s["num_ready"], 1)
                nc.vector.memset(state[:, :, :], 0.0)
                nc.vector.memset(v_one[:, :, P:V1], 1.0)
                dve.drain().then_inc(s["state_ready"], 1)
                dve.sem_inc(s["page_used"], RING)

                def weigh_pages(c, half):
                    for g in range(half * (PAGES // 2), (half + 1) * (PAGES // 2)):
                        dve.wait_ge(landed[g % RING], c * (PAGES // RING * 16) + (g // RING + 1) * 16)
                        if g == 0:
                            dve.wait_ge(s["dec_summed"], c + 1)
                        for h in range(H):
                            values = page[:, g % RING, h * P:(h + 1) * P].unsqueeze(1)
                            weight = k.dec_prob[:, bass.ds(c, 1), g, h]
                            if g == 0:
                                nc.vector.tensor_scalar(v_sum[:, h:h + 1, :], values, weight, None, ALU.mult)
                            else:
                                nc.vector.scalar_tensor_tensor(out=v_sum[:, h:h + 1, :], in0=values, scalar=weight,
                                                               in1=v_sum[:, h:h + 1, :], op0=ALU.mult, op1=ALU.add)
                        dve.drain().then_inc(s["page_used"], 1)
                    dve.sem_inc(s["weighed"], PAGES // 2)

                with dve.Fori(0, TB) as c:
                    dve.wait_ge(s["pe1"], c + 1)
                    nc.vector.tensor_tensor(spread[:, :, :], k.ident[:, :].unsqueeze(1).to_broadcast([P, H, P]),
                                            k.mu[:, bass.ds(c, 1), :].squeeze(1).unsqueeze(2).to_broadcast([P, H, P]),
                                            ALU.mult).then_inc(s["spread_ready"], 1)
                    weigh_pages(c, 0)
                    dve.wait_ge(s["pe1"], c + 1 + 1)
                    dve.wait_ge(s["expo_ready"], c + 1)
                    for h in range(H):
                        op = nc.vector.scalar_tensor_tensor(out=expo[:, h, :], in0=bank(M_)[:, h, :],
                                                            scalar=k.g_col[:, bass.ds(c, 1), h], in1=k.late_big[:, :],
                                                            op0=ALU.subtract, op1=ALU.max)
                    op.then_inc(s["args_ready"], 1)
                    dve.wait_ge(s["expo_ready"], c + 1 + 1)
                    dve.wait_ge(s["pe2"], c + 1)
                    nc.vector.tensor_tensor(w_T[:, :, :], expo[:, :, :], bank(S_), ALU.mult).then_inc(s["weights_ready"], 1)
                    weigh_pages(c, 1)
                    dve.wait_ge(s["inter_ready"], c + 1)
                    for i in range(2):
                        op = nc.vector.tensor_tensor(num[:, 2 * i:2 * i + 2, :], inter[:, 2 * i:2 * i + 2, :],
                                                     pair(INTRA[i]), ALU.add)
                    dve.drain().then_inc(s["num_ready"], 1)
                    nc.vector.scalar_tensor_tensor(out=den[:, 0, :], in0=num[:, :, P], scalar=-1.0, in1=num[:, :, P],
                                                   op0=ALU.mult, op1=ALU.max)
                    dve.drain()
                    nc.vector.tensor_tensor(den[:, 1, :], den[:, 0, :], k.exps[:, E_NEGM, bass.ds(c, 1), :].squeeze(1), ALU.max)
                    dve.drain()
                    nc.vector.reciprocal(den[:, 2, :], den[:, 1, :])
                    dve.drain()
                    dve.wait_ge(s["pe3"], c + 1)
                    nc.vector.tensor_tensor(h_tok[:, :, :], num[:, :, 0:P],
                                            den[:, 2, :].unsqueeze(2).to_broadcast([P, H, P]), ALU.mult)\
                      .then_inc(s["h_ready"], 1)
                    dve.wait_ge(s["pe3"], c + 1 + 1)
                    for h in range(H):
                        op = nc.vector.scalar_tensor_tensor(out=state[:, h, :], in0=state[:, h, :],
                                                            scalar=k.exps[:, E_DECAY, bass.ds(c, 1), h],
                                                            in1=pair(STATE[h // 2])[:, h % 2, :], op0=ALU.mult, op1=ALU.add)
                    op.then_inc(s["state_ready"], 1)
                    dve.wait_ge(s["y_sent"], c * 16 + 16)
                    nc.vector.tensor_tensor(y_m[:, :, :], bank(TURNED), m_T[:, 3 * H:4 * H, bass.ds(c * P, P)],
                                            ALU.mult).then_inc(s["y_ready"], 1)
                nc.vector.tensor_copy(k.m_dec[:, :, :], m_T[:, :, T:TT])
                dve.wait_ge(s["dec_done"], 1)
                dve.wait_ge(k.acc_free, (base + TB * NB) * NCH + NCH)
                nc.vector.tensor_copy(y_dec[:, :, :], y.rearrange("p b h -> p h b")).then_inc(s["dec_read"], 1)
    k.blocks = base + TB * NB


class MlstmDecode:
    FIRST = 3

    def __init__(self, k, ctx):
        N = B * H
        self.k = k
        self.spread = k.sb(ctx, "dec_spread", [B, B, 2 * H])
        self.m_old = k.sb(ctx, "m_old", [P, N])
        self.gate = k.sb(ctx, "dec_gate", [P, B, 2 * H])
        self.f_abs = k.sb(ctx, "dec_f_abs", [P, B, H])
        self.f_pos = k.sb(ctx, "dec_f_pos", [P, B, H])
        self.m_new = k.sb(ctx, "m_new", [P, B, H])
        self.terms = k.sb(ctx, "dec_terms", [P, 3, B, H])
        self.keys = k.q_tok
        self.values = k.sb(ctx, "dec_values", [B, W])
        self.own = k.sb(ctx, "dec_own", [B, B, H])
        self.v_own = k.sb(ctx, "dec_v_own", [B, B, P])
        self.c = k.sb(ctx, "dec_c", [P, 2, B, P])
        self.n_new = k.sb(ctx, "n_new", [P, B, H])
        self.n_add = k.sb(ctx, "n_add", [P, B, H])
        self.n_rows = k.sb(ctx, "n_new_rows", [N, P])
        self.dot = k.sb(ctx, "dec_dot", [P, B, H])
        self.den = k.sb(ctx, "dec_den", [P, B, H])
        self.y_d = k.sb(ctx, "y_dec", [P, H, B])
        self.reps = k.ps(ctx, "dec_reps", [P, 512])
        self.turned = k.ps(ctx, "dec_turned", [B, 2, 512])
        self.outer = k.ps(ctx, "dec_outer", [P, B, P])
        self.s = {n: k.sem(ctx, "md_" + n) for n in (
            "m_in", "spread_ready", "gates_ready", "gate_ready", "log_ready", "terms_in", "terms_ready", "kv_turned",
            "kv_ready", "own_ready", "outer_ready", "new_ready", "dot_ready", "dots", "nums", "n_turned",
            "n_rows_ready", "y_ready", "sent")}
        self.old_in = [k.sem(ctx, f"C_old_in{i}") for i in range(2)]
        self.new_out = [k.sem(ctx, f"C_new_out{i}") for i in range(2)]

    def load_c(self, sp, h):
        if h >= 2:
            sp.wait_ge(self.new_out[h % 2], 16)
            sp.wait_ge(self.s["nums"], h - 1)
        sp.dma_start(self.c[:, h % 2, :, :], self.k.io["state_mlstm_C"][0, :, h].rearrange("b d e -> d b e"))\
          .then_inc(self.old_in[h % 2], 16)

    def store_c(self, sp, h):
        sp.wait_ge(self.s["new_ready"], h + 1)
        sp.dma_start(self.k.io["C_sample"][0, :, h].rearrange("b d e -> d b e"), self.c[:, h % 2, :, :])\
          .then_inc(self.new_out[h % 2], 16)

    def loads_first(self, sp):
        sp.dma_start(self.m_old[:, :], self.k.io["state_mlstm_m"].rearrange("l b h -> l (b h)").to_broadcast([P, B * H]),
                     allow_slow_non_contiguous=True).then_inc(self.s["m_in"], 16)
        self.load_c(sp, 0)
        self.load_c(sp, 1)

    def loads(self, sp, m):
        h = m - self.FIRST - 2
        if 0 < h < H - 1:
            self.load_c(sp, h + 1)
        if 0 <= h < H - 1:
            self.store_c(sp, h)

    def stores_last(self, sp):
        s, io = self.s, self.k.io
        self.store_c(sp, H - 1)
        sp.dma_start(io["m_sample"].rearrange("l b h -> l (b h)"), self.m_new[0:1, :, :].rearrange("p b h -> p (b h)"))\
          .then_inc(s["sent"], 16)
        sp.wait_ge(s["n_rows_ready"], 1)
        sp.dma_start(io["n_sample"].rearrange("l b h d -> (l b h) d"), self.n_rows[:, :]).then_inc(s["sent"], 16)
        sp.wait_ge(s["y_ready"], 1)
        sp.dma_start(self.k.branch[0, :, :, T:TT], self.y_d[:, :, :]).then_inc(s["sent"], 16)
        sp.wait_ge(s["sent"], 48)
        for i in range(2):
            sp.wait_ge(self.new_out[i], 32)

    def tensor(self, pe, m):
        k, nc, s = self.k, self.k.nc, self.s
        N = B * H
        flat = "p b h -> p (b h)"
        if m == 0:
            for a in range(2):
                for h in range(H):
                    tr = nc.tensor.transpose(self.turned[:, a, h * P:(h + 1) * P], k.m_dec[:, (a + 1) * H + h, :], k.ident[:, :])
            tr.then_inc(s["kv_turned"], 1)
            pe.wait_ge(s["spread_ready"], 1)
            nc.tensor.matmul(self.reps[:, 0:B * 2 * H], k.ones[0:B, :], self.spread[:, :, :].rearrange("p b g -> p (b g)"),
                             start=True, stop=True).then_inc(s["gates_ready"], 1)
        h = m - self.FIRST - 1
        if 0 <= h < H:
            pe.wait_ge(s["new_ready"], h + 1)
            for b in range(B):
                mm = nc.tensor.matmul(self.reps[:, 128 + h * B + b:129 + h * B + b], self.c[:, h % 2, b, :],
                                      k.m_dec[:, h, b:b + 1], start=True, stop=True)
            mm.then_inc(s["nums"], 1)
        h = m - self.FIRST
        if 0 <= h < H:
            pe.wait_ge(s["kv_ready"], 1)
            pe.wait_ge(s["own_ready"], h + 1)
            if h:
                pe.wait_ge(s["new_ready"], h)
            for half in range(2):
                mm = nc.tensor.matmul(self.outer[:, 4 * half:4 * half + 4, :], self.keys[:, h * P:(h + 1) * P],
                                      self.v_own[:, 4 * half:4 * half + 4, :], start=True, stop=True)
            mm.then_inc(s["outer_ready"], 1)
        if m == KD - 1:
            pe.wait_ge(s["dot_ready"], 1)
            nc.tensor.matmul(self.reps[:, 256:256 + N], k.ones[:, :], self.dot[:, :, :].rearrange(flat), start=True, stop=True)\
                .then_inc(s["dots"], 1)
            nc.tensor.transpose(self.outer[0:N, 0, :], self.n_new[:, :, :].rearrange(flat),
                                k.ident[:, :]).then_inc(s["n_turned"], 1)

    def scalar(self, act, m):
        nc, s, f_abs = self.k.nc, self.s, self.f_abs
        if m == 1:
            act.preload_act_table_set(EXP_LN)
            act.wait_ge(s["gate_ready"], 1)
            nc.scalar.activation(f_abs[:, :, :], self.gate[:, :, H:2 * H], ACT.Abs)
            act.drain()
            nc.scalar.activation(f_abs[:, :, :], f_abs[:, :, :], ACT.Exp, scale=-1.0)
            act.drain()
            nc.scalar.activation(f_abs[:, :, :], f_abs[:, :, :], ACT.Ln, bias=1.0).then_inc(s["log_ready"], 1)
            act.wait_ge(s["terms_in"], 1)
            nc.scalar.activation(self.terms[:, :, :, :], self.terms[:, :, :, :], ACT.Exp).then_inc(s["terms_ready"], 1)
            act.preload_act_table_set("sigmoid_and_others")

    def vector_first(self, dve):
        k = self.k
        k.nc.vector.tensor_tensor(self.spread[:, :, :], k.ident[0:B, 0:B].unsqueeze(2).to_broadcast([B, B, 2 * H]),
                                  k.gates_dec[:, :].unsqueeze(1).to_broadcast([B, B, 2 * H]),
                                  ALU.mult).then_inc(self.s["spread_ready"], 1)

    def weigh_values(self, h):
        self.k.nc.vector.tensor_tensor(self.v_own[:, :, :], self.values[:, h * P:(h + 1) * P].unsqueeze(1).to_broadcast([B, B, P]),
                                       self.own[:, :, h].unsqueeze(2).to_broadcast([B, B, P]),
                                       ALU.mult).then_inc(self.s["own_ready"], 1)

    def vector(self, dve, m):
        k, nc, s, terms, gate, f_pos = self.k, self.k.nc, self.s, self.terms, self.gate, self.f_pos
        flat = "p b h -> p (b h)"
        N = B * H
        if m == 0:
            dve.wait_ge(s["kv_turned"], 1)
            nc.vector.tensor_copy(self.keys[:, :], self.turned[:, 0, :])
            nc.vector.tensor_copy(self.values[:, :], self.turned[:, 1, :]).then_inc(s["kv_ready"], 1)
            dve.wait_ge(s["gates_ready"], 1)
            nc.vector.tensor_copy(gate[:, :, :].rearrange("p b g -> p (b g)"), self.reps[:, 0:B * 2 * H])\
              .then_inc(s["gate_ready"], 1)
            dve.wait_ge(s["gate_ready"], 1)
            nc.vector.tensor_scalar(f_pos[:, :, :], gate[:, :, H:2 * H], -1.0, 0.0, ALU.mult, ALU.max)
            dve.drain()
        if m == 1:
            dve.wait_ge(s["log_ready"], 1)
            nc.vector.scalar_tensor_tensor(out=f_pos[:, :, :], in0=f_pos[:, :, :], scalar=-1.0, in1=self.f_abs[:, :, :],
                                           op0=ALU.mult, op1=ALU.subtract)
            dve.drain()
            dve.wait_ge(s["m_in"], 16)
            nc.vector.tensor_tensor(f_pos[:, :, :], f_pos[:, :, :], self.m_old[:, :].rearrange("p (b h) -> p b h", h=H), ALU.add)
            dve.drain()
            nc.vector.tensor_tensor(self.m_new[:, :, :], f_pos[:, :, :], gate[:, :, 0:H], ALU.max)
            dve.drain()
            nc.vector.tensor_tensor(terms[:, 0, :, :], f_pos[:, :, :], self.m_new[:, :, :], ALU.subtract)
            nc.vector.tensor_tensor(terms[:, 1, :, :], gate[:, :, 0:H], self.m_new[:, :, :], ALU.subtract)
            nc.vector.tensor_scalar(terms[:, 2, :, :], self.m_new[:, :, :], -1.0, None, ALU.mult)
            dve.drain().then_inc(s["terms_in"], 1)
        if m == 2:
            dve.wait_ge(s["terms_ready"], 1)
            nc.vector.tensor_tensor(self.own[:, :, :], k.ident[0:B, 0:B].unsqueeze(2).to_broadcast([B, B, H]),
                                    terms[0:B, 1, :, :], ALU.mult)
            nc.vector.tensor_tensor(self.n_new[:, :, :], k.n_old[:, :].rearrange("p (b h) -> p b h", h=H), terms[:, 0, :, :], ALU.mult)
            nc.vector.tensor_tensor(self.n_add[:, :, :], k.m_dec[:, H:2 * H, :].rearrange("p h b -> p b h"), terms[:, 1, :, :], ALU.mult)
            dve.drain()
            nc.vector.tensor_tensor(self.n_new[:, :, :], self.n_new[:, :, :], self.n_add[:, :, :], ALU.add)
            dve.drain()
            nc.vector.tensor_tensor(self.dot[:, :, :], self.n_new[:, :, :], k.m_dec[:, 0:H, :].rearrange("p h b -> p b h"),
                                    ALU.mult).then_inc(s["dot_ready"], 1)
            self.weigh_values(0)
        h = m - self.FIRST
        if 0 <= h < H:
            c = self.c[:, h % 2, :, :]
            dve.wait_ge(self.old_in[h % 2], 16 * (h // 2 + 1))
            nc.vector.tensor_tensor(c, c, terms[:, 0, :, h].unsqueeze(2).to_broadcast([P, B, P]), ALU.mult)
            dve.drain()
            dve.wait_ge(s["outer_ready"], h + 1)
            nc.vector.tensor_tensor(c, c, self.outer[:, :, :], ALU.add).then_inc(s["new_ready"], 1)
            if h + 1 < H:
                self.weigh_values(h + 1)
        if m == KD - 1:
            den, dot, y_d = self.den, self.dot, self.y_d
            dve.wait_ge(s["dots"], 1)
            nc.vector.tensor_copy(den[:, :, :].rearrange(flat), self.reps[:, 256:256 + N])
            dve.drain()
            nc.vector.scalar_tensor_tensor(out=dot[:, :, :], in0=den[:, :, :], scalar=-1.0, in1=den[:, :, :],
                                           op0=ALU.mult, op1=ALU.max)
            dve.drain()
            nc.vector.tensor_tensor(den[:, :, :], dot[:, :, :], terms[:, 2, :, :], ALU.max)
            dve.drain()
            nc.vector.reciprocal(dot[:, :, :], den[:, :, :])
            dve.wait_ge(s["nums"], H)
            nc.vector.tensor_tensor(y_d[:, :, :], self.reps[:, 128:128 + N].rearrange("p (h b) -> p h b", h=H),
                                    k.m_dec[:, 3 * H:4 * H, :], ALU.mult)
            dve.drain()
            nc.vector.tensor_tensor(y_d[:, :, :], y_d[:, :, :], dot[:, :, :].rearrange("p b h -> p h b"), ALU.mult)\
              .then_inc(s["y_ready"], 1)
            dve.wait_ge(s["n_turned"], 1)
            nc.vector.tensor_copy(self.n_rows[:, :], self.outer[0:N, 0, :]).then_inc(s["n_rows_ready"], 1)


BRANCHES = (1, 2, 0)


def merge_branches(k, merged, then):
    nc, io = k.nc, k.io
    base = k.blocks
    NBR = 3
    with ExitStack() as ctx:
        y_raw = k.sb(ctx, "y_raw", [P, H, TT])
        y_hi = k.sb(ctx, "y_hi", [P, H, TT], F32R)
        y_lo = k.sb(ctx, "y_lo", [P, H, TT], F32R)
        gate = k.sb(ctx, "merge_gate", [P, 2, TT])
        part = k.sb(ctx, "merge_part", [P, TT])
        y_in = [k.sem(ctx, f"y_in{c}") for c in range(NCH)]
        s = {n: k.sem(ctx, "mb_" + n) for n in ("y_rounded", "y_split", "sigmoid", "merged", "hi_ready")}
        gate_in = [k.sem(ctx, f"gate_in{i}") for i in range(2)]
        decode = MlstmDecode(k, ctx)

        def walk(eng, r, step, after):
            if r == 0:
                for m in range(KD):
                    step(m, m % 2, m // 2)
                    after(eng, m)
            else:
                with eng.Fori(0, KD // 2) as i:
                    for par in range(2):
                        step(i * 2 + par, par, i)

        with nc.Block() as block:
            @block.sync
            def _(sp):
                def weights(r):
                    return io["w_branch"][0, BRANCHES[r]].rearrange("(k p) n -> p k n", p=P)

                def load_gate(r, m, par):
                    sp.wait_ge(s["merged"], r * KD + m + 1)
                    sp.dma_start(gate[:, par:par + 1, :], k.gates[:, bass.ds(m + BRANCHES[r] * KD, 1), :]).then_inc(gate_in[par], 16)

                def load_branch(r):
                    for c, cols in enumerate(CHUNKS):
                        if r:
                            sp.wait_ge(s["y_split"], (r - 1) * NCH + c + 1)
                        sp.dma_start(y_raw[:, :, cols], k.branch[BRANCHES[r], :, :, cols]).then_inc(y_in[c], 16)

                load_branch(0)
                decode.loads_first(sp)
                for r in range(NBR):
                    w = weights(r)
                    load_gate(r, 0, 0)
                    load_weights(k, sp, base + r * KD + 1, 1, w[:, :, P:2 * P], H)
                    load_gate(r, 1, 1)
                    if r == 1:
                        decode.stores_last(sp)
                    if r < NBR - 1:
                        load_branch(r + 1)

                    def step(m, par, i):
                        load_weights(k, sp, base + r * KD + m, par, w[:, :, bass.ds(m * P, P)], H)
                        load_gate(r, m, par)

                    if r == 0:
                        for m in range(2, KD):
                            step(m, m % 2, m // 2)
                            decode.loads(sp, m)
                    else:
                        with sp.Fori(1, KD // 2) as i:
                            for par in range(2):
                                step(i * 2 + par, par, i)
                    if r < NBR - 1:
                        load_weights(k, sp, base + r * KD + KD, 0, weights(r + 1)[:, :, 0:P], H)
                    else:
                        load_weights(k, sp, base + NBR * KD, 0, then)

            @block.gpsimd
            def _(pool):
                split_ahead(k, pool, base, NBR * KD, kb=H)

            @block.tensor
            def _(pe):
                for r in range(NBR):
                    def step(m, par, i):
                        for c in range(NCH):
                            if par == 0:
                                pe.wait_ge(s["y_split"], r * NCH + c + 1)
                            project_chunk(k, pe, base + r * KD + m, par, c, y_hi[:, :, :], y_lo[:, :, :], H)
                    walk(pe, r, step, decode.tensor)

            @block.scalar
            def _(act):
                act.preload_act_table_set("sigmoid_and_others")
                for r in range(NBR):
                    for c, cols in enumerate(CHUNKS):
                        act.wait_ge(y_in[c], 16 * (r + 1))
                        if r:
                            acc_wait(k, act, base + r * KD - 1, c)
                        nc.scalar.activation(y_hi[:, :, cols], y_raw[:, :, cols], ACT.Copy).then_inc(s["y_rounded"], 1)

                    def step(m, par, i):
                        act.wait_ge(gate_in[par], (i + r * (KD // 2) + 1) * 16)
                        nc.scalar.activation(gate[:, par, :], gate[:, par, :], ACT.Sigmoid).then_inc(s["sigmoid"], 1)
                        if r == NBR - 1:
                            act.wait_ge(s["merged"], r * KD + m + 1 + 2)
                            nc.scalar.activation(k.x_hi[:, bass.ds(m, 1), :], merged[:, bass.ds(m, 1), :], ACT.Copy)\
                              .then_inc(s["hi_ready"], 1)
                    walk(act, r, step, decode.scalar)

            @block.vector
            def _(dve):
                dve.sem_inc(s["merged"], 2)
                decode.vector_first(dve)
                for r in range(NBR):
                    for c, cols in enumerate(CHUNKS):
                        dve.wait_ge(s["y_rounded"], r * NCH + c + 1)
                        nc.vector.tensor_tensor(y_lo[:, :, cols], y_raw[:, :, cols], y_hi[:, :, cols].bitcast(F32),
                                                ALU.subtract).then_inc(s["y_split"], 1)

                    def step(m, par, i):
                        n = base + r * KD + m
                        dve.wait_ge(s["sigmoid"], r * KD + m + 1)
                        if r:
                            dve.wait_ge(s["merged"], r * KD + m + 2)
                        for c in range(NCH):
                            acc_wait(k, dve, n, c)
                            cols = slice(c * CW, (c + 1) * CW)
                            out = merged[:, bass.ds(m, 1), cols] if r == 0 else part[:, cols].unsqueeze(1)
                            nc.vector.tensor_tensor(out, k.acc[:, c:c + 1, 0:CW], gate[:, par:par + 1, cols],
                                                    ALU.mult).then_inc(k.acc_free, 1)
                        if r == 0:
                            dve.drain().then_inc(s["merged"], 1)
                        else:
                            dve.wait_ge(k.acc_free, (n + 1) * NCH + NCH)
                            nc.vector.tensor_tensor(merged[:, bass.ds(m, 1), :], merged[:, bass.ds(m, 1), :],
                                                    part[:, :].unsqueeze(1), ALU.add).then_inc(s["merged"], 1)
                        if r == NBR - 1:
                            dve.wait_ge(s["hi_ready"], m + 1)
                            nc.vector.tensor_tensor(k.x_lo[:, bass.ds(m, 1), :], merged[:, bass.ds(m, 1), :],
                                                    k.x_hi[:, bass.ds(m, 1), :].bitcast(F32), ALU.subtract)
                    walk(dve, r, step, decode.vector)
    k.blocks = base + NBR * KD


def mix_out(k, h, z_hi, z_lo, then):
    nc, io = k.nc, k.io
    base = k.blocks
    w = io["w_out"][0].rearrange("(k p) n -> p k n", p=P)
    with ExitStack() as ctx:
        h_in = [k.sem(ctx, f"h_in{i}") for i in range(3)]
        s = {n: k.sem(ctx, "mo_" + n) for n in SQUARES + ("rounded",)}
        squares = k.sb(ctx, "h_squares", [P, TT])[:, :]
        with nc.Block() as block:
            @block.sync
            def _(sp):
                load_weights(k, sp, base + 1, 1, w[:, :, P:2 * P])
                for i, blocks in enumerate((slice(0, 1), slice(1, 2), slice(2, KD))):
                    sp.dma_start(h[:, blocks, :], k.x_T[:, blocks, :]).then_inc(h_in[i], 16)
                with sp.Fori(1, KD // 2) as i:
                    for par in range(2):
                        load_weights(k, sp, base + i * 2 + par, par, w[:, :, bass.ds((i * 2 + par) * P, P)])
                load_weights(k, sp, base + KD, 0, then)

            @block.gpsimd
            def _(pool):
                split_ahead(k, pool, base, KD)

            @block.tensor
            def _(pe):
                with pe.Fori(0, KD // 2) as i:
                    for par in range(2):
                        for c in range(NCH):
                            project_chunk(k, pe, base + i * 2 + par, par, c, k.x_hi, k.x_lo)

            @block.scalar
            def _(act):
                with act.Fori(0, KD // 2) as i:
                    for par in range(2):
                        b = i * 2 + par
                        act.wait_ge(s["h_ready"], b + 1)
                        act.sem_inc(s["act_tick"], 1)
                        nc.scalar.activation(z_hi[:, bass.ds(b, 1), :], h[:, bass.ds(b, 1), :], ACT.Copy,
                                             scale=k.g_mlp[:, bass.ds(b, 1)]).then_inc(s["rounded"], 1)
                        square_block(k, act, h, b, squares, s)

            @block.vector
            def _(dve):
                nc.vector.memset(k.sq_sum[:, :], 0.0)
                dve.sem_inc(s["sq_added"], 1)

                def step(b, n):
                    for c in range(NCH):
                        add_chunk(k, dve, n, c, h[:, bass.ds(b, 1), :])
                    dve.drain().then_inc(s["h_ready"], 1)
                    dve.wait_ge(s["rounded"], b + 1)
                    nc.vector.scalar_tensor_tensor(out=z_lo[:, bass.ds(b, 1), :], in0=h[:, bass.ds(b, 1), :],
                                                   scalar=k.g_mlp[:, bass.ds(b, 1)],
                                                   in1=z_hi[:, bass.ds(b, 1), :].bitcast(F32), op0=ALU.mult, op1=ALU.subtract)
                    add_square(k, dve, b, squares, s)

                for b in range(2):
                    dve.wait_ge(h_in[b], 16)
                    step(b, base + b)
                dve.wait_ge(h_in[2], 16)
                with dve.Fori(1, KD // 2) as i:
                    for par in range(2):
                        step(i * 2 + par, base + i * 2 + par)
    k.blocks = base + KD


def add_chunk(k, dve, n, c, out):
    cols = slice(c * CW, (c + 1) * CW)
    acc_wait(k, dve, n, c)
    k.nc.vector.tensor_tensor(out[:, :, cols], k.acc[:, c:c + 1, 0:CW], out[:, :, cols], ALU.add).then_inc(k.acc_free, 1)


SQUARES = ("h_ready", "sq_ready", "sq_added", "act_tick")

def square_block(k, act, h, b, squares, s):
    act.wait_ge(s["h_ready"], b + 1)
    act.wait_ge(s["sq_added"], b + 1)
    act.sem_inc(s["act_tick"], 1)
    k.nc.scalar.activation(squares.unsqueeze(1), h[:, bass.ds(b, 1), :], ACT.Square).then_inc(s["sq_ready"], 1)


def add_square(k, dve, b, squares, s):
    dve.wait_ge(s["sq_ready"], b + 1)
    dve.wait_ge(s["sq_added"], b + 1)
    k.nc.vector.tensor_tensor(k.sq_sum[:, :], k.sq_sum[:, :], squares, ALU.add).then_inc(s["sq_added"], 1)


class Norm:
    POOL_BLOCKS = (2, 4, 6)

    def __init__(self, k, ctx, h, gain, places, name):
        self.k, self.h, self.gain = k, h, gain
        self.places = places
        self.sums = k.ps(ctx, name + "_sums", [P, NCH, 512])
        self.rstd = k.sq_sum
        self.summed, self.log_ready, self.rstd_ready, self.x_ready, self.hi_ready, self.lo_dve, self.lo_pool = (
            k.sem(ctx, f"{name}_{n}") for n in ("summed", "log_ready", "rstd_ready", "x_ready", "hi_ready", "lo_dve", "lo_pool"))

    def place(self, c, m):
        return self.places[(c * KD + m) % len(self.places)]

    def sum(self, pe):
        for c in range(NCH):
            self.k.nc.tensor.matmul(self.sums[:, c, 0:CW], self.k.ones[:, :], self.k.sq_sum[:, c * CW:(c + 1) * CW],
                                    start=True, stop=True).then_inc(self.summed, 1)

    def wait(self, eng, c):
        eng.wait_ge(self.lo_dve, (c + 1) * (KD - len(self.POOL_BLOCKS)))
        eng.wait_ge(self.lo_pool, (c + 1) * len(self.POOL_BLOCKS))

    def scale(self, dve):
        k, nc = self.k, self.k.nc
        for c in range(NCH):
            cols = slice(c * CW, (c + 1) * CW)

            def low(m):
                dve.wait_ge(self.hi_ready, c * KD + m + 1)
                nc.vector.tensor_tensor(k.x_lo[:, m, cols], self.place(c, m),
                                        k.x_hi[:, m, cols].bitcast(F32), ALU.subtract).then_inc(self.lo_dve, 1)

            dve.wait_ge(self.rstd_ready, c + 1)
            for m in range(KD):
                last = c * KD + m - len(self.places)
                if last >= 0:
                    done = [j % KD in self.POOL_BLOCKS for j in range(last + 1)]
                    dve.wait_ge(self.lo_pool if done[-1] else self.lo_dve, done.count(done[-1]))
                nc.vector.scalar_tensor_tensor(out=self.place(c, m), in0=self.h[:, m, cols],
                                               scalar=self.gain[:, m:m + 1], in1=self.rstd[:, cols],
                                               op0=ALU.mult, op1=ALU.mult).then_inc(self.x_ready, 1)
                if m and m - 1 not in self.POOL_BLOCKS:
                    low(m - 1)
            low(KD - 1)
        self.wait(dve, NCH - 1)

    def root(self, act):
        act.preload_act_table_set(EXP_LN)
        for c in range(NCH):
            cols = slice(c * CW, (c + 1) * CW)
            act.wait_ge(self.summed, c + 1)
            self.k.nc.scalar.activation(self.rstd[:, cols], self.sums[:, c, 0:CW], ACT.Ln, scale=1.0 / D,
                                        bias=self.k.eps[:, :]).then_inc(self.log_ready, 1)
            act.wait_ge(self.log_ready, c + 1)
            self.k.nc.scalar.activation(self.rstd[:, cols], self.rstd[:, cols], ACT.Exp, scale=-0.5)\
                .then_inc(self.rstd_ready, 1)

    def round(self, act):
        self.root(act)
        for c in range(NCH):
            cols = slice(c * CW, (c + 1) * CW)
            for m in range(KD):
                act.wait_ge(self.x_ready, c * KD + m + 1)
                self.k.nc.scalar.activation(self.k.x_hi[:, m, cols], self.place(c, m), ACT.Copy).then_inc(self.hi_ready, 1)

    def low(self, pool):
        k = self.k
        for c in range(NCH):
            cols = slice(c * CW, (c + 1) * CW)
            for m in self.POOL_BLOCKS:
                pool.wait_ge(self.hi_ready, c * KD + m + 1)
                k.nc.gpsimd.tensor_tensor(k.x_lo[:, m, cols], self.place(c, m),
                                          k.x_hi[:, m, cols].bitcast(F32), ALU.subtract).then_inc(self.lo_pool, 1)


def feed_forward(k, h, z_hi, z_lo, then):
    nc, io = k.nc, k.io
    base = k.blocks
    G = FFN // D
    w_up = io["w_up"][0].rearrange("(k p) n -> p k n", p=P)
    w_down = io["w_down"][0].rearrange("(g k p) n -> p g k n", p=P, k=KD)
    with ExitStack() as ctx:
        u_hi, u_lo = k.x_hi, k.x_lo
        relu = k.sb(ctx, "relu", [P, 3, CW])
        square = k.sb(ctx, "relu_sq", [P, 3, CW])
        squares = relu[:, :, :].rearrange("p c n -> p (c n)")
        s = {n: k.sem(ctx, "ff_" + n) for n in ("relu_ready", "squared", "rounded", "split") + SQUARES}
        norm = Norm(k, ctx, h, k.g_mlp, (), "n1")
        PG = KD * NCH
        with nc.Block() as block:
            @block.sync
            def _(sp):
                def up(g, b, par):
                    load_weights(k, sp, base + g * (2 * KD) + b, par, w_up[:, :, bass.ds(g * D + b * P, P)])

                def down(g, b, par):
                    load_weights(k, sp, base + g * (2 * KD) + KD + b, par,
                                 w_down[:, bass.ds(g, 1), :, bass.ds(b * P, P)].squeeze(1))

                def group(g):
                    with sp.Fori(0, KD // 2 - 1) as i:
                        up(g, i * 2 + 1, 1)
                        up(g, i * 2 + 2, 0)
                    up(g, KD - 1, 1)
                    down(g, 0, 0)
                    with sp.Fori(0, KD // 2 - 1) as i:
                        down(g, i * 2 + 1, 1)
                        down(g, i * 2 + 2, 0)
                    down(g, KD - 1, 1)

                with sp.Fori(0, G - 1) as g:
                    group(g)
                    load_weights(k, sp, base + g * (2 * KD) + 2 * KD, 0, w_up[:, :, bass.ds(g * D + D, P)])
                group(G - 1)
                load_weights(k, sp, base + G * 2 * KD, 0, then)

            @block.gpsimd
            def _(pool):
                split_ahead(k, pool, base, G * 2 * KD)

            @block.tensor
            def _(pe):
                norm.sum(pe)
                with pe.Fori(0, G) as g:
                    n0 = base + g * (2 * KD)
                    with pe.Fori(0, KD // 2) as i:
                        for par in range(2):
                            for c in range(NCH):
                                project_chunk(k, pe, n0 + i * 2 + par, par, c, z_hi, z_lo)
                    for par in range(2):
                        for c in range(NCH):
                            if par == 0:
                                pe.wait_ge(s["split"], g * PG + (KD - 1) * NCH + c + 1 + 1)
                            project_chunk(k, pe, n0 + KD + par, par, c, u_hi, u_lo)
                    with pe.Fori(1, KD // 2) as i:
                        for par in range(2):
                            for c in range(NCH):
                                project_chunk(k, pe, n0 + KD + i * 2 + par, par, c, u_hi, u_lo)

            @block.vector
            def _(dve):
                dve.sem_inc(s["split"], 1)
                dve.wait_ge(norm.rstd_ready, NCH)

                def up(g, n0):
                    with dve.Fori(0, KD // 2) as i:
                        def finish(e):
                            par, c = divmod(e, NCH)
                            t = g * PG + i * (2 * NCH) + e
                            dve.wait_ge(s["rounded"], t + 1)
                            nc.vector.tensor_tensor(u_lo[:, bass.ds(i * 2 + par, 1), c * CW:(c + 1) * CW],
                                                    square[:, c:c + 1, :],
                                                    u_hi[:, bass.ds(i * 2 + par, 1), c * CW:(c + 1) * CW].bitcast(F32),
                                                    ALU.subtract).then_inc(s["split"], 1)
                        for e in range(2 * NCH):
                            par, c = divmod(e, NCH)
                            acc_wait(k, dve, n0 + i * 2 + par, c)
                            if e >= NCH:
                                dve.wait_ge(s["rounded"], g * PG + i * (2 * NCH) + e - NCH + 1)
                            nc.vector.scalar_tensor_tensor(out=relu[:, c, :], in0=k.acc[:, c, 0:CW], scalar=0.0,
                                                           in1=norm.rstd[:, c * CW:(c + 1) * CW],
                                                           op0=ALU.max, op1=ALU.mult)\
                              .then_inc(k.acc_free, 1)
                            dve.drain().then_inc(s["relu_ready"], 1)
                            if e:
                                finish(e - 1)
                        finish(2 * NCH - 1)

                def down(n0, last):
                    with dve.Fori(0, KD // 2) as i:
                        for par in range(2):
                            b = i * 2 + par
                            for c in range(NCH):
                                add_chunk(k, dve, n0 + KD + b, c, h[:, bass.ds(b, 1), :])
                            if last:
                                dve.drain().then_inc(s["h_ready"], 1)
                                add_square(k, dve, b, squares, s)

                with dve.Fori(0, G - 1) as g:
                    up(g, base + g * (2 * KD))
                    down(base + g * (2 * KD), False)
                up(G - 1, base + (G - 1) * 2 * KD)
                nc.vector.memset(k.sq_sum[:, :], 0.0)
                dve.sem_inc(s["sq_added"], 1)
                down(base + (G - 1) * 2 * KD, True)

            @block.scalar
            def _(act):
                norm.root(act)
                with act.Fori(0, G) as g:
                    with act.Fori(0, KD // 2) as i:
                        for e in range(2 * NCH):
                            par, c = divmod(e, NCH)
                            t = g * PG + i * (2 * NCH) + e
                            act.wait_ge(s["relu_ready"], t + 1)
                            act.wait_ge(s["split"], (t - NCH + 1 if e >= NCH else g * PG + i * (2 * NCH)) + 1)
                            nc.scalar.activation(square[:, c, :], relu[:, c, :], ACT.Square).then_inc(s["squared"], 1)
                            nc.scalar.activation(u_hi[:, bass.ds(i * 2 + par, 1), c * CW:(c + 1) * CW], relu[:, c:c + 1, :],
                                                 ACT.Square).then_inc(s["rounded"], 1)
                with act.Fori(0, KD // 2) as i:
                    for par in range(2):
                        square_block(k, act, h, i * 2 + par, squares, s)
    k.blocks = base + G * 2 * KD


def per_layer_embedding(k, h):
    nc, io = k.nc, k.io
    base = k.blocks
    KP = PLE // P
    w_gate = io["w_ple_gate"][0].rearrange("(k p) n -> p k n", p=P)
    w_ple = io["w_ple"][0].rearrange("(k p) n -> p k n", p=P)
    with ExitStack() as ctx:
        rows = k.sb(ctx, "p_rows", [P, TB + 1, PLE])
        p_hi = k.sb(ctx, "p_hi", [P, KP, TT], F32R)
        p_lo = k.sb(ctx, "p_lo", [P, KP, TT], F32R)
        p_raw = k.sb(ctx, "p_raw", [P, 2, KP, P])
        pt = k.ps(ctx, "p_turned", [P, 2, 4, P])
        prod = k.sb(ctx, "ple_prod", [P, TT])
        gate = k.sb(ctx, "ple_gate", [P, TT])
        emb = k.sb(ctx, "ple_emb", [P, TT])
        squares = k.sb(ctx, "h_squares3", [P, TT])[:, :]
        s = {n: k.sem(ctx, "pl_" + n) for n in ("product",
            "rows_in", "turned", "rounded", "split") + SQUARES}
        norm = Norm(k, ctx, h, k.g_ple, [t[:, c * CW:(c + 1) * CW] for t in (gate, emb) for c in range(NCH)], "n2")
        with nc.Block() as block:
            @block.sync
            def _(sp):
                sp.dma_start(rows[:, 0:TB, :], io["p_prompt"][0, 0].rearrange("(b p) c -> p b c", p=P)).then_inc(s["rows_in"], 16)
                sp.dma_start(rows[0:B, TB, :], io["p_sample"][0, :, 0, :]).then_inc(s["rows_in"], 16)
                with sp.Fori(0, KD - 1) as m:
                    load_weights(k, sp, base + m * 2 + 1, 1, w_ple[:, :, bass.ds(m * P, P)], KP)
                    load_weights(k, sp, base + m * 2 + 2, 0, w_gate[:, :, bass.ds(m * P + P, P)])
                load_weights(k, sp, base + KD * 2 - 1, 1, w_ple[:, :, D - P:D], KP)

            @block.gpsimd
            def _(pool):
                norm.low(pool)
                split_weights(k, pool, base + 1, 1, base // 2, KP)
                for t in range(TB + 1):
                    m = P if t < TB else B
                    pool.wait_ge(s["rounded"], t + 1)
                    nc.gpsimd.tensor_tensor(p_lo[:, :, t * P:t * P + m], p_raw[:, t % 2, :, 0:m],
                                            p_hi[:, :, t * P:t * P + m].bitcast(F32), ALU.subtract).then_inc(s["split"], 1)
                with pool.Fori(1, KD) as m:
                    split_weights(k, pool, base + m * 2, 0, base // 2 + m)
                    split_weights(k, pool, base + m * 2 + 1, 1, base // 2 + m, KP)

            @block.tensor
            def _(pe):
                norm.sum(pe)
                for c in range(NCH):
                    norm.wait(pe, c)
                    project_chunk(k, pe, base, 0, c, k.x_hi, k.x_lo)
                pe.wait_ge(s["rows_in"], 32)
                for t in range(TB + 1):
                    m = P if t < TB else B
                    if t >= 2:
                        pe.wait_ge(s["rounded"], t - 1)
                    for i in range(KP):
                        tr = nc.tensor.transpose(pt[:, t % 2, i, 0:m], rows[0:m, t, i * P:(i + 1) * P], k.ident[0:m, 0:m])
                    tr.then_inc(s["turned"], 1)
                pe.wait_ge(s["split"], TB + 1)
                for c in range(NCH):
                    project_chunk(k, pe, base + 1, 1, c, p_hi, p_lo, KP)
                with pe.Fori(1, KD) as m:
                    for c in range(NCH):
                        project_chunk(k, pe, base + m * 2, 0, c, k.x_hi, k.x_lo)
                    for c in range(NCH):
                        project_chunk(k, pe, base + m * 2 + 1, 1, c, p_hi, p_lo, KP)

            @block.scalar
            def _(act):
                norm.round(act)
                for t in range(TB + 1):
                    m = P if t < TB else B
                    act.wait_ge(s["turned"], t + 1)
                    if t >= 2:
                        act.wait_ge(s["split"], t - 1)
                    nc.scalar.activation(p_raw[:, t % 2, :, 0:m], pt[:, t % 2, 0:KP, 0:m], ACT.Copy)
                    nc.scalar.activation(p_hi[:, :, t * P:t * P + m], pt[:, t % 2, 0:KP, 0:m], ACT.Copy).then_inc(s["rounded"], 1)
                norm.wait(act, NCH - 1)
                act.preload_act_table_set("sigmoid_and_others")
                with act.Fori(0, KD) as m:
                    for half, (out, func) in enumerate(((gate, ACT.Sigmoid), (emb, ACT.Copy))):
                        for c in range(NCH):
                            acc_wait(k, act, base + m * 2 + half, c)
                            if half == 0 and c == 0:
                                act.wait_ge(s["product"], m + 1)
                            nc.scalar.activation(out[:, c * CW:(c + 1) * CW], k.acc[:, c, 0:CW], func).then_inc(k.acc_free, 1)
                    square_block(k, act, h, m, squares, s)

            @block.vector
            def _(dve):
                dve.sem_inc(s["product"], 1)
                norm.scale(dve)
                nc.vector.memset(k.sq_sum[:, :], 0.0)
                dve.sem_inc(s["sq_added"], 1)
                with dve.Fori(0, KD) as m:
                    dve.wait_ge(k.acc_free, (base + m * 2 + 2) * NCH + NCH)
                    dve.wait_ge(s["sq_added"], m + 1)
                    nc.vector.tensor_tensor(prod[:, :], gate[:, :], emb[:, :], ALU.mult).then_inc(s["product"], 1)
                    dve.wait_ge(s["product"], m + 1 + 1)
                    nc.vector.tensor_tensor(h[:, bass.ds(m, 1), :], h[:, bass.ds(m, 1), :], prod[:, :].unsqueeze(1),
                                            ALU.add).then_inc(s["h_ready"], 1)
                    add_square(k, dve, m, squares, s)
    k.blocks = base + KD * 2


def final_norm(k, h):
    nc, io = k.nc, k.io
    tiles = [(t * P, P) for t in range(TB)] + [(T, B)]
    NT = len(tiles)
    with ExitStack() as ctx:
        gain = k.sb(ctx, "g_final_rows", [P, D])
        rstd = k.sb(ctx, "fn_rstd", [P, NT])
        y = k.sb(ctx, "fn_y", [P, 3, D])
        sums = k.ps(ctx, "fn_sums", [P, NT])
        pt = k.ps(ctx, "fn_pt", [P, 2, D])
        s = {n: k.sem(ctx, "fn_" + n) for n in ("gain_in", "summed", "turned", "rstd_ready", "y_ready")}
        sent = [k.sem(ctx, f"y_sent{i}") for i in range(3)]
        y_p = io["y_prompt"].rearrange("b t d -> (b t) d")
        y_s = io["y_sample"].rearrange("b t d -> (b t) d")
        with nc.Block() as block:
            @block.sync
            def _(sp):
                sp.dma_start(gain[:, :], io["g_final"].unsqueeze(0).to_broadcast([P, D])).then_inc(s["gain_in"], 16)
                for i, (t0, m) in enumerate(tiles):
                    sp.wait_ge(s["y_ready"], i + 1)
                    sp.dma_start(y_p[t0:t0 + m, :] if t0 < T else y_s, y[0:m, i % 3, :]).then_inc(sent[i % 3], 16)
                for i in range(3):
                    sp.wait_ge(sent[i], 16 * len(tiles[i::3]))

            @block.tensor
            def _(pe):
                for i, (t0, m) in enumerate(tiles):
                    mm = nc.tensor.matmul(sums[0:m, i:i + 1], k.sq_sum[:, t0:t0 + m], k.ones[:, 0:1], start=True, stop=True)
                mm.then_inc(s["summed"], 1)
                for i, (t0, m) in enumerate(tiles):
                    if i >= 2:
                        pe.wait_ge(s["y_ready"], i - 1)
                    for b in range(KD):
                        tr = nc.tensor.transpose(pt[0:m, i % 2, b * P:(b + 1) * P], h[:, b, t0:t0 + m], k.ident[:, :])
                    tr.then_inc(s["turned"], 1)

            @block.scalar
            def _(act):
                act.preload_act_table_set(EXP_LN)
                act.wait_ge(s["summed"], 1)
                for cols, m in ((slice(0, TB), P), (slice(TB, NT), B)):
                    nc.scalar.activation(rstd[0:m, cols], sums[0:m, cols], ACT.Ln, scale=1.0 / D, bias=k.eps[0:m, :])
                    act.drain()
                    op = nc.scalar.activation(rstd[0:m, cols], rstd[0:m, cols], ACT.Exp, scale=-0.5)
                op.then_inc(s["rstd_ready"], 1)

            @block.vector
            def _(dve):
                dve.wait_ge(s["gain_in"], 16)
                dve.wait_ge(s["rstd_ready"], 1)
                for i, (t0, m) in enumerate(tiles):
                    dve.wait_ge(s["turned"], i + 1)
                    if i >= 3:
                        dve.wait_ge(sent[i % 3], 16 * (i // 3))
                    nc.vector.scalar_tensor_tensor(out=y[0:m, i % 3, :], in0=pt[0:m, i % 2, :], scalar=rstd[0:m, i:i + 1],
                                                   in1=gain[0:m, :], op0=ALU.mult, op1=ALU.mult).then_inc(s["y_ready"], 1)

def allocate(k, ctx):
    k.x_hi = k.sb(ctx, "x_hi", [P, KD, TT], F32R)
    k.x_lo = k.sb(ctx, "x_lo", [P, KD, TT], F32R)
    k.w_raw = k.sb(ctx, "w_raw", [P, 2, KD, P])
    k.w_hi = k.sb(ctx, "w_hi", [P, 2, KD, P], F32R)
    k.w_lo = k.sb(ctx, "w_lo", [P, 2, KD, P], F32R)
    k.ident, k.ones, k.neg_ones, k.sum_to, k.neg_from, k.late_big, k.late_neg = (
        k.sb(ctx, name, [P, P])
        for name in ("ident", "ones", "neg_ones", "sum_to", "neg_from", "late_big", "late_neg"))
    k.eps = k.sb(ctx, "eps", [P, 1])
    k.g_mix, k.g_mlp, k.g_ple = (k.sb(ctx, name, [P, KD]) for name in ("g_mix_c", "g_mlp_c", "g_ple_c"))
    k.b_if = k.sb(ctx, "b_if_c", [P, 2 * H])
    k.b_sb = k.sb(ctx, "b_sb_c", [P, H])
    k.conv_w = k.sb(ctx, "conv_w_c", [P, 3, H])
    k.acc = k.ps(ctx, "acc", [P, NCH, 512])
    k.w_landed = [k.sem(ctx, f"w_landed{i}") for i in range(2)]
    k.w_rounded, k.w_split, k.acc_ready, k.acc_free, k.pool_tick, k.params_in, k.consts_ready = (
        k.sem(ctx, name) for name in ("w_rounded", "w_split", "acc_ready", "acc_free", "pool_tick", "params_in",
                                "consts_ready"))
    k.before = k.sb(ctx, "before", [P, P])
    k.conv_state = k.sb(ctx, "conv_state", [P, H, 2 * B])
    k.n_old = k.sb(ctx, "n_old", [P, B * H])
    k.g_col = k.sb(ctx, "g_col", [P, TB, H])
    k.mu = k.sb(ctx, "mu", [P, TB, H])
    k.exps = k.sb(ctx, "exps", [P, N_E, TB, H])
    k.gates_dec = k.sb(ctx, "gates_dec", [B, 2 * H])
    k.q_tok = k.sb(ctx, "q_tok", [B, W])
    k.two_idents = k.sb(ctx, "two_idents", [4 * H, 2 * H])
    k.m_dec = k.sb(ctx, "m_dec", [P, 4 * H, B])


def hybrid_layer(nc, io):
    k = Chip(nc, io)
    k.x_T = nc.dram_tensor("x_feature_major", [P, KD, TT], F32, kind="Internal").ap()
    k.gates = nc.dram_tensor("merge_gates", [P, 3 * KD, TT], F32, kind="Internal").ap()
    k.branch = nc.dram_tensor("branch_outputs", [3, P, H, TT], F32, kind="Internal").ap()
    w_in = io["w_in"].rearrange("l (k p) n -> p (l k) n", p=P)

    w_branch = io["w_branch"][0, BRANCHES[0]].rearrange("(k p) n -> p k n", p=P)
    w_out, w_up, w_ple_gate = (io[n][0].rearrange("(k p) n -> p k n", p=P) for n in ("w_out", "w_up", "w_ple_gate"))

    def group(col, out, scale=1.0, func=ACT.Copy):
        return dict(col=col, out=out, scale=scale, func=func)

    def block_of(t, first):
        return lambda b: t[:, bass.ds(b + first, 1), :]

    with ExitStack() as ctx:
        allocate(k, ctx)
        k.phase_sems = []
        normalise_input(k, w_in[:, :, C_SQ:C_SQ + P])
        with ExitStack() as part:
            s_T = k.sb(part, "s_T", [P, 3 * H, TT])
            project_attention(k, [group(C_SQ, block_of(s_T, 0), HD_SCALE), group(C_SK, block_of(s_T, H)),
                                  group(C_SV, block_of(s_T, 2 * H))], s_T, w_in[:, :, C_CC:C_CC + P])
            stick_breaking_prompt(k, s_T, w_in[:, :, C_MQ:C_MQ + P])
        with ExitStack() as part:
            m_T = k.sb(part, "m_T", [P, 4 * H, TT])
            k.dec_prob = k.sb(part, "dec_prob", [P, B, PAGES, H])
            project_mlstm(k, m_T, [group(C_MQ, block_of(m_T, 0)), group(C_MK, block_of(m_T, H), HD_SCALE),
                                   group(C_MV, block_of(m_T, 2 * H)),
                                   group(C_MO, block_of(m_T, 3 * H), func=ACT.Sigmoid)],
                          w_in[:, :, C_G + H * P:C_G + H * P + P])
            mlstm_prompt(k, m_T, w_branch[:, :, 0:P])
        h = k.sb(ctx, "h", [P, KD, TT])
        merge_branches(k, h, w_out[:, :, 0:P])
        k.sq_sum = k.sb(ctx, "sq_sum", [P, TT])
        with ExitStack() as part:
            z_hi = k.sb(part, "z_hi", [P, KD, TT], F32R)
            z_lo = k.sb(part, "z_lo", [P, KD, TT], F32R)
            mix_out(k, h, z_hi, z_lo, w_up[:, :, 0:P])
            feed_forward(k, h, z_hi, z_lo, w_ple_gate[:, :, 0:P])
        per_layer_embedding(k, h)
        final_norm(k, h)


_INS = ["x_prompt", "x_sample", "cache_k", "cache_v", "state_mlstm_C", "state_mlstm_n", "state_mlstm_m", "state_conv",
        "page_table", "p_prompt", "p_sample", "g_mix", "w_in", "b_if", "b_sb", "conv_w", "w_branch", "w_out", "g_mlp",
        "w_up", "w_down", "g_ple", "w_ple_gate", "w_ple", "g_final"]
_OUTS = [("y_prompt", (1, T, D)), ("y_sample", (B, 1, D)), ("k_prompt", (1, 1, T, H, P)), ("v_prompt", (1, 1, T, H, P)),
         ("C_prompt", (1, 1, H, P, P)), ("n_prompt", (1, 1, H, P)), ("m_prompt", (1, 1, H)), ("conv_prompt", (1, 1, 2, W)),
         ("k_sample", (1, B, 1, H, P)), ("v_sample", (1, B, 1, H, P)), ("C_sample", (1, B, H, P, P)),
         ("n_sample", (1, B, H, P)), ("m_sample", (1, B, H)), ("conv_sample", (1, B, 2, W))]


def kernel(**inputs):
    import numpy as _np
    import concourse.bacc as _bacc
    from concourse import mybir as _mybir
    from concourse.bass_utils import run_bass_kernel_spmd as _run

    nc = _bacc.Bacc("TRN2", target_bir_lowering=False, num_devices=1)
    arrays, io = {}, {}
    for name in _INS:
        a = _np.ascontiguousarray(inputs[name])
        arrays[f"in_{name}"] = a
        io[name] = nc.dram_tensor(f"in_{name}", a.shape, _mybir.dt.from_np(a.dtype), kind="ExternalInput").ap()
    for name, shape in _OUTS:
        io[name] = nc.dram_tensor(f"out_{name}", shape, _mybir.dt.float32, kind="ExternalOutput").ap()
    hybrid_layer(nc, io)
    r = _run(nc, [arrays], core_ids=[0])
    return tuple(r.results[0][f"out_{name}"] for name, _ in _OUTS)
```
